# Optimizing a Trainium2 kernel written in Bass

```python
import jax, jax.numpy as jnp
from jax import lax
import numpy as np

D_MODEL = 1024
BATCH = 1
SEQ = 512
DEPTH = 2

N_HEADS = 16
N_KV_GROUPS = 2
HEADS_PER_GROUP = N_HEADS // N_KV_GROUPS
HEAD_DIM = 64
N_KV_PARTS = 6
N_BRANCH = 3
L_CMP = 32
STRIDE_CMP = 16
L_SLC = 64
N_SEL = 16
WINDOW = 512
Q_CHUNK = 64
CONV_WIDTH = 31
FFN_HIDDEN = -(-(8 * D_MODEL) // (3 * 256)) * 256
EPS = 1e-6
NEG = -1e30
FORCE = 1e9


def rmsnorm(x, g):
    xf = x.astype(jnp.float32)
    y = xf * lax.rsqrt(jnp.mean(xf * xf, axis=-1, keepdims=True) + EPS)
    return (y * g.astype(jnp.float32)).astype(x.dtype)

def layernorm(x, g, b):
    xf = x.astype(jnp.float32)
    mu = jnp.mean(xf, axis=-1, keepdims=True)
    var = jnp.mean(jnp.square(xf - mu), axis=-1, keepdims=True)
    y = (xf - mu) * lax.rsqrt(var + EPS)
    return (y * g.astype(jnp.float32) + b.astype(jnp.float32)).astype(x.dtype)

def swiglu_ffn(x, norm_g, w_in, w_out):
    gate, up = jnp.split(rmsnorm(x, norm_g) @ w_in, 2, axis=-1)
    return (jax.nn.silu(gate) * up) @ w_out

def conformer_conv(x, norm_g, pw1_w, pw1_b, dw_w, dw_b, ln_g, ln_b, pw2_w, pw2_b):
    a, b = jnp.split(rmsnorm(x, norm_g) @ pw1_w + pw1_b, 2, axis=-1)
    h = a * jax.nn.sigmoid(b)
    h = lax.conv_general_dilated(
        h, dw_w[:, None, :], window_strides=(1,),
        padding=[(CONV_WIDTH - 1, 0)],
        dimension_numbers=('NWC', 'WIO', 'NWC'),
        feature_group_count=h.shape[-1]) + dw_b
    h = jax.nn.silu(layernorm(h, ln_g, ln_b))
    return h @ pw2_w + pw2_b

def shared_kv(h, kv_norm, w_kv, cmp_pos_k, cmp_pos_v, phi_k_w1, phi_k_w2, phi_v_w1, phi_v_w2):
    B, S, _ = h.shape
    kv = (rmsnorm(h, kv_norm) @ w_kv).reshape(B, S, N_KV_PARTS, N_KV_GROUPS, HEAD_DIM)
    kv = kv.transpose(2, 0, 3, 1, 4)
    k_cmp_raw, v_cmp_raw, k_slc, v_slc, k_win, v_win = kv
    n_cmp = (S - L_CMP) // STRIDE_CMP + 1
    idx = np.arange(n_cmp)[:, None] * STRIDE_CMP + np.arange(L_CMP)[None, :]

    def compress(raw, pos, w1, w2):
        blk = raw[:, :, idx] + pos
        blk = blk.reshape(B, N_KV_GROUPS, n_cmp, L_CMP * HEAD_DIM)
        return jax.nn.silu(blk @ w1) @ w2

    k_cmp = compress(k_cmp_raw, cmp_pos_k, phi_k_w1, phi_k_w2)
    v_cmp = compress(v_cmp_raw, cmp_pos_v, phi_v_w1, phi_v_w2)
    n_slc = S // L_SLC
    k_slc_blk = k_slc.reshape(B, N_KV_GROUPS, n_slc, L_SLC, HEAD_DIM)
    v_slc_blk = v_slc.reshape(B, N_KV_GROUPS, n_slc, L_SLC, HEAD_DIM)
    pad = ((0, 0), (0, 0), (WINDOW, 0), (0, 0))
    k_win_pad = jnp.pad(k_win, pad)
    v_win_pad = jnp.pad(v_win, pad)
    return (k_cmp, v_cmp, k_slc_blk, v_slc_blk, k_win_pad, v_win_pad)

def nsa_attention(x, norm_g, w_in, w_out, kv):
    k_cmp, v_cmp, k_slc_blk, v_slc_blk, k_win_pad, v_win_pad = kv
    B, S, _ = x.shape
    G, Hg, dh = N_KV_GROUPS, HEADS_PER_GROUP, HEAD_DIM
    n_chunk = S // Q_CHUNK
    n_cmp = k_cmp.shape[2]
    n_slc = k_slc_blk.shape[2]
    k_sel = min(N_SEL, n_slc)
    scale = HEAD_DIM ** -0.5

    proj = rmsnorm(x, norm_g) @ w_in
    q = proj[..., :N_HEADS * dh]
    gates = jax.nn.sigmoid(proj[..., N_HEADS * dh:])
    q = q.reshape(B, n_chunk, Q_CHUNK, G, Hg, dh).transpose(1, 0, 3, 4, 2, 5)
    gates = gates.reshape(B, n_chunk, Q_CHUNK, N_BRANCH, G, Hg).transpose(1, 3, 0, 4, 5, 2)
    starts = jnp.arange(n_chunk, dtype=jnp.int32) * Q_CHUNK

    slopes = jnp.asarray(2.0 ** (-8.0 * (np.arange(N_HEADS) + 1) / N_HEADS), jnp.float32)
    slopes = slopes.reshape(G, Hg)[:, :, None, None]
    cmp_end = jnp.arange(n_cmp, dtype=jnp.int32) * STRIDE_CMP + (L_CMP - 1)
    cs = np.arange(n_cmp)[:, None] * STRIDE_CMP
    ss = np.arange(n_slc)[None, :] * L_SLC
    overlap = jnp.asarray((cs <= ss + L_SLC - 1) & (cs + L_CMP - 1 >= ss), jnp.float32)
    blk = jnp.arange(n_slc, dtype=jnp.int32)
    bidx = jnp.arange(B)[:, None, None, None]
    gidx = jnp.arange(G)[None, :, None, None]

    def chunk_fn(args):
        q_c, g_c, c0 = args
        t = c0 + jnp.arange(Q_CHUNK, dtype=jnp.int32)

        dist = (t[:, None] - cmp_end[None, :]).astype(jnp.float32)
        valid = dist >= 0
        s = jnp.einsum('bghqd,bgnd->bghqn', q_c, k_cmp).astype(jnp.float32) * scale
        s = jnp.where(valid, s - slopes * dist, NEG)
        p_cmp = jax.nn.softmax(s, axis=-1) * valid.any(-1, keepdims=True)
        o_cmp = jnp.einsum('bghqn,bgnd->bghqd', p_cmp.astype(v_cmp.dtype), v_cmp)

        imp = jnp.einsum('bghqn,nj->bgqj', p_cmp, overlap)
        t_blk = t // L_SLC
        forced = (blk[None] == 0) | (blk[None] == t_blk[:, None]) | (blk[None] == t_blk[:, None] - 1)
        causal = blk[None] * L_SLC <= t[:, None]
        imp = jnp.where(forced, FORCE, jnp.where(causal, imp, -FORCE))
        _, sel = lax.top_k(imp, k_sel)
        ks = k_slc_blk[bidx, gidx, sel]
        vs = v_slc_blk[bidx, gidx, sel]
        pos = sel[..., None] * L_SLC + jnp.arange(L_SLC, dtype=jnp.int32)
        dist = (t[None, None, :, None, None] - pos).astype(jnp.float32)[:, :, None]
        s = jnp.einsum('bghqd,bgqkld->bghqkl', q_c, ks).astype(jnp.float32) * scale
        s = jnp.where(dist >= 0, s - slopes[..., None] * dist, NEG)
        p = jax.nn.softmax(s.reshape(B, G, Hg, Q_CHUNK, k_sel * L_SLC), axis=-1)
        o_slc = jnp.einsum('bghqm,bgqmd->bghqd', p.astype(vs.dtype),
                           vs.reshape(B, G, Q_CHUNK, k_sel * L_SLC, dh))

        kw = lax.dynamic_slice_in_dim(k_win_pad, c0, WINDOW + Q_CHUNK, axis=2)
        vw = lax.dynamic_slice_in_dim(v_win_pad, c0, WINDOW + Q_CHUNK, axis=2)
        s_pos = c0 - WINDOW + jnp.arange(WINDOW + Q_CHUNK, dtype=jnp.int32)
        dist = (t[:, None] - s_pos[None, :]).astype(jnp.float32)
        ok = (dist >= 0) & (dist < WINDOW) & (s_pos[None, :] >= 0)
        s = jnp.einsum('bghqd,bgmd->bghqm', q_c, kw).astype(jnp.float32) * scale
        s = jnp.where(ok, s - slopes * dist, NEG)
        p = jax.nn.softmax(s, axis=-1)
        o_win = jnp.einsum('bghqm,bgmd->bghqd', p.astype(vw.dtype), vw)

        o = (g_c[0][..., None] * o_cmp + g_c[1][..., None] * o_slc
             + g_c[2][..., None] * o_win)
        return o.transpose(0, 3, 1, 2, 4).reshape(B, Q_CHUNK, N_HEADS * dh).astype(x.dtype)

    out = lax.map(chunk_fn, (q, gates, starts))
    out = out.transpose(1, 0, 2, 3).reshape(B, S, N_HEADS * dh)
    return out @ w_out

def first_inputs(seed: int = 0) -> dict:
    key = jax.random.key(seed)
    ks = jax.random.split(key, 32)
    n_a = DEPTH // 2
    n_b = DEPTH - n_a
    D, F = D_MODEL, FFN_HIDDEN
    f32 = jnp.float32

    def w(k, shape, fan_in):
        return jax.random.normal(k, shape, f32) * fan_in ** -0.5

    def gain(k, shape):
        return 1.0 + 0.05 * jax.random.normal(k, shape, f32)

    def bias(k, shape):
        return 0.02 * jax.random.normal(k, shape, f32)

    return {
        "x": jax.random.normal(ks[0], (BATCH, SEQ, D), f32),
        "a_norm": gain(ks[1], (n_a, D)),
        "a_pw1_w": w(ks[2], (n_a, D, 2 * D), D),
        "a_pw1_b": bias(ks[3], (n_a, 2 * D)),
        "a_dw_w": w(ks[4], (n_a, CONV_WIDTH, D), CONV_WIDTH),
        "a_dw_b": bias(ks[5], (n_a, D)),
        "a_ln_g": gain(ks[6], (n_a, D)),
        "a_ln_b": bias(ks[7], (n_a, D)),
        "a_pw2_w": w(ks[8], (n_a, D, D), D),
        "a_pw2_b": bias(ks[9], (n_a, D)),
        "kv_norm": gain(ks[10], (D,)),
        "w_kv": w(ks[11], (D, N_KV_PARTS * N_KV_GROUPS * HEAD_DIM), D),
        "cmp_pos_k": 0.1 * jax.random.normal(ks[12], (L_CMP, HEAD_DIM), f32),
        "cmp_pos_v": 0.1 * jax.random.normal(ks[13], (L_CMP, HEAD_DIM), f32),
        "phi_k_w1": w(ks[14], (L_CMP * HEAD_DIM, HEAD_DIM), L_CMP * HEAD_DIM),
        "phi_k_w2": w(ks[15], (HEAD_DIM, HEAD_DIM), HEAD_DIM),
        "phi_v_w1": w(ks[16], (L_CMP * HEAD_DIM, HEAD_DIM), L_CMP * HEAD_DIM),
        "phi_v_w2": w(ks[17], (HEAD_DIM, HEAD_DIM), HEAD_DIM),
        "b_norm": gain(ks[18], (n_b, D)),
        "b_w_in": w(ks[19], (n_b, D, N_HEADS * HEAD_DIM + N_BRANCH * N_HEADS), D),
        "b_w_out": w(ks[20], (n_b, N_HEADS * HEAD_DIM, D), N_HEADS * HEAD_DIM),
        "ffn_norm": gain(ks[21], (DEPTH, D)),
        "ffn_w_in": w(ks[22], (DEPTH, D, 2 * F), D),
        "ffn_w_out": w(ks[23], (DEPTH, F, D), F),
        "final_norm": gain(ks[24], (D,)),
    }

def first_block(x, a_norm, a_pw1_w, a_pw1_b, a_dw_w, a_dw_b, a_ln_g, a_ln_b, a_pw2_w, a_pw2_b,
              kv_norm, w_kv, cmp_pos_k, cmp_pos_v, phi_k_w1, phi_k_w2, phi_v_w1, phi_v_w2,
              b_norm, b_w_in, b_w_out, ffn_norm, ffn_w_in, ffn_w_out, final_norm):
    n_a = DEPTH // 2
    h = x
    kv = None
    for layer in range(DEPTH):
        if layer < n_a:
            i = layer
            h = h + conformer_conv(h, a_norm[i], a_pw1_w[i], a_pw1_b[i], a_dw_w[i], a_dw_b[i],
                                   a_ln_g[i], a_ln_b[i], a_pw2_w[i], a_pw2_b[i])
        else:
            j = layer - n_a
            h = h + nsa_attention(h, b_norm[j], b_w_in[j], b_w_out[j], kv)
        h = h + swiglu_ffn(h, ffn_norm[layer], ffn_w_in[layer], ffn_w_out[layer])
        if layer == n_a - 1:
            kv = shared_kv(h, kv_norm, w_kv, cmp_pos_k, cmp_pos_v,
                           phi_k_w1, phi_k_w2, phi_v_w1, phi_v_w2)
    return rmsnorm(h, final_norm)


CHUNK = 64
N_MEM = 256
A_GROUPS = 4
A_GROUP_DIM = 128
A_WIDTH = A_GROUPS * A_GROUP_DIM
A_BLOCK = 128
FOX_HEADS = 8
FOX_HEAD_DIM = 64
FOX_WIDTH = FOX_HEADS * FOX_HEAD_DIM
Q_BLOCK = 128
POOL_WINDOWS = (2, 4, 8, 16)
POOL_GROUP_DIM = 128
POOL_WIDTH = len(POOL_WINDOWS) * POOL_GROUP_DIM
CONV_WIDTH_2 = 512
CONV_K = 3
MIX_WIDTH = 1024
EVEN_IN = 2 * A_WIDTH + 3 * FOX_WIDTH + FOX_HEADS
ODD_IN = POOL_WIDTH + 3 * CONV_WIDTH_2
XA_HEADS = 4
XA_HEAD_DIM = 128
XA_WIDTH = XA_HEADS * XA_HEAD_DIM
D_FF = -(-(8 * D_MODEL) // (3 * 256)) * 256
N_EVEN = (DEPTH + 1) // 2
N_ODD = DEPTH // 2


def rms_norm(x, g):
    xf = x.astype(jnp.float32)
    y = xf * lax.rsqrt(jnp.mean(xf * xf, axis=-1, keepdims=True) + EPS)
    return (y * g.astype(jnp.float32)).astype(x.dtype)

def chunk_gmlp(u, v, g_v, w_s, b_s):
    B, S, _ = v.shape
    v = rms_norm(v.reshape(B, S, A_GROUPS, A_GROUP_DIM), g_v.reshape(A_GROUPS, A_GROUP_DIM))
    vb = v.reshape(B, S // A_BLOCK, A_BLOCK, A_GROUPS, A_GROUP_DIM)
    cpos = np.arange(A_BLOCK) // CHUNK
    mask = jnp.asarray(cpos[:, None] >= cpos[None, :]).astype(w_s.dtype)
    w = w_s * mask[None]
    s = jnp.einsum('gts,bnsgc->bntgc', w, vb) + b_s.T[None, None, :, :, None]
    return u * s.reshape(B, S, A_WIDTH)

def forgetting_attention(q, k, v, log_f):
    B, S, H, hd = q.shape
    nb = S // Q_BLOCK
    scale = 1.0 / np.sqrt(hd)
    c = jnp.cumsum(log_f.astype(jnp.float32), axis=1).transpose(0, 2, 1)
    qb = q.reshape(B, nb, Q_BLOCK, H, hd).transpose(1, 0, 2, 3, 4)
    cb = c.reshape(B, H, nb, Q_BLOCK).transpose(2, 0, 1, 3)
    kpos = jnp.arange(S)

    def block(args):
        qi, ci, i = args
        logits = jnp.einsum('bqhd,bkhd->bhqk', qi, k).astype(jnp.float32) * scale
        logits = logits + ci[..., :, None] - c[:, :, None, :]
        qpos = i * Q_BLOCK + jnp.arange(Q_BLOCK)
        allowed = kpos[None, :] <= qpos[:, None]
        logits = jnp.where(allowed[None, None], logits, -jnp.inf)
        p = jax.nn.softmax(logits, axis=-1)
        return jnp.einsum('bhqk,bkhd->bqhd', p.astype(v.dtype), v)

    out = lax.map(block, (qb, cb, jnp.arange(nb)))
    return out.transpose(1, 0, 2, 3, 4).reshape(B, S, H * hd)

def multiscale_pool(z, w_pool, s_pool):
    B, S, _ = z.shape
    zf = z.astype(jnp.float32)
    cs = jnp.cumsum(zf, axis=1)
    pos = jnp.arange(S)
    outs = []
    for g, w in enumerate(POOL_WINDOWS):
        sl = slice(g * POOL_GROUP_DIM, (g + 1) * POOL_GROUP_DIM)
        csg = cs[..., sl]
        lag = jnp.pad(csg, ((0, 0), (w, 0), (0, 0)))[:, :S]
        cnt = jnp.minimum(pos + 1, w).astype(jnp.float32)[None, :, None]
        outs.append((csg - lag) / cnt - zf[..., sl])
    p = jnp.concatenate(outs, axis=-1).astype(z.dtype)
    p = p.reshape(B, S, len(POOL_WINDOWS), POOL_GROUP_DIM)
    y = jnp.einsum('bsgc,gcd->bsgd', p, w_pool).reshape(B, S, POOL_WIDTH)
    return y * s_pool

def short_gated_conv(h, gate_b, gate_c, conv_w):
    S = h.shape[1]
    xg = gate_c * h
    xp = jnp.pad(xg, ((0, 0), (CONV_K - 1, 0), (0, 0)))
    conv = sum(conv_w[j] * xp[:, j:j + S] for j in range(CONV_K))
    return gate_b * conv

def even_mixer(h, w_in, b_f, g_v, w_s, b_s, g_qn, g_kn, w_out):
    B, S, _ = h.shape
    z = h @ w_in
    uv = jax.nn.gelu(z[..., :2 * A_WIDTH])
    u, v = uv[..., :A_WIDTH], uv[..., A_WIDTH:]
    o = 2 * A_WIDTH
    q = z[..., o:o + FOX_WIDTH].reshape(B, S, FOX_HEADS, FOX_HEAD_DIM)
    k = z[..., o + FOX_WIDTH:o + 2 * FOX_WIDTH].reshape(B, S, FOX_HEADS, FOX_HEAD_DIM)
    vv = z[..., o + 2 * FOX_WIDTH:o + 3 * FOX_WIDTH].reshape(B, S, FOX_HEADS, FOX_HEAD_DIM)
    f_logit = z[..., o + 3 * FOX_WIDTH:].astype(jnp.float32) + b_f.astype(jnp.float32)
    log_f = jax.nn.log_sigmoid(f_logit)
    q = rms_norm(q, g_qn)
    k = rms_norm(k, g_kn)
    y_a = chunk_gmlp(u, v, g_v, w_s, b_s)
    y_b = forgetting_attention(q, k, vv, log_f).astype(h.dtype)
    return jnp.concatenate([y_a, y_b], axis=-1) @ w_out

def odd_mixer(h, w_in, w_pool, s_pool, conv_w, w_out):
    z = h @ w_in
    zc = z[..., :POOL_WIDTH]
    o = POOL_WIDTH
    hd = z[..., o:o + CONV_WIDTH_2]
    gb = z[..., o + CONV_WIDTH_2:o + 2 * CONV_WIDTH_2]
    gc = z[..., o + 2 * CONV_WIDTH_2:]
    y_c = multiscale_pool(zc, w_pool, s_pool)
    y_d = short_gated_conv(hd, gb, gc, conv_w)
    return jnp.concatenate([y_c, y_d], axis=-1) @ w_out

def memory_cross_attention(h, m, w_q, w_kv, w_o, g_qn, g_kn):
    B, S, _ = h.shape
    M = m.shape[1]
    q = rms_norm((h @ w_q).reshape(B, S, XA_HEADS, XA_HEAD_DIM), g_qn)
    kv = m @ w_kv
    k = rms_norm(kv[..., :XA_WIDTH].reshape(B, M, XA_HEADS, XA_HEAD_DIM), g_kn)
    v = kv[..., XA_WIDTH:].reshape(B, M, XA_HEADS, XA_HEAD_DIM)
    logits = jnp.einsum('bshd,bmhd->bhsm', q, k).astype(jnp.float32) / np.sqrt(XA_HEAD_DIM)
    p = jax.nn.softmax(logits, axis=-1).astype(v.dtype)
    o = jnp.einsum('bhsm,bmhd->bshd', p, v).reshape(B, S, XA_WIDTH)
    return o @ w_o

def swiglu(h, w_gate, w_up, w_down):
    return (jax.nn.silu(h @ w_gate) * (h @ w_up)) @ w_down

def second_inputs(seed: int = 0) -> dict:
    key = jax.random.key(seed)
    ks = jax.random.split(key, 32)
    f32 = jnp.float32

    def nrm(k, shape, scale):
        return jax.random.normal(k, shape, f32) * scale

    def gain(k, shape):
        return 1.0 + 0.05 * jax.random.normal(k, shape, f32)

    L, NE, NO, D = DEPTH, N_EVEN, N_ODD, D_MODEL
    return {
        "x": nrm(ks[0], (BATCH, SEQ, D), 1.0),
        "mem": nrm(ks[1], (BATCH, N_MEM, D), 1.0),
        "g_mix": gain(ks[2], (L, D)),
        "g_xa": gain(ks[3], (L, D)),
        "g_mem": gain(ks[4], (L, D)),
        "xa_wq": nrm(ks[5], (L, D, XA_WIDTH), D ** -0.5),
        "xa_wkv": nrm(ks[6], (L, D, 2 * XA_WIDTH), D ** -0.5),
        "xa_wo": nrm(ks[7], (L, XA_WIDTH, D), XA_WIDTH ** -0.5),
        "xa_gq": gain(ks[8], (L, XA_HEAD_DIM)),
        "xa_gk": gain(ks[9], (L, XA_HEAD_DIM)),
        "g_ffn": gain(ks[10], (L, D)),
        "w_gate": nrm(ks[11], (L, D, D_FF), D ** -0.5),
        "w_up": nrm(ks[12], (L, D, D_FF), D ** -0.5),
        "w_down": nrm(ks[13], (L, D_FF, D), D_FF ** -0.5),
        "e_w_in": nrm(ks[14], (NE, D, EVEN_IN), D ** -0.5),
        "e_b_f": jnp.linspace(1.0, 6.0, FOX_HEADS, dtype=f32)[None] + 0.1 * jax.random.normal(ks[15], (NE, FOX_HEADS), f32),
        "e_g_v": gain(ks[16], (NE, A_WIDTH)),
        "e_w_s": nrm(ks[17], (NE, A_GROUPS, A_BLOCK, A_BLOCK), A_BLOCK ** -0.5),
        "e_b_s": gain(ks[18], (NE, A_GROUPS, A_BLOCK)),
        "e_g_qn": gain(ks[19], (NE, FOX_HEAD_DIM)),
        "e_g_kn": gain(ks[20], (NE, FOX_HEAD_DIM)),
        "e_w_out": nrm(ks[21], (NE, MIX_WIDTH, D), MIX_WIDTH ** -0.5),
        "o_w_in": nrm(ks[22], (NO, D, ODD_IN), D ** -0.5),
        "o_w_pool": nrm(ks[23], (NO, len(POOL_WINDOWS), POOL_GROUP_DIM, POOL_GROUP_DIM), POOL_GROUP_DIM ** -0.5),
        "o_s_pool": gain(ks[24], (NO, POOL_WIDTH)),
        "o_conv_w": nrm(ks[25], (NO, CONV_K, CONV_WIDTH_2), CONV_K ** -0.5),
        "o_w_out": nrm(ks[26], (NO, MIX_WIDTH, D), MIX_WIDTH ** -0.5),
    }

def second_block(x, mem, g_mix, g_xa, g_mem, xa_wq, xa_wkv, xa_wo, xa_gq, xa_gk,
              g_ffn, w_gate, w_up, w_down,
              e_w_in, e_b_f, e_g_v, e_w_s, e_b_s, e_g_qn, e_g_kn, e_w_out,
              o_w_in, o_w_pool, o_s_pool, o_conv_w, o_w_out):
    for layer in range(DEPTH):
        i = layer // 2
        h = rms_norm(x, g_mix[layer])
        if layer % 2 == 0:
            y = even_mixer(h, e_w_in[i], e_b_f[i], e_g_v[i], e_w_s[i], e_b_s[i],
                           e_g_qn[i], e_g_kn[i], e_w_out[i])
        else:
            y = odd_mixer(h, o_w_in[i], o_w_pool[i], o_s_pool[i], o_conv_w[i], o_w_out[i])
        x = x + y
        m = rms_norm(mem, g_mem[layer])
        x = x + memory_cross_attention(rms_norm(x, g_xa[layer]), m, xa_wq[layer], xa_wkv[layer],
                                       xa_wo[layer], xa_gq[layer], xa_gk[layer])
        x = x + swiglu(rms_norm(x, g_ffn[layer]), w_gate[layer], w_up[layer], w_down[layer])
    return x


def setup_inputs(seed=0):
    out = dict(first_inputs(seed))
    for name, value in second_inputs(seed + 1).items():
        if name != "x":
            out[name + "_2"] = value
    return out


def reference(
    x, a_norm, a_pw1_w, a_pw1_b, a_dw_w, a_dw_b, a_ln_g, a_ln_b, a_pw2_w, a_pw2_b, kv_norm,
    w_kv, cmp_pos_k, cmp_pos_v, phi_k_w1, phi_k_w2, phi_v_w1, phi_v_w2, b_norm, b_w_in, b_w_out,
    ffn_norm, ffn_w_in, ffn_w_out, final_norm, mem_2, g_mix_2, g_xa_2, g_mem_2, xa_wq_2,
    xa_wkv_2, xa_wo_2, xa_gq_2, xa_gk_2, g_ffn_2, w_gate_2, w_up_2, w_down_2, e_w_in_2, e_b_f_2,
    e_g_v_2, e_w_s_2, e_b_s_2, e_g_qn_2, e_g_kn_2, e_w_out_2, o_w_in_2, o_w_pool_2, o_s_pool_2,
    o_conv_w_2, o_w_out_2,
):
    x = first_block(
        x, a_norm, a_pw1_w, a_pw1_b, a_dw_w, a_dw_b, a_ln_g, a_ln_b, a_pw2_w, a_pw2_b, kv_norm,
        w_kv, cmp_pos_k, cmp_pos_v, phi_k_w1, phi_k_w2, phi_v_w1, phi_v_w2, b_norm, b_w_in,
        b_w_out, ffn_norm, ffn_w_in, ffn_w_out, final_norm,
    )
    return second_block(
        x, mem_2, g_mix_2, g_xa_2, g_mem_2, xa_wq_2, xa_wkv_2, xa_wo_2, xa_gq_2, xa_gk_2,
        g_ffn_2, w_gate_2, w_up_2, w_down_2, e_w_in_2, e_b_f_2, e_g_v_2, e_w_s_2, e_b_s_2,
        e_g_qn_2, e_g_kn_2, e_w_out_2, o_w_in_2, o_w_pool_2, o_s_pool_2, o_conv_w_2, o_w_out_2,
    )


_drawn_inputs = setup_inputs


def setup_inputs(seed=0):
    import zlib

    import numpy as np

    out = dict(_drawn_inputs(seed))
    spreads = {}
    factors = {'a_ln_b': 2.719,
     'cmp_pos_k': 8.0,
     'b_norm': 3.994,
     'g_xa_2': 8.0,
     'g_mem_2': 5.565,
     'xa_gq_2': 8.0,
     'xa_gk_2': 8.0,
     'e_g_qn_2': 6.368,
     'e_g_kn_2': 5.733,
     'o_s_pool_2': 3.029}
    for name, (base, spread) in spreads.items():
        noise = np.random.default_rng([zlib.crc32(name.encode()), seed]).standard_normal(out[name].shape)
        drawn = base * np.exp(spread * noise) if base else spread * noise
        out[name] = __import__('jax').numpy.asarray(drawn.astype(out[name].dtype))
    for name, factor in factors.items():
        out[name] = (out[name] * factor).astype(out[name].dtype)
    return out
```

```python
from contextlib import ExitStack

import numpy as np
import concourse.bass as bass
from concourse import mybir

F32 = mybir.dt.float32
FR = mybir.dt.float32r
ALU = mybir.AluOpType
ACT = mybir.ActivationFunctionType
AXX = mybir.AxisListType.X

P = 128
S = 512
NT = S // P
D = 1024
KD = D // P
F = 2816
KF = F // P
HALF = 64
HEADS = 16
FOX = 8
XAH = 4
MEM = 256
TAPS = 31
NCMP = 31
LCMP = 32
STRIDE = 16
EPS = 1e-6
NEG = -1e30
BIG = 3e38
POOLS = (2, 4, 8, 16)
PAD = TAPS - 1

SLOTS = 4
PANEL = 1024
ARENA = 88
RING_BANKS = 4

COLUMNS = [
    ("a_norm", KD), ("pw1_b", 2 * KD), ("dw_w", KD * TAPS), ("dw_b", KD), ("ln_g", KD), ("ln_b", KD),
    ("pw2_b", KD), ("kv_norm", KD), ("b_norm", KD), ("ffn_norm", 2 * KD), ("final_norm", KD),
    ("g_mix", 2 * KD), ("g_xa", 2 * KD), ("g_mem", 2 * KD), ("xa_gq", 2), ("xa_gk", 2), ("g_ffn", 2 * KD),
    ("e_gq", 1), ("e_gk", 1), ("s_pool", 4), ("conv_w", 12), ("slopes", HEADS), ("seen", 1),
]
AT = {}
_n = 0
for _name, _w in COLUMNS:
    AT[_name] = _n
    _n += _w
NCOLS = _n
SQUARES = ["ident", "ones", "mean", "mean64", "mean128"]


class Signal:

    def __init__(self, sem):
        self.sem, self.total = sem, 0

    def reserve(self, n):
        base = self.total
        self.total += n
        return base


def after(eng, signal, value):
    if isinstance(value, int) and value <= 0:
        return
    eng.wait_ge(signal.sem, value)


def repeat(eng, n, body, straight=False):
    if straight or n == 1:
        for i in range(n):
            body(i)
    else:
        with eng.Fori(0, n) as i:
            body(i)


class Core:

    def __init__(self, nc, ctx, dram):
        self.nc, self.dram = nc, dram
        self.at = 16512
        self.ctx = ctx
        self.flags = {}
        self.x = self.place("x", [P, KD, S])
        self.xh_at = self.at
        self.xh = self.place("xh", [P, KD, S], FR)
        self.xl = self.place("xl", [P, KD, S], FR)
        self.raw = self.place("raw", [P, SLOTS, PANEL])
        self.wh = self.place("wh", [P, SLOTS, PANEL], FR)
        self.wl = self.place("wl", [P, SLOTS, PANEL], FR)
        self.rstd = self.place("rstd", [P, S])
        self.rstd_tok = self.place("rstd_tok", [P, NT])
        self.root = self.place("root", [P, S])
        self.root_tok = self.place("root_tok", [P, NT])
        self.ssq = self.place("ssq", [P, S])
        self.square = self.place("square", [P, S])
        self.pre = self.place("pre", [P, 2, S])
        self.up = self.place("up", [P, 2, S])
        self.cols = self.place("cols", [P, NCOLS])
        self.sq = {n: self.place(n, [P, P]) for n in SQUARES}
        self.small = self.place("small", [P, 256])
        self.eps = self.place("eps", [P, 1])
        self.arena0 = self.at
        self.at += ARENA * 1024
        self.psum = ctx.enter_context(nc.psum_tensor("psum", [P, 8, S], F32))
        self.landed = [Signal(ctx.enter_context(nc.semaphore(f"landed{i}"))) for i in range(SLOTS)]
        self.weights_high = self.flag("weights_high")
        self.weights_split = self.flag("weights_split")
        self.panels_used = self.flag("panels_used")
        self.banks_freed = self.flag("banks_freed")
        self.consts = self.flag("consts")
        self.panels = SLOTS
        self.products = RING_BANKS
        self.last_panel = None

    def place(self, name, shape, dtype=F32, offset=None):
        size = int(np.prod(shape[1:])) * 4
        if offset is None:
            offset = self.at
            self.at = (offset + size + 31) // 32 * 32
            assert self.at <= 229344, (name, self.at)
        assert offset + size <= 229344, (name, offset + size - 229344)
        return self.nc.alloc_sbuf_tensor_at(name, shape, dtype, offset=offset)

    def arena(self, name, kib, shape, dtype=F32):
        return self.place(name, shape, dtype, offset=int(self.arena0 + kib * 1024))

    def flag(self, name):
        if name not in self.flags:
            self.flags[name] = Signal(self.ctx.enter_context(self.nc.semaphore(name)))
        return self.flags[name]

    def col(self, name, i=0):
        return self.cols[:, bass.ds(AT[name] + i, 1)]

    def take_panels(self, n):
        base, self.panels = self.panels, self.panels + n
        return base

    def take_products(self, n):
        base, self.products = self.products, self.products + n
        return base

    def load_panel(self, sp, n0, lap, n, source, width):
        slot = n0 % SLOTS
        after(sp, self.weights_split, n - (SLOTS - 1))
        sp.dma_start(self.raw[:, slot, 0:width], source).then_inc(self.landed[slot].sem, 16)

    def split_high(self, act, n0, lap, n):
        slot = n0 % SLOTS
        act.wait_ge(self.landed[slot].sem, 16 * lap)
        after(act, self.panels_used, n - (SLOTS - 1))
        self.nc.scalar.activation(self.wh[:, slot, :], self.raw[:, slot, :], ACT.Copy).then_inc(
            self.weights_high.sem, 1)

    def split_low(self, dve, n0, lap, n):
        slot = n0 % SLOTS
        dve.wait_ge(self.weights_high.sem, n + 1)
        self.nc.vector.tensor_tensor(self.wl[:, slot, :], self.raw[:, slot, :],
                                     self.wh[:, slot, :].bitcast(F32), ALU.subtract).then_inc(
            self.weights_split.sem, 1)

    def ahead(self, split, eng, base, j, i, per):
        m = base + j + SLOTS
        if isinstance(i, int):
            m += i * per
            if m < self.last_panel:
                split(eng, m, m // SLOTS, m)
        else:
            split(eng, m, m // SLOTS + i * (per // SLOTS), m + i * per)


def three(nc, out, ah, al, bh, bl, start, stop):
    nc.tensor.matmul(out, ah, bh, start=start, stop=False)
    nc.tensor.matmul(out, ah, bl, start=False, stop=False)
    return nc.tensor.matmul(out, al, bh, start=False, stop=stop)


class Stage:

    def sync(self, sp):
        pass

    def gpsimd(self, pool):
        pass

    def scalar(self, act):
        pass

    def vector(self, dve):
        pass

    def tensor(self, pe):
        pass


class Load(Stage):

    def __init__(self, c):
        self.c = c
        self.x_in = c.flag("x_in")
        self.eps_set = c.flag("eps_set")

    def sync(self, sp):
        c = self.c
        sp.dma_start(c.cols[:], c.dram["cols"]).then_inc(c.consts.sem, 16)
        for m in range(2):
            sp.dma_start(c.x[:, 4 * m:4 * m + 4, :], c.dram["xT"][:, 4 * m:4 * m + 4, :]).then_inc(self.x_in.sem, 16)
        for k, n in enumerate(SQUARES):
            sp.dma_start(c.sq[n][:], c.dram["squares"][k]).then_inc(c.consts.sem, 16)

    def gpsimd(self, pool):
        pool.memset(self.c.eps[:], EPS).then_inc(self.eps_set.sem, 1)

    def scalar(self, act):
        act.wait_ge(self.c.consts.sem, 16 * (1 + len(SQUARES)))
        act.wait_ge(self.eps_set.sem, 1)
        act.sem_inc(self.c.weights_high.sem, SLOTS)
        for n in range(SLOTS, 2 * SLOTS):
            self.c.split_high(act, n, 1, n)

    def vector(self, dve):
        dve.wait_ge(self.c.consts.sem, 16 * (1 + len(SQUARES)))
        dve.wait_ge(self.x_in.sem, 32)
        dve.sem_inc(self.c.weights_split.sem, SLOTS)
        dve.sem_inc(self.c.banks_freed.sem, RING_BANKS)
        for n in range(SLOTS, 2 * SLOTS):
            self.c.split_low(dve, n, 1, n)

    def tensor(self, pe):
        pe.sem_inc(self.c.panels_used.sem, SLOTS)
        pe.wait_ge(self.c.consts.sem, 16 * (1 + len(SQUARES)))


class Prepare(Stage):

    def __init__(self, c, gain, norm=None):
        self.c, self.gain, self.norm = c, gain, norm
        self.high, self.ready = c.flag("x_high"), c.flag("x_ready")
        self.high0, self.ready0 = self.high.reserve(KD), self.ready.reserve(KD)
        self.squared, self.summed = c.flag("squared"), c.flag("summed")
        self.squared0, self.summed0 = self.squared.reserve(KD), self.summed.reserve(KD + 1)
        self.x_new = c.flag("x_new")
        self.x_new0 = self.x_new.reserve(KD) if norm else 0

    def gpsimd(self, pool):
        c = self.c
        if self.norm:
            pool.wait_ge(self.norm.stat.sem, self.norm.stat0 + 2)
        pool.memset(c.ssq[:], 0.0).then_inc(self.summed.sem, 1)
        if not self.norm:
            pool.wait_ge(c.flag("x_in").sem, 32)
        for m in range(KD):
            if self.norm:
                pool.wait_ge(self.x_new.sem, self.x_new0 + m + 1)
            pool.wait_ge(self.summed.sem, self.summed0 + 1 + m)
            pool.tensor_tensor(c.square[:], c.x[:, m, :], c.x[:, m, :], ALU.mult).then_inc(self.squared.sem, 1)
            pool.wait_ge(self.squared.sem, self.squared0 + m + 1)
            pool.tensor_tensor(c.ssq[:], c.ssq[:], c.square[:], ALU.add).then_inc(self.summed.sem, 1)

    def scalar(self, act):
        c = self.c
        if not self.norm:
            act.wait_ge(c.flag("x_in").sem, 32)
        for m in range(KD):
            if self.norm:
                act.wait_ge(self.x_new.sem, self.x_new0 + m + 1)
            c.nc.scalar.activation(c.xh[:, m, :], c.x[:, m, :], ACT.Copy, scale=c.col(*self.at(m))).then_inc(
                self.high.sem, 1)

    def at(self, m):
        return self.gain[0], self.gain[1] + m

    def vector(self, dve):
        c = self.c
        for m in range(KD):
            if self.norm:
                if m == 0:
                    dve.wait_ge(self.norm.done.sem, self.norm.done0 + 1)
                c.nc.vector.scalar_tensor_tensor(c.x[:, m, :], c.x[:, m, :], c.col("final_norm", m), c.rstd[:],
                                                 ALU.mult, ALU.mult).then_inc(self.x_new.sem, 1)
        for m in range(KD):
            dve.wait_ge(self.high.sem, self.high0 + m + 1)
            c.nc.vector.scalar_tensor_tensor(c.xl[:, m, :], c.x[:, m, :], c.col(*self.at(m)),
                                             c.xh[:, m, :].bitcast(F32), ALU.mult, ALU.subtract).then_inc(
                self.ready.sem, 1)


class Norm(Stage):

    def __init__(self, c, source):
        self.c, self.source = c, source
        c.last_norm = self
        self.stat, self.root, self.done = c.flag("stat"), c.flag("root_s"), c.flag("rstd_s")
        self.stat0, self.root0, self.done0 = self.stat.reserve(2), self.root.reserve(2), self.done.reserve(2)

    def tensor(self, pe):
        c, s = self.c, self.source
        pe.wait_ge(s.summed.sem, s.summed0 + KD + 1)
        after(pe, self.root, self.root0)
        pe.matmul(c.psum[:, 4, :], c.sq["mean"][:], c.ssq[:], start=True, stop=True).then_inc(self.stat.sem, 1)
        for i in range(NT):
            mm = pe.matmul(c.psum[:, 5, i:i + 1], c.ssq[:, i * P:(i + 1) * P], c.sq["mean"][:, 0:1],
                           start=(i == 0), stop=(i == NT - 1), skip_group_check=True)
        mm.then_inc(self.stat.sem, 1)

    def scalar(self, act):
        c = self.c
        after(act, self.done, self.done0)
        act.wait_ge(self.stat.sem, self.stat0 + 1)
        c.nc.scalar.activation(c.root[:], c.psum[:, 4, :], ACT.Sqrt, bias=c.eps[:]).then_inc(self.root.sem, 1)
        act.wait_ge(self.stat.sem, self.stat0 + 2)
        c.nc.scalar.activation(c.root_tok[:], c.psum[:, 5, 0:NT], ACT.Sqrt, bias=c.eps[:]).then_inc(self.root.sem, 1)

    def vector(self, dve):
        c = self.c
        dve.wait_ge(self.root.sem, self.root0 + 1)
        dve.reciprocal(c.rstd[:], c.root[:]).then_inc(self.done.sem, 1)
        dve.wait_ge(self.root.sem, self.root0 + 2)
        dve.reciprocal(c.rstd_tok[:], c.root_tok[:]).then_inc(self.done.sem, 1)
        dve.wait_ge(self.done.sem, self.done0 + 2)


class Gated(Stage):

    def __init__(self, c, weights, pairs, source, norm, hidden=None, conv=None, layer=0):
        self.c, self.weights, self.pairs, self.source, self.norm = c, weights, pairs, source, norm
        self.hidden, self.conv = hidden, conv
        self.panel0, self.product0 = c.take_panels(2 * pairs), c.take_products(2 * pairs)
        self.gated = c.flag("gated")
        self.made = c.flag("made")
        self.high = c.flag("hidden_high")
        self.ready = c.flag("hidden_ready")
        self.gated0, self.made0 = self.gated.reserve(pairs), self.made.reserve(pairs)
        if hidden:
            self.high0, self.ready0 = self.high.reserve(pairs), self.ready.reserve(pairs)

    def sync(self, sp):
        c, w = self.c, self.c.dram[self.weights]

        def four(i):
            for j in range(4):
                n0 = self.panel0 + j
                c.load_panel(sp, n0, None, n0 + 4 * i, w[bass.ds(4 * i + j, 1)].rearrange("a p n -> (a p) n"), PANEL)
        repeat(sp, self.pairs // 2, four)

    def tensor(self, pe):
        c = self.c

        def four(i):
            for j in range(4):
                n0, t0 = self.panel0 + j, self.product0 + j
                after(pe, c.banks_freed, t0 + 4 * i - (RING_BANKS - 1))
                pe.wait_ge(c.weights_split.sem, n0 + 4 * i + 1)
                out = c.psum[:, t0 % RING_BANKS, :]
                slot = n0 % SLOTS
                for k in range(KD):
                    if j == 0:
                        pe.wait_ge(self.source.ready.sem, self.source.ready0 + k + 1)
                    w = slice(k * P, (k + 1) * P)
                    mm = three(c.nc, out, c.wh[:, slot, w], c.wl[:, slot, w], c.xh[:, k, :], c.xl[:, k, :],
                               k == 0, k == KD - 1)
                mm.then_inc(c.panels_used.sem, 1)
        repeat(pe, self.pairs // 2, four)

    def scalar(self, act):
        c = self.c

        act.preload_act_table(ACT.Sigmoid if self.conv else ACT.Silu)

        def four(i):
            for r in range(2):
                c.ahead(c.split_high, act, self.panel0, 2 * r, i, 4)
                act.wait_ge(c.banks_freed.sem, self.product0 + 2 * r + 1 + 4 * i)
                func = ACT.Sigmoid if self.conv else ACT.Silu
                more = {"bias": c.col("pw1_b", KD + r + 2 * i)} if self.conv else {}
                c.nc.scalar.activation(c.pre[:, r, :], c.pre[:, r, :], func, **more).then_inc(self.gated.sem, 1)
                c.ahead(c.split_high, act, self.panel0, 2 * r + 1, i, 4)
                if self.hidden:
                    act.wait_ge(self.made.sem, self.made0 + r + 1 + 2 * i)
                    c.nc.scalar.activation(self.hidden[0][:, bass.ds(2 * i + r, 1), :],
                                           c.up[:, r:r + 1, :], ACT.Copy).then_inc(self.high.sem, 1)
        repeat(act, self.pairs // 2, four)

    def vector(self, dve):
        c = self.c
        dve.wait_ge(self.norm.done.sem, self.norm.done0 + 2)

        def four(i):
            for r in range(2):
                dve.wait_ge(c.panels_used.sem, self.panel0 + 2 * r + 1 + 4 * i)
                bank = (self.product0 + 2 * r) % RING_BANKS
                dve.tensor_tensor(c.pre[:, r, :], c.psum[:, bank, :], c.rstd[:], ALU.mult).then_inc(
                    c.banks_freed.sem, 1)
                c.ahead(c.split_low, dve, self.panel0, 2 * r, i, 4)
                dve.wait_ge(c.panels_used.sem, self.panel0 + 2 * r + 2 + 4 * i)
                bank = (self.product0 + 2 * r + 1) % RING_BANKS
                dve.tensor_tensor(c.up[:, r, :], c.psum[:, bank, :], c.rstd[:], ALU.mult).then_inc(
                    c.banks_freed.sem, 1)
                c.ahead(c.split_low, dve, self.panel0, 2 * r + 1, i, 4)
                dve.wait_ge(c.banks_freed.sem, self.product0 + 2 * r + 2 + 4 * i)
                dve.wait_ge(self.gated.sem, self.gated0 + r + 1 + 2 * i)
                if self.conv:
                    dve.scalar_tensor_tensor(self.conv[:, bass.ds(2 * i + r, 1), PAD:PAD + S],
                                             c.up[:, r:r + 1, :], c.col("pw1_b", r + 2 * i), c.pre[:, r:r + 1, :],
                                             ALU.add, ALU.mult).then_inc(self.made.sem, 1)
                else:
                    dve.tensor_tensor(c.up[:, r, :], c.up[:, r, :], c.pre[:, r, :], ALU.mult).then_inc(
                        self.made.sem, 1)
                    dve.wait_ge(self.high.sem, self.high0 + r + 1 + 2 * i)
                    at = bass.ds(2 * i + r, 1)
                    dve.tensor_tensor(self.hidden[1][:, at, :], c.up[:, r:r + 1, :],
                                      self.hidden[0][:, at, :].bitcast(F32), ALU.subtract).then_inc(self.ready.sem, 1)
        repeat(dve, self.pairs // 2, four)


class Residual(Stage):

    def __init__(self, c, weights, act_parts, source, cuts, pack, gain, bias=None, last=False):
        self.c, self.weights, self.parts, self.source = c, weights, act_parts, source
        self.cuts, self.pack, self.gain, self.bias, self.last = cuts, pack, gain, bias, last
        self.norm = c.last_norm
        self.per = KD * len(cuts) // pack
        self.panel0, self.product0 = c.take_panels(self.per), c.take_products(KD)
        self.body = 4 * pack if len(cuts) == 1 else 4
        self.turns = KD // self.body
        self.body_panels = self.body * len(cuts) // pack
        self.high, self.ready = c.flag("x_high"), c.flag("x_ready")
        self.squared, self.summed = c.flag("squared"), c.flag("summed")
        if gain:
            self.high0, self.ready0 = self.high.reserve(KD), self.ready.reserve(KD)
        if not last:
            self.squared0, self.summed0 = self.squared.reserve(KD), self.summed.reserve(KD + 1)

    def sync(self, sp):
        c, w = self.c, self.c.dram[self.weights]

        def turn(i):
            for j in range(self.body_panels):
                n0 = self.panel0 + j
                if len(self.cuts) == 1:
                    width = self.cuts[0] * self.pack * P
                    src = w[bass.ds(self.body_panels * i + j, 1)].rearrange("a p n -> (a p) n")
                else:
                    m, q = divmod(j, len(self.cuts))
                    lo = sum(self.cuts[:q]) * P
                    width = self.cuts[q] * P
                    src = w[bass.ds(self.body * i + m, 1), :, lo:lo + width].rearrange("a p n -> (a p) n")
                c.load_panel(sp, n0, None, n0 + self.body_panels * i, src, width)
        repeat(sp, self.turns, turn, straight=self.last)

    def tensor(self, pe):
        c = self.c
        ah, al = self.parts

        def turn(i):
            for m in range(self.body):
                t0 = self.product0 + m
                after(pe, c.banks_freed, t0 + self.body * i - (RING_BANKS - 1))
                out = c.psum[:, t0 % RING_BANKS, :]
                for q, blocks in enumerate(self.cuts):
                    j = (m * len(self.cuts) + q) // self.pack
                    n0 = self.panel0 + j
                    slot = n0 % SLOTS
                    if m % self.pack == 0:
                        pe.wait_ge(c.weights_split.sem, n0 + self.body_panels * i + 1)
                    for b in range(blocks):
                        k = sum(self.cuts[:q]) + b
                        if m == 0:
                            pe.wait_ge(self.source.ready.sem, self.source.ready0 + k + 1)
                        at = ((m % self.pack) * blocks + b) * P
                        mm = three(c.nc, out, c.wh[:, slot, at:at + P], c.wl[:, slot, at:at + P],
                                   ah[:, k, :], al[:, k, :], k == 0, k == sum(self.cuts) - 1)
                    if m % self.pack == self.pack - 1:
                        mm.then_inc(c.panels_used.sem, 1)
        repeat(pe, self.turns, turn, straight=self.last)

    def panels_of(self, m):
        if self.pack > 1:
            return [m // self.pack] if m % self.pack == self.pack - 1 else []
        return [m * len(self.cuts) + q for q in range(len(self.cuts))]

    def gpsimd(self, pool):
        c = self.c
        if self.last:
            return
        pool.wait_ge(self.norm.stat.sem, self.norm.stat0 + 2)
        pool.memset(c.ssq[:], 0.0).then_inc(self.summed.sem, 1)

        def turn(i):
            for m in range(self.body):
                at = bass.ds(self.body * i + m, 1)
                pool.wait_ge(c.banks_freed.sem, self.product0 + m + 1 + self.body * i)
                pool.wait_ge(self.summed.sem, self.summed0 + 1 + m + self.body * i)
                pool.tensor_tensor(c.square[:].rearrange("p (a n) -> p a n", a=1), c.x[:, at, :], c.x[:, at, :],
                                   ALU.mult).then_inc(self.squared.sem, 1)
                pool.wait_ge(self.squared.sem, self.squared0 + m + 1 + self.body * i)
                pool.tensor_tensor(c.ssq[:], c.ssq[:], c.square[:], ALU.add).then_inc(self.summed.sem, 1)
        repeat(pool, self.turns, turn)

    def scalar(self, act):
        c = self.c

        def turn(i):
            for m in range(self.body):
                if self.gain:
                    at = bass.ds(self.body * i + m, 1)
                    act.wait_ge(c.banks_freed.sem, self.product0 + m + 1 + self.body * i)
                    c.nc.scalar.activation(c.xh[:, at, :], c.x[:, at, :], ACT.Copy,
                                           scale=c.col(self.gain[0], self.gain[1] + m + self.body * i)).then_inc(
                        self.high.sem, 1)
                for j in self.panels_of(m):
                    c.ahead(c.split_high, act, self.panel0, j, i, self.body_panels)
        repeat(act, self.turns, turn, straight=self.last)

    def vector(self, dve):
        c = self.c

        def turn(i):
            for m in range(self.body):
                at = bass.ds(self.body * i + m, 1)
                last = (m // self.pack * len(self.cuts)) + len(self.cuts)
                dve.wait_ge(c.panels_used.sem, self.panel0 + last + self.body_panels * i)
                bank = (self.product0 + m) % RING_BANKS
                out = c.psum[:, bank:bank + 1, :]
                if self.bias:
                    dve.scalar_tensor_tensor(c.x[:, at, :], out, c.col(self.bias, m + self.body * i), c.x[:, at, :],
                                             ALU.add, ALU.add).then_inc(c.banks_freed.sem, 1)
                else:
                    dve.tensor_tensor(c.x[:, at, :], out, c.x[:, at, :], ALU.add).then_inc(c.banks_freed.sem, 1)
                for j in self.panels_of(m):
                    c.ahead(c.split_low, dve, self.panel0, j, i, self.body_panels)
                if self.gain:
                    dve.wait_ge(self.high.sem, self.high0 + m + 1 + self.body * i)
                    dve.scalar_tensor_tensor(c.xl[:, at, :], c.x[:, at, :],
                                             c.col(self.gain[0], self.gain[1] + m + self.body * i),
                                             c.xh[:, at, :].bitcast(F32), ALU.mult, ALU.subtract).then_inc(
                        self.ready.sem, 1)
        repeat(dve, self.turns, turn, straight=self.last)


class Store(Stage):

    def __init__(self, c, source):
        self.c, self.source = c, source
        self.out_done = c.flag("out_done")

    def gpsimd(self, pool):
        c = self.c
        for m in range(KD):
            pool.wait_ge(c.banks_freed.sem, self.source.product0 + m + 1)
            pool.dma_start(c.dram["out"][m], c.x[:, m, :]).then_inc(self.out_done.sem, 16)
        pool.wait_ge(self.out_done.sem, 16 * KD)


class Chain:

    def __init__(self, eng, signal):
        self.eng, self.flag = eng, signal

    def link(self, ins):
        ins.then_inc(self.flag.sem, 1)
        self.flag.total += 1
        self.eng.wait_ge(self.flag.sem, self.flag.total)


class Convolution(Stage):

    def __init__(self, c, source):
        self.c, self.source = c, source
        self.padded = c.arena("conv_in", 0, [P, KD, PAD + S])
        self.out = c.arena("conv_out", 17, [P, KD, S])
        self.parts = (c.arena("conv_high", 34, [P, KD, S], FR), c.arena("conv_low", 50, [P, KD, S], FR))
        self.total = c.arena("conv_total", 66, [P, S])
        self.sq = c.arena("conv_square", 68, [P, 2, S])
        self.var = c.arena("conv_var", 72, [P, S])
        self.root = c.arena("conv_root", 74, [P, S])
        self.rs = c.arena("conv_rstd", 76, [P, S])
        self.pads = c.flag("pads")
        self.tapped, self.added = c.flag("tapped"), c.flag("added")
        self.ln_stat, self.centred = c.flag("ln_stat"), c.flag("centred")
        self.sq_done, self.ln_root = c.flag("sq_done"), c.flag("ln_root")
        self.ln_scaled, self.silu_done = c.flag("ln_scaled"), c.flag("silu_done")
        self.high, self.ready = c.flag("conv_high_s"), c.flag("conv_ready")
        self.ready0 = 0

    def gpsimd(self, pool):
        pool.memset(self.total[:], 0.0).then_inc(self.added.sem, 1)
        for m in range(KD):
            pool.wait_ge(self.tapped.sem, 2 * TAPS * (m // 2 + 1))
            pool.wait_ge(self.added.sem, m + 1)
            pool.tensor_tensor(self.total[:], self.total[:], self.out[:, m, :], ALU.add).then_inc(self.added.sem, 1)
        pool.memset(self.var[:], 0.0).then_inc(self.added.sem, 1)
        for m in range(KD):
            pool.wait_ge(self.sq_done.sem, m + 1)
            pool.wait_ge(self.added.sem, KD + 2 + m)
            pool.tensor_tensor(self.var[:], self.var[:], self.sq[:, m % 2, :], ALU.add).then_inc(self.added.sem, 1)

    def vector(self, dve):
        c = self.c
        dve.wait_ge(self.pads.sem, 1)
        dve.wait_ge(c.flag("made").sem, self.source.made0 + KD)

        def pair(i):
            for k in range(TAPS):
                for a in range(2):
                    at = bass.ds(2 * i + a, 1)
                    out, taps = self.out[:, at, :], self.padded[:, at, k:k + S]
                    w = c.col("dw_w", (2 * i + a) * TAPS + k)
                    if k == 0:
                        dve.tensor_scalar(out, taps, w, c.col("dw_b", 2 * i + a), ALU.mult, ALU.add).then_inc(
                            self.tapped.sem, 1)
                        continue
                    dve.wait_ge(self.tapped.sem, 2 * TAPS * i + 2 * (k - 1) + a + 1)
                    dve.scalar_tensor_tensor(out, taps, w, out, ALU.mult, ALU.add).then_inc(self.tapped.sem, 1)
        repeat(dve, KD // 2, pair)
        dve.wait_ge(self.ln_stat.sem, 1)
        dve.wait_ge(self.tapped.sem, TAPS * KD)
        for m in range(KD):
            dve.tensor_tensor(self.out[:, m, :], self.out[:, m, :], c.psum[:, 6, :], ALU.subtract).then_inc(
                self.centred.sem, 1)
        dve.wait_ge(self.ln_root.sem, 1)
        dve.reciprocal(self.rs[:], self.root[:]).then_inc(self.centred.sem, 1)
        dve.wait_ge(self.centred.sem, KD + 1)
        dve.wait_ge(self.sq_done.sem, KD)
        for m in range(KD):
            dve.scalar_tensor_tensor(self.out[:, m, :], self.out[:, m, :], c.col("ln_g", m), self.rs[:],
                                     ALU.mult, ALU.mult).then_inc(self.ln_scaled.sem, 1)
            if m >= 1:
                self.low(dve, m - 1)
        self.low(dve, KD - 1)

    def low(self, dve, m):
        dve.wait_ge(self.high.sem, m + 1)
        dve.tensor_tensor(self.parts[1][:, m, :], self.out[:, m, :], self.parts[0][:, m, :].bitcast(F32),
                          ALU.subtract).then_inc(self.ready.sem, 1)

    def scalar(self, act):
        c = self.c
        for m in range(KD):
            act.wait_ge(self.centred.sem, m + 1)
            after(act, self.added, KD + 2 + m - 1 if m >= 2 else 0)
            act.activation(self.sq[:, m % 2, :], self.out[:, m, :], ACT.Square).then_inc(self.sq_done.sem, 1)
        act.wait_ge(self.ln_stat.sem, 2)
        act.activation(self.root[:], c.psum[:, 7, :], ACT.Sqrt, bias=c.eps[:]).then_inc(self.ln_root.sem, 1)
        for m in range(KD):
            act.wait_ge(self.ln_scaled.sem, m + 1)
            act.activation(self.out[:, m, :], self.out[:, m, :], ACT.Silu, bias=c.col("ln_b", m)).then_inc(
                self.silu_done.sem, 1)
            act.wait_ge(self.silu_done.sem, m + 1)
            act.activation(self.parts[0][:, m, :], self.out[:, m, :], ACT.Copy).then_inc(self.high.sem, 1)

    def tensor(self, pe):
        c = self.c
        pe.wait_ge(self.added.sem, KD + 1)
        pe.matmul(c.psum[:, 6, :], c.sq["mean"][:], self.total[:], start=True, stop=True).then_inc(self.ln_stat.sem, 1)
        pe.wait_ge(self.added.sem, 2 * KD + 2)
        pe.matmul(c.psum[:, 7, :], c.sq["mean"][:], self.var[:], start=True, stop=True).then_inc(self.ln_stat.sem, 1)


class PadZeros(Stage):
    def __init__(self, c, buffer, width, signal):
        self.buffer, self.width, self.done = buffer, width, c.flag(signal)

    def gpsimd(self, pool):
        pool.memset(self.buffer[:, :, 0:self.width], 0.0).then_inc(self.done.sem, 1)


class Project(Stage):

    def __init__(self, c, weights, count, parts, source, norm, dest, scale=None, func=None, pad=0):
        self.c, self.weights, self.count, self.parts, self.source = c, weights, count, parts, source
        self.norm, self.dest, self.scale, self.func, self.pad = norm, dest, scale, func, pad
        self.panel0, self.product0 = c.take_panels(count), c.take_products(count)
        self.acted = c.flag("acted")
        self.acted0 = self.acted.reserve(count) if func else 0

    def sync(self, sp):
        c, w = self.c, self.c.dram[self.weights]

        def four(i):
            for j in range(4):
                n0 = self.panel0 + j
                c.load_panel(sp, n0, None, n0 + 4 * i, w[bass.ds(4 * i + j, 1)].rearrange("a p n -> (a p) n"), PANEL)
        repeat(sp, self.count // 4, four)

    def tensor(self, pe):
        c = self.c
        ah, al = self.parts

        def four(i):
            for j in range(4):
                n0, t0 = self.panel0 + j, self.product0 + j
                slot = n0 % SLOTS
                after(pe, c.banks_freed, t0 + 4 * i - (RING_BANKS - 1))
                pe.wait_ge(c.weights_split.sem, n0 + 4 * i + 1)
                for k in range(KD):
                    if j == 0:
                        pe.wait_ge(self.source.ready.sem, self.source.ready0 + k + 1)
                    w = slice(k * P, (k + 1) * P)
                    mm = three(c.nc, c.psum[:, t0 % RING_BANKS, :], c.wh[:, slot, w], c.wl[:, slot, w],
                               ah[:, k, :], al[:, k, :], k == 0, k == KD - 1)
                mm.then_inc(c.panels_used.sem, 1)
        repeat(pe, self.count // 4, four)

    def scalar(self, act):
        c = self.c
        if self.func:
            act.preload_act_table(self.func)

        def four(i):
            for j in range(4):
                c.ahead(c.split_high, act, self.panel0, j, i, 4)
                if self.func:
                    act.wait_ge(c.banks_freed.sem, self.product0 + j + 1 + 4 * i)
                    d = self.dest[:, bass.ds(4 * i + j, 1), self.pad:self.pad + S]
                    act.activation(d, d, self.func).then_inc(self.acted.sem, 1)
        repeat(act, self.count // 4, four)

    def vector(self, dve):
        c = self.c
        dve.wait_ge(self.norm.done.sem, self.norm.done0 + 2)

        def four(i):
            for j in range(4):
                dve.wait_ge(c.panels_used.sem, self.panel0 + j + 1 + 4 * i)
                bank = (self.product0 + j) % RING_BANKS
                d = self.dest[:, bass.ds(4 * i + j, 1), self.pad:self.pad + S]
                r = c.rstd[:].rearrange("p (a n) -> p a n", a=1)
                if self.scale:
                    dve.scalar_tensor_tensor(d, c.psum[:, bank:bank + 1, :], self.scale, r, ALU.mult,
                                             ALU.mult).then_inc(c.banks_freed.sem, 1)
                else:
                    dve.tensor_tensor(d, c.psum[:, bank:bank + 1, :], r, ALU.mult).then_inc(c.banks_freed.sem, 1)
                c.ahead(c.split_low, dve, self.panel0, j, i, 4)
        repeat(dve, self.count // 4, four)


class ProjectTokens(Stage):

    def __init__(self, c, weights, parts, source, dest, tiles_=NT, norm=None, func=None):
        self.c, self.weights, self.parts, self.source = c, weights, parts, source
        self.dest, self.tiles, self.norm, self.func = dest, tiles_, norm, func
        self.panel0, self.product0 = c.take_panels(4), c.take_products(4)
        self.acted = c.flag("acted")
        self.acted0 = self.acted.reserve(tiles_) if func else 0

    def sync(self, sp):
        c, w = self.c, self.c.dram[self.weights]
        for j in range(4):
            n = self.panel0 + j
            c.load_panel(sp, n, None, n, w[j], PANEL)

    def tensor(self, pe):
        c = self.c
        ah, al = self.parts
        after(pe, c.banks_freed, self.product0)
        for j in range(4):
            n = self.panel0 + j
            slot = n % SLOTS
            pe.wait_ge(c.weights_split.sem, n + 1)
            for b in range(2):
                k = 2 * j + b
                pe.wait_ge(self.source.ready.sem, self.source.ready0 + k + 1)
                for i in range(self.tiles):
                    t = slice(i * P, (i + 1) * P)
                    w = slice(b * 512, (b + 1) * 512)
                    mm = three(c.nc, c.psum[:, (self.product0 + i) % RING_BANKS, :], ah[:, k, t], al[:, k, t],
                               c.wh[:, slot, w], c.wl[:, slot, w], k == 0, k == KD - 1)
            mm.then_inc(c.panels_used.sem, 1)

    def scalar(self, act):
        c = self.c
        for j in range(4):
            c.ahead(c.split_high, act, self.panel0, j, 0, 4)
        for i in range(self.tiles):
            if self.func:
                act.wait_ge(c.banks_freed.sem, self.product0 + i + 1)
                act.activation(self.dest[:, i, :], self.dest[:, i, :], self.func).then_inc(self.acted.sem, 1)

    def vector(self, dve):
        c = self.c
        for j in range(4):
            c.ahead(c.split_low, dve, self.panel0, j, 0, 4)
        dve.wait_ge(c.panels_used.sem, self.panel0 + 4)
        if self.norm:
            dve.wait_ge(self.norm.done.sem, self.norm.done0 + 2)
        for i in range(self.tiles):
            bank = (self.product0 + i) % RING_BANKS
            if self.norm:
                dve.tensor_scalar(self.dest[:, i, :], c.psum[:, bank, :], c.rstd_tok[:, i:i + 1], None,
                                  ALU.mult).then_inc(c.banks_freed.sem, 1)
            else:
                dve.tensor_copy(self.dest[:, i, :], c.psum[:, bank, :]).then_inc(c.banks_freed.sem, 1)
        if self.tiles < RING_BANKS:
            dve.wait_ge(c.banks_freed.sem, self.product0 + self.tiles)
            dve.sem_inc(c.banks_freed.sem, RING_BANKS - self.tiles)


class HeadNorm(Stage):

    def __init__(self, c, items, mean, width, wait):
        self.c, self.items, self.mean, self.width, self.held_until = c, items, mean, width, wait
        n = len(items)
        self.squares, self.stat = c.flag("hn_square"), c.flag("hn_stat")
        self.root, self.done = c.flag("hn_root"), c.flag("hn_done")
        self.s0, self.t0 = self.squares.reserve(n), self.stat.reserve(n)
        self.r0, self.d0 = self.root.reserve(n), self.done.reserve(2 * n)

    def tensor(self, pe):
        c = self.c
        for t in range(len(self.items)):
            pe.wait_ge(self.squares.sem, self.s0 + t + 1)
            after(pe, self.root, self.r0 + t - 1)
            pe.matmul(c.psum[:, 6 + t % 2, 0:self.width], c.sq[self.mean][:], c.pre[:, t % 2, 0:self.width],
                      start=True, stop=True).then_inc(self.stat.sem, 1)

    def scalar(self, act):
        c = self.c
        self.held_until(act)
        for t in range(len(self.items) + 1):
            if t < len(self.items):
                act.activation(c.pre[:, t % 2, 0:self.width], self.items[t][0], ACT.Square).then_inc(
                    self.squares.sem, 1)
            if t >= 1:
                u = t - 1
                act.wait_ge(self.stat.sem, self.t0 + u + 1)
                after(act, self.done, self.d0 + 2 * (u - 1))
                act.activation(c.up[:, u % 2, 0:self.width], c.psum[:, 6 + u % 2, 0:self.width], ACT.Sqrt,
                               bias=c.eps[:]).then_inc(self.root.sem, 1)

    def vector(self, dve):
        c = self.c
        self.held_until(dve)
        for t, (z, gain) in enumerate(self.items):
            up = c.up[:, t % 2, 0:self.width]
            dve.wait_ge(self.root.sem, self.r0 + t + 1)
            dve.reciprocal(up, up).then_inc(self.done.sem, 1)
            dve.wait_ge(self.done.sem, self.d0 + 2 * t + 1)
            dve.scalar_tensor_tensor(z, z, gain, up, ALU.mult, ALU.mult).then_inc(self.done.sem, 1)


class Split(Stage):

    def __init__(self, c, source, count, parts, first, waits):
        self.c, self.from_, self.count, self.parts, self.first, self.waits = c, source, count, parts, first, waits
        self.turned, self.high = c.flag("o_turned"), c.flag("o_high")
        self.ready = c.flag("o_ready")
        self.t0, self.h0, self.r0 = self.turned.reserve(count), self.high.reserve(count), self.ready.reserve(count)

    def tensor(self, pe):
        c = self.c
        self.waits(pe)
        for m in range(self.count):
            after(pe, self.ready, self.r0 + m - 1 if m >= 2 else 0)
            for i in range(NT):
                mm = pe.transpose(c.psum[:, 6 + m % 2, i * P:(i + 1) * P], self.from_[:, i, m * P:(m + 1) * P],
                                  c.sq["ident"][:])
            mm.then_inc(self.turned.sem, 1)

    def scalar(self, act):
        c = self.c
        for m in range(self.count):
            act.wait_ge(self.turned.sem, self.t0 + m + 1)
            act.activation(self.parts[0][:, self.first + m, :], c.psum[:, 6 + m % 2, :], ACT.Copy).then_inc(
                self.high.sem, 1)

    def vector(self, dve):
        c = self.c
        for m in range(self.count):
            dve.wait_ge(self.high.sem, self.h0 + m + 1)
            dve.tensor_tensor(self.parts[1][:, self.first + m, :], c.psum[:, 6 + m % 2, :],
                              self.parts[0][:, self.first + m, :].bitcast(F32), ALU.subtract).then_inc(
                self.ready.sem, 1)


class KeysValues(Stage):
    PARTS = 6

    def __init__(self, c, source, norm):
        self.c, self.source, self.norm = c, source, norm
        self.panel0, self.product0 = c.take_panels(self.PARTS), c.take_products(self.PARTS)
        c.take_products(2)
        self.parts = (c.arena("xb_high", 0, [P, KD, S], FR), c.arena("xb_low", 16, [P, KD, S], FR))
        self.cmp = c.arena("kv_cmp", 56, [P, 2, S])
        self.keys = c.arena("keys", 60, [P, 4, S])
        self.values = c.arena("values", 68, [P, 2, NT, P])
        self.vt = c.pre
        self.high, self.ready = c.flag("xb_high_s"), c.flag("xb_ready")
        self.ready0 = 0
        self.key_copies = c.flag("key_copies")
        self.written = c.flag("kv_written")
        self.turned = c.flag("v_turned")
        self.copied = c.flag("v_copied")

    def sync(self, sp):
        c = self.c
        for j in range(self.PARTS):
            n = self.panel0 + j
            c.load_panel(sp, n, None, n, c.dram["w_kv"][j], PANEL)

    def tensor(self, pe):
        c = self.c
        for j in range(self.PARTS):
            n, t = self.panel0 + j, self.product0 + j
            slot = n % SLOTS
            after(pe, c.banks_freed, t - (RING_BANKS - 1))
            pe.wait_ge(c.weights_split.sem, n + 1)
            for k in range(KD):
                pe.wait_ge(self.source.ready.sem, self.source.ready0 + k + 1)
                w = slice(k * P, (k + 1) * P)
                mm = three(c.nc, c.psum[:, t % RING_BANKS, :], c.wh[:, slot, w], c.wl[:, slot, w],
                           c.xh[:, k, :], c.xl[:, k, :], k == 0, k == KD - 1)
            mm.then_inc(c.panels_used.sem, 1)
        for b in range(2):
            after(pe, c.banks_freed, self.product0 + 4 + 2 * b)
            for i in range(NT):
                mm = pe.transpose(c.psum[:, 6 + b, i * P:(i + 1) * P], self.vt[:, b, i * P:(i + 1) * P],
                                  c.sq["ident"][:])
            mm.then_inc(self.turned.sem, 1)

    def scalar(self, act):
        c = self.c
        for j in range(KD):
            if j < self.PARTS:
                c.ahead(c.split_high, act, self.panel0, j, 0, self.PARTS)
            act.activation(self.parts[0][:, j, :], c.x[:, j, :], ACT.Copy, scale=c.col("b_norm", j)).then_inc(
                self.high.sem, 1)
        for b in range(2):
            act.wait_ge(self.turned.sem, b + 1)
            act.activation(self.values[:, b], c.psum[:, 6 + b, :].rearrange("p (t n) -> p t n", t=NT),
                           ACT.Copy).then_inc(self.copied.sem, 1)

    def low(self, dve, m):
        c = self.c
        dve.wait_ge(self.high.sem, m + 1)
        dve.scalar_tensor_tensor(self.parts[1][:, m, :], c.x[:, m, :], c.col("b_norm", m),
                                 self.parts[0][:, m, :].bitcast(F32), ALU.mult, ALU.subtract).then_inc(
            self.ready.sem, 1)

    def vector(self, dve):
        c = self.c
        dve.wait_ge(self.norm.done.sem, self.norm.done0 + 2)
        for j in range(self.PARTS):
            dve.wait_ge(c.panels_used.sem, self.panel0 + j + 1)
            bank = c.psum[:, (self.product0 + j) % RING_BANKS, :]
            if j < 2:
                dve.tensor_tensor(self.cmp[:, j, :], bank, c.rstd[:], ALU.mult).then_inc(c.banks_freed.sem, 1)
            elif j % 2 == 0:
                b = j // 2 - 1
                dve.tensor_tensor(self.keys[0:64, 2 * b, :], bank[0:64], c.rstd[0:64, :], ALU.mult).then_inc(
                    self.written.sem, 1)
                dve.tensor_tensor(self.keys[64:128, 2 * b + 1, :], bank[64:128], c.rstd[64:128, :],
                                  ALU.mult).then_inc(c.banks_freed.sem, 1)
            else:
                b = j // 2 - 1
                dve.tensor_tensor(self.vt[:, b, :], bank, c.rstd[:], ALU.mult).then_inc(c.banks_freed.sem, 1)
            c.ahead(c.split_low, dve, self.panel0, j, 0, self.PARTS)
            self.low(dve, j)
        dve.wait_ge(c.banks_freed.sem, self.product0 + self.PARTS)
        dve.sem_inc(c.banks_freed.sem, 2)
        self.low(dve, 6)
        self.low(dve, 7)

    def gpsimd(self, pool):
        c = self.c
        for b in range(2):
            pool.wait_ge(self.written.sem, b + 1)
            pool.wait_ge(c.banks_freed.sem, self.product0 + 3 + 2 * b)
            pool.dma_start(self.keys[64:128, 2 * b, :], self.keys[0:64, 2 * b, :]).then_inc(self.key_copies.sem, 16)
            pool.dma_start(self.keys[0:64, 2 * b + 1, :], self.keys[64:128, 2 * b + 1, :]).then_inc(
                self.key_copies.sem, 16)


class Compress(Stage):

    def __init__(self, c, kv):
        self.c, self.kv = c, kv
        self.w1 = c.arena("phi_w1", 32, [P, 2, LCMP * HALF])
        self.blk = c.arena("cmp_blocks", 48, [P, 2, LCMP, 32])
        self.pos = c.place("cmp_pos", [P, 2, LCMP])
        self.w2 = c.place("phi_w2", [P, 2, HALF])
        self.vc = c.arena("cmp_values", 56, [P, 2, 4 * HALF])
        self.kc = c.arena("cmp_keys", 58, [P, 2, 32])
        self.hid = c.arena("cmp_hidden", 58.25, [P, 2, 32])
        self.loaded, self.cleared = c.flag("phi_loaded"), c.flag("cmp_cleared")
        self.blocked, self.hidden, self.silued = c.flag("blocked"), c.flag("phi_hidden"), c.flag("phi_silu")
        self.mapped, self.kept = c.flag("phi_mapped"), c.flag("cmp_kept")

    def gpsimd(self, pool):
        c = self.c
        pool.wait_ge(c.banks_freed.sem, self.kv.source.product0 + KD)
        for t, n in ((self.w1, "phi_w1"), (self.pos, "cmp_pos"), (self.w2, "phi_w2")):
            pool.dma_start(t[:], c.dram[n]).then_inc(self.loaded.sem, 16)
        pool.wait_ge(self.blocked.sem, 4)
        pool.memset(self.kc[:], 0.0).then_inc(self.cleared.sem, 1)
        pool.memset(self.vc[:], 0.0).then_inc(self.cleared.sem, 1)

    def vector(self, dve):
        c = self.c
        dve.wait_ge(self.loaded.sem, 48)
        dve.wait_ge(c.banks_freed.sem, self.kv.product0 + 2)
        for j in range(2):
            v = self.kv.cmp[:, j, :].rearrange("p (n l) -> p l n", l=STRIDE)
            for h in range(2):
                dve.tensor_tensor(self.blk[:, j, h * STRIDE:(h + 1) * STRIDE, 0:NCMP], v[:, :, h:h + NCMP],
                                  self.pos[:, j, h * STRIDE:(h + 1) * STRIDE].rearrange(
                                      "p (l a) -> p l a", a=1).to_broadcast([P, STRIDE, NCMP]),
                                  ALU.add).then_inc(self.blocked.sem, 1)
        dve.wait_ge(self.cleared.sem, 2)
        dve.wait_ge(self.mapped.sem, 1)
        for g in range(2):
            dve.tensor_copy(self.kc[:, g, 0:NCMP], c.psum[:, 6 - g, 0:NCMP]).then_inc(self.kept.sem, 1)
        dve.wait_ge(self.mapped.sem, 2)
        for g in range(2):
            for h in range(4):
                q = slice(32 * h, 32 * h + NCMP)
                dve.tensor_copy(self.vc[q, g, h * HALF:(h + 1) * HALF],
                                c.psum[q, 7 - 3 * g, h * HALF:(h + 1) * HALF]).then_inc(self.kept.sem, 1)

    def scalar(self, act):
        act.wait_ge(self.hidden.sem, 1)
        act.activation(self.hid[:, :, 0:NCMP], self.c.psum[:, 4, 0:64].rearrange("p (a n) -> p a n", a=2)[:, :, 0:NCMP],
                       ACT.Silu).then_inc(self.silued.sem, 1)

    def tensor(self, pe):
        c = self.c
        halves = [slice(0, 64), slice(64, 128)]
        for j in range(2):
            pe.wait_ge(self.blocked.sem, 2 * j + 2)
            for l in range(LCMP):
                for q in halves:
                    mm = pe.matmul(c.psum[q, 4, j * 32:j * 32 + NCMP], self.w1[q, j, l * HALF:(l + 1) * HALF],
                                   self.blk[q, j, l, 0:NCMP], start=(l == 0), stop=(l == LCMP - 1),
                                   skip_group_check=True)
        mm.then_inc(self.hidden.sem, 1)
        pe.wait_ge(self.silued.sem, 1)
        after(pe, self.kv.copied, 2)
        for g, q in enumerate(halves):
            for o in halves:
                mm = pe.matmul(c.psum[o, 6 - g, 0:NCMP], self.w2[q, 0, :], self.hid[q, 0, 0:NCMP],
                               start=True, stop=True, skip_group_check=True)
        mm.then_inc(self.mapped.sem, 1)
        for g, q in enumerate(halves):
            for h in range(4):
                mm = pe.matmul(c.psum[32 * h:32 * h + NCMP, 7 - 3 * g, h * HALF:(h + 1) * HALF],
                               self.hid[q, 1, 0:NCMP], self.w2[q, 1, :], start=True, stop=True,
                               skip_group_check=True)
        mm.then_inc(self.mapped.sem, 1)


class Gates(Stage):
    N = 3 * HEADS

    def __init__(self, c, source, norm):
        self.c, self.source, self.norm = c, source, norm
        self.panel0, self.product0 = c.take_panels(1), c.take_products(1)
        c.take_products(3)
        self.gates = c.arena("gates", 59, [P, NT, self.N])
        self.done, self.turned, self.kept = c.flag("gates_done"), c.flag("gates_turned"), c.flag("gates_kept")

    def sync(self, sp):
        c = self.c
        c.load_panel(sp, self.panel0, None, self.panel0, c.dram["w_gates"], KD * self.N)

    def tensor(self, pe):
        c = self.c
        ah, al = self.source.parts
        n, slot = self.panel0, self.panel0 % SLOTS
        after(pe, c.banks_freed, self.product0 - (RING_BANKS - 1))
        pe.wait_ge(c.weights_split.sem, n + 1)
        for k in range(KD):
            w = slice(k * self.N, (k + 1) * self.N)
            mm = three(c.nc, c.psum[0:self.N, self.product0 % RING_BANKS, :], c.wh[:, slot, w], c.wl[:, slot, w],
                       ah[:, k, :], al[:, k, :], k == 0, k == KD - 1)
        mm.then_inc(c.panels_used.sem, 1)
        pe.wait_ge(self.done.sem, 1)
        for i in range(NT):
            mm = pe.transpose(c.psum[:, 5, i * 64:i * 64 + self.N], c.pre[0:self.N, 0, i * P:(i + 1) * P],
                              c.sq["ident"][0:self.N, 0:self.N])
        mm.then_inc(self.turned.sem, 1)

    def scalar(self, act):
        c = self.c
        c.ahead(c.split_high, act, self.panel0, 0, 0, 1)
        act.wait_ge(c.banks_freed.sem, self.product0 + 1)
        act.activation(c.pre[0:self.N, 0, :], c.pre[0:self.N, 0, :], ACT.Sigmoid).then_inc(self.done.sem, 1)

    def vector(self, dve):
        c = self.c
        n = slice(0, self.N)
        dve.wait_ge(c.panels_used.sem, self.panel0 + 1)
        dve.tensor_tensor(c.pre[n, 0, :], c.psum[n, self.product0 % RING_BANKS, :], c.rstd[n, :],
                          ALU.mult).then_inc(c.banks_freed.sem, 1)
        dve.wait_ge(c.banks_freed.sem, self.product0 + 1)
        dve.sem_inc(c.banks_freed.sem, 3)
        c.ahead(c.split_low, dve, self.panel0, 0, 0, 1)
        dve.wait_ge(self.turned.sem, 1)
        dve.tensor_copy(self.gates[:], c.psum[:, 5, 0:256].rearrange("p (i n) -> p i n", i=NT)[:, :, 0:self.N]
                        ).then_inc(self.kept.sem, 1)


class CompressedAttention(Stage):

    def __init__(self, c, q, kv, comp, gates, project):
        self.c, self.q, self.kv, self.comp, self.gates, self.project = c, q, kv, comp, gates, project
        self.bias = c.arena("cmp_bias", 48, [P, NT, HEADS, 32])
        self.o = c.arena("o", 32, [P, NT, D])
        self.t = c.arena("cmp_scores", 0, [P, 2, 256])
        self.prob = c.arena("cmp_probs", 2, [P, 2, 256])
        self.pt = c.arena("cmp_probs_turned", 4, [P, 2, 256])
        self.m = c.arena("cmp_small", 6, [P, 8, 32])
        names = ("cs_loaded", "cs_scores", "cs_scored", "cs_exp", "cs_prob", "cs_turned", "cs_copied", "cs_out",
                 "cs_kept")
        (self.loaded, self.scores, self.scored, self.exped, self.probs, self.turned, self.copied, self.out,
         self.kept) = [c.flag(n) for n in names]
        self.chain = c.flag("vector_chain")

    def gpsimd(self, pool):
        c = self.c
        pool.wait_ge(self.comp.hidden.sem, 1)
        pool.dma_start(self.bias[:], c.dram["cmp_bias"]).then_inc(self.loaded.sem, 16)

    def tensor(self, pe):
        c = self.c
        pe.wait_ge(self.comp.kept.sem, 10)
        pe.wait_ge(self.gates.turned.sem, 1)
        pe.wait_ge(self.gates.kept.sem, 1)
        pe.wait_ge(c.banks_freed.sem, self.project.product0 + KD)
        for u in range(8 + 1):
            if u < 8:
                g, i = divmod(u, NT)
                after(pe, self.scored, u - 1)
                for h in range(8):
                    half = slice(64 * (h % 2), 64 * (h % 2) + 64)
                    mm = pe.matmul(c.psum[:, 4 + 2 * (u % 2), h * 32:(h + 1) * 32] if h % 2 == 0 else
                                   c.psum[:, 5 + 2 * (u % 2), h * 32:(h + 1) * 32],
                                   self.q[half, 4 * g + h // 2, i * P:(i + 1) * P], self.comp.kc[half, g, :],
                                   start=True, stop=True, skip_group_check=True)
                mm.then_inc(self.scores.sem, 1)
            if u >= 1:
                v = u - 1
                pe.wait_ge(self.probs.sem, v + 1)
                for a in range(2):
                    mm = pe.transpose(c.psum[:, 0, a * P:(a + 1) * P], self.prob[:, v % 2, a * P:(a + 1) * P],
                                      c.sq["ident"][:])
                mm.then_inc(self.turned.sem, 1)
                pe.wait_ge(self.copied.sem, v + 1)
                after(pe, self.kept, v)
                for a in range(2):
                    mm = pe.matmul(c.psum[:, 1, a * 256:(a + 1) * 256], self.pt[:, v % 2, a * P:(a + 1) * P],
                                   self.comp.vc[:, v // NT, :], start=True, stop=True, skip_group_check=True)
                mm.then_inc(self.out.sem, 1)

    def scalar(self, act):
        c = self.c
        for u in range(8):
            act.wait_ge(self.scored.sem, 0 + u + 1)
            act.activation(self.prob[:, u % 2, :], self.t[:, u % 2, :], ACT.Exp).then_inc(self.exped.sem, 1)
            act.wait_ge(self.turned.sem, u + 1)
            act.activation(self.pt[:, u % 2, :], c.psum[:, 0, 0:256], ACT.Copy).then_inc(self.copied.sem, 1)

    def vector(self, dve):
        c = self.c
        ch = Chain(dve, self.chain)
        dve.wait_ge(self.loaded.sem, 16)
        dve.wait_ge(self.gates.kept.sem, 1)
        for u in range(8):
            g, i = divmod(u, NT)
            t = self.t[:, u % 2, :].rearrange("p (h n) -> p h n", h=8)
            p = self.prob[:, u % 2, :].rearrange("p (h n) -> p h n", h=8)
            row = lambda k: self.m[:, k, 0:8]
            wide = lambda k: self.m[:, k, 0:8].rearrange("p (h a) -> p h a", a=1).to_broadcast([P, 8, 32])
            dve.wait_ge(self.scores.sem, u + 1)
            for a in range(2):
                s = c.psum[:, 4 + a + 2 * (u % 2), 0:256].rearrange("p (h n) -> p h n", h=8)[:, a:8:2, :]
                ch.link(dve.tensor_tensor(t[:, a:8:2, :], s, self.bias[:, i, 8 * g + a:8 * g + 8:2, :], ALU.add))
            ch.link(dve.tensor_reduce(row(0), t, AXX, ALU.max))
            dve.tensor_tensor(t, t, wide(0), ALU.subtract).then_inc(self.scored.sem, 1)
            dve.wait_ge(self.exped.sem, u + 1)
            ch.link(dve.tensor_reduce(row(1), p, AXX, ALU.add))
            ch.link(dve.reciprocal(row(2), row(1)))
            ch.link(dve.tensor_tensor(row(3), row(2), self.gates.gates[:, i, 8 * g:8 * g + 8], ALU.mult))
            if i == 0:
                ch.link(dve.tensor_scalar(row(3), row(3), c.col("seen"), None, ALU.mult))
            dve.tensor_tensor(p, p, wide(3), ALU.mult).then_inc(self.probs.sem, 1)
            dve.wait_ge(self.out.sem, u + 1)
            dve.tensor_copy(self.o[:, i, g * 512:(g + 1) * 512], c.psum[:, 1, :]).then_inc(self.kept.sem, 1)


class CausalAttention(Stage):

    def __init__(self, c, name, kind, q, tiles_, where, **more):
        self.c, self.kind, self.q, self.tiles, self.more = c, kind, q, tiles_, more
        self.branches = 2 if kind == "sparse" else 1
        self.units = [(h, b, i) for h in range(2) for b in range(self.branches) for i in range(NT)]
        self.U = len(self.units)
        a = where
        self.scores_sb = [c.arena(f"{name}_sc{k}", a[0] + 2 * k, [P, S]) for k in range(3)]
        self.probs_sb = [c.arena(f"{name}_pr{k}", a[1] + 2 * k, [P, S]) for k in range(3)]
        self.pt_sb = [c.arena(f"{name}_pt{k}", a[2] + 2 * k, [P, S]) for k in range(2)]
        self.qs = c.up[:, 0, :]
        self.ks = c.up[:, 1, :]
        self.bias = c.pre
        names = ("at_staged", "at_scores", "at_scored", "at_probs", "at_turned", "at_copied", "at_out", "at_added",
                 "at_coef", "at_fox")
        (self.staged, self.scores, self.scored, self.probs, self.turned, self.copied, self.out, self.added,
         self.coef, self.foxed) = [c.flag(n) for n in names]
        n = tiles_ * self.U
        self.b0 = {s: s.reserve(n) for s in (self.scores, self.scored, self.probs, self.turned, self.copied,
                                             self.out, self.added)}
        self.per_stage = 3 if kind == "sparse" else 2
        self.staged0 = self.staged.reserve(self.per_stage * tiles_)
        self.coef0 = self.coef.reserve(2 * n if kind == "sparse" else n)
        self.fox0 = self.foxed.reserve(n) if kind == "fox" else 0

    def v(self, signal, it, u):
        return self.b0[signal] + u + 1 + self.U * it

    def turns(self, eng, body):
        if self.kind == "sparse":
            half = self.tiles // 2
            for g in range(2):
                def group(i, g=g):
                    body(g * half + i, g)
                with eng.Fori(0, half) as i:
                    group(i)
        else:
            with eng.Fori(0, self.tiles) as i:
                body(i, 0)

    def small(self, k, u):
        return self.c.small[:, 16 * k + u:16 * k + u + 1]

    def tensor(self, pe):
        c, U = self.c, self.U
        self.more["wait_tensor"](pe)

        def body(it, g):
            pe.wait_ge(self.staged.sem, self.staged0 + self.per_stage + self.per_stage * it)
            for s in range(U + 3):
                if s < U:
                    h, b, i = self.units[s]
                    if s >= 3:
                        pe.wait_ge(self.scored.sem, self.v(self.scored, it, s - 3))
                    half = slice(64 * h, 64 * h + 64)
                    width = (i + 1) * P
                    keys = self.more["keys"][half, 2 * b + g, 0:width] if self.kind == "sparse" else \
                        self.ks[half, 0:width]
                    out = c.psum[:, 4 + s % 3, 0:width]
                    mm = pe.matmul(out, self.qs[half, i * P:(i + 1) * P], keys, start=True,
                                   stop=(self.kind == "sparse"))
                    if self.kind == "fox":
                        mm = pe.matmul(c.psum[:, 4 + s % 3, i * P:width], c.sq["ident"][:], self.more["mask"][:],
                                       start=False, stop=True)
                    mm.then_inc(self.scores.sem, 1)
                u = s - 2
                if 0 <= u < U:
                    i = self.units[u][2]
                    pe.wait_ge(self.probs.sem, self.v(self.probs, it, u))
                    if u >= 2:
                        pe.wait_ge(self.copied.sem, self.v(self.copied, it, u - 2))
                    for t in range(i + 1):
                        mm = pe.transpose(c.psum[:, (7, 0)[u % 2], t * P:(t + 1) * P],
                                          self.probs_sb[u % 3][:, t * P:(t + 1) * P], c.sq["ident"][:])
                    mm.then_inc(self.turned.sem, 1)
                u = s - 3
                if 0 <= u < U:
                    h, b, i = self.units[u]
                    pe.wait_ge(self.copied.sem, self.v(self.copied, it, u))
                    if u >= 2:
                        pe.wait_ge(self.added.sem, self.v(self.added, it, u - 2))
                    for t in range(i + 1):
                        vals = self.more["values"][:, b, t, g * HALF:(g + 1) * HALF] if self.kind == "sparse" else \
                            self.more["values"][:, t, bass.ds(it * P + h * HALF, HALF)]
                        mm = pe.matmul(c.psum[:, 1 + u % 2, 0:HALF], self.pt_sb[u % 2][:, t * P:(t + 1) * P], vals,
                                       start=(t == 0), stop=(t == i))
                    mm.then_inc(self.out.sem, 1)
        self.turns(pe, body)

    def scalar(self, act):
        c, U = self.c, self.U
        self.more["wait_scalar"](act)
        act.preload_act_table(ACT.Exp)

        def body(it, g):
            act.activation(self.qs.rearrange("p (a n) -> p a n", a=1), self.q[:, bass.ds(it, 1), :],
                           ACT.Copy).then_inc(self.staged.sem, 1)
            if self.kind == "sparse":
                for h in range(2):
                    act.activation(self.bias[:, h, :], self.more["distance"][:], ACT.Copy,
                                   scale=c.col("slopes", 2 * it + h)).then_inc(self.staged.sem, 1)
            else:
                act.activation(self.ks.rearrange("p (a n) -> p a n", a=1), self.more["keys"][:, bass.ds(it, 1), :],
                               ACT.Copy).then_inc(self.staged.sem, 1)
            for s in range(U + 2):
                if s < U:
                    i = self.units[s][2]
                    width = (i + 1) * P
                    act.wait_ge(self.scored.sem, self.v(self.scored, it, s))
                    if s >= 3:
                        act.wait_ge(self.turned.sem, self.v(self.turned, it, s - 3))
                    act.activation(self.probs_sb[s % 3][:, 0:width], self.scores_sb[s % 3][:, 0:width], ACT.Exp,
                                   bias=self.small(0, s), scale=-1.0, accum_out=self.small(1, s)).then_inc(
                        self.probs.sem, 1)
                u = s - 2
                if 0 <= u < U:
                    width = (self.units[u][2] + 1) * P
                    act.wait_ge(self.turned.sem, self.v(self.turned, it, u))
                    if u >= 2:
                        act.wait_ge(self.out.sem, self.v(self.out, it, u - 2))
                    act.activation(self.pt_sb[u % 2][:, 0:width], c.psum[:, (7, 0)[u % 2], 0:width],
                                   ACT.Copy).then_inc(self.copied.sem, 1)
        self.turns(act, body)

    def vector(self, dve):
        c, U = self.c, self.U
        self.more["wait_vector"](dve)

        def body(it, g):
            dve.wait_ge(self.staged.sem, self.staged0 + self.per_stage + self.per_stage * it)
            for s in range(U + 4):
                if s < U:
                    h, b, i = self.units[s]
                    width = (i + 1) * P
                    dve.wait_ge(self.scores.sem, self.v(self.scores, it, s))
                    if s >= 3:
                        dve.wait_ge(self.probs.sem, self.v(self.probs, it, s - 3))
                    scores, out = c.psum[:, 4 + s % 3, 0:width], self.scores_sb[s % 3][:, 0:width]
                    if self.kind == "sparse":
                        dve.tensor_copy(self.small(4, s), c.eps[:])
                        dve.tensor_tensor_reduce(out, scores, self.bias[:, h, S - width:S], -1.0, BIG, ALU.add,
                                                 ALU.min, self.small(0, s)).then_inc(self.scored.sem, 1)
                    else:
                        at = it * 2 + h
                        dve.scalar_tensor_tensor(out.rearrange("p (a n) -> p a n", a=1),
                                                 self.more["sums"][:, bass.ds(at, 1), 0:width],
                                                 self.more["own_sum"][:, i, bass.ds(at, 1)],
                                                 scores.rearrange("p (a n) -> p a n", a=1),
                                                 ALU.subtract, ALU.subtract).then_inc(self.foxed.sem, 1)
                        dve.wait_ge(self.foxed.sem, self.fox0 + s + 1 + self.U * it)
                        dve.tensor_reduce(self.small(0, s), out, AXX, ALU.min).then_inc(self.scored.sem, 1)
                u = s - 4
                if 0 <= u < U:
                    h, b, i = self.units[u]
                    acc = c.psum[:, 1 + u % 2, 0:HALF]
                    o = self.more["out"][:, i, bass.ds(it * P + h * HALF, HALF)]
                    dve.wait_ge(self.out.sem, self.v(self.out, it, u))
                    if self.kind == "sparse":
                        dve.reciprocal(self.small(2, u), self.small(1, u)).then_inc(self.coef.sem, 1)
                        dve.wait_ge(self.coef.sem, self.coef0 + 2 * u + 1 + 2 * self.U * it)
                        gate = self.more["gates"][:, i, bass.ds((b + 1) * HEADS + it * 2 + h, 1)]
                        dve.tensor_tensor(self.small(3, u), self.small(2, u), gate, ALU.mult).then_inc(
                            self.coef.sem, 1)
                        dve.wait_ge(self.coef.sem, self.coef0 + 2 * u + 2 + 2 * self.U * it)
                        dve.scalar_tensor_tensor(o, acc, self.small(3, u), o, ALU.mult, ALU.add).then_inc(
                            self.added.sem, 1)
                    else:
                        dve.reciprocal(self.small(2, u), self.small(1, u)).then_inc(self.coef.sem, 1)
                        dve.wait_ge(self.coef.sem, self.coef0 + u + 1 + self.U * it)
                        dve.tensor_scalar(o, acc, self.small(2, u), None, ALU.mult).then_inc(self.added.sem, 1)
        self.turns(dve, body)


class Loads(Stage):

    def __init__(self, c, items, wait, signal):
        self.c, self.items, self.held_until = c, items, wait
        self.done = c.flag(signal)
        self.d0 = self.done.total
        self.done.reserve(16 * len(items))

    def value(self):
        return self.d0 + 16 * len(self.items)

    def gpsimd(self, pool):
        self.held_until(pool)
        for dst, src in self.items:
            pool.dma_start(dst, src).then_inc(self.done.sem, 16)


class SpatialGate(Stage):

    def __init__(self, c, loads, u, v, u_stage, v_stage, w, gain, bias, parts):
        self.c, self.loads, self.u, self.v, self.us, self.vs = c, loads, u, v, u_stage, v_stage
        self.w, self.gain, self.bias, self.parts = w, gain, bias, parts
        names = ("sg_masked", "sg_square", "sg_summed", "sg_root", "sg_ready", "sg_mixed", "sg_made", "sg_high",
                 "sg_split")
        (self.masked, self.squared, self.summed, self.root, self.normed, self.mixed, self.made, self.high,
         self.ready) = [c.flag(n) for n in names]
        self.ms = c.small[:, 0:16]
        self.chain = c.flag("vector_chain")

    def gpsimd(self, pool):
        pool.wait_ge(self.us.norm.stat.sem, self.us.norm.stat0 + 1)
        pool.wait_ge(self.loads.done.sem, self.loads.value())
        pool.memset(self.w[64:128, :, 0:64], 0.0).then_inc(self.masked.sem, 1)

    def scalar(self, act):
        c = self.c
        for i in range(NT):
            act.wait_ge(self.vs.acted.sem, self.vs.acted0 + i + 1)
            after(act, self.summed, i - 1)
            act.activation(c.pre[:, i % 2, :], self.v[:, i, :], ACT.Square).then_inc(self.squared.sem, 1)
        act.wait_ge(self.summed.sem, NT)
        act.activation(self.ms, self.ms, ACT.Sqrt, bias=c.eps[:], scale=1.0 / P).then_inc(self.root.sem, 1)
        for g in range(4):
            act.wait_ge(self.made.sem, g + 1)
            act.activation(self.parts[0][:, g, :], c.up[:, g % 2, :], ACT.Copy).then_inc(self.high.sem, 1)

    def vector(self, dve):
        c = self.c
        ch = Chain(dve, self.chain)
        for i in range(NT):
            dve.wait_ge(self.squared.sem, i + 1)
            dve.tensor_reduce(self.ms[:, 4 * i:4 * i + 4], c.pre[:, i % 2, :].rearrange("p (g n) -> p g n", g=4), AXX,
                              ALU.add).then_inc(self.summed.sem, 1)
        dve.wait_ge(self.root.sem, 1)
        ch.link(dve.reciprocal(self.ms, self.ms))
        dve.wait_ge(self.loads.done.sem, self.loads.value())
        for i in range(NT):
            for g in range(4):
                v = self.v[:, i, g * P:(g + 1) * P]
                dve.scalar_tensor_tensor(v, v, self.ms[:, 4 * i + g:4 * i + g + 1], self.gain[:, g * P:(g + 1) * P],
                                         ALU.mult, ALU.mult).then_inc(self.normed.sem, 1)
        dve.wait_ge(self.us.acted.sem, self.us.acted0 + 4)
        for g in range(4):
            dve.wait_ge(self.mixed.sem, g + 1)
            after(dve, self.high, g - 1)
            t = c.pre[:, g % 2, :]
            ch.link(dve.tensor_tensor(t.rearrange("p (i n) -> p i n", i=NT),
                                      c.psum[:, 6 + g % 2, :].rearrange("p (i n) -> p i n", i=NT),
                                      self.bias[:, g:g + 1, :].to_broadcast([P, NT, P]), ALU.add))
            dve.tensor_tensor(c.up[:, g % 2, :], t, self.u[:, g, :], ALU.mult).then_inc(self.made.sem, 1)
            dve.wait_ge(self.high.sem, g + 1)
            dve.tensor_tensor(self.parts[1][:, g, :], c.up[:, g % 2, :], self.parts[0][:, g, :].bitcast(F32),
                              ALU.subtract).then_inc(self.ready.sem, 1)

    def tensor(self, pe):
        c = self.c
        pe.wait_ge(self.masked.sem, 1)
        pe.wait_ge(self.normed.sem, 16)
        for g in range(4):
            after(pe, self.made, g - 1)
            for i in range(NT):
                mm = pe.matmul(c.psum[:, 6 + g % 2, i * P:(i + 1) * P], self.v[:, i, g * P:(g + 1) * P],
                               self.w[:, g, :], start=True, stop=True, skip_group_check=True)
            mm.then_inc(self.mixed.sem, 1)


class LogForget(Stage):

    def __init__(self, c, loads, source, bf, tri, sums, free):
        self.c, self.loads, self.source, self.bf, self.tri, self.sums, self.free = c, loads, source, bf, tri, sums, free
        self.panel0, self.product0 = c.take_panels(1), c.take_products(1)
        c.take_products(3)
        self.own = c.place("own_sums", [P, NT, FOX])
        self.gq = c.place("fox_gain", [P, 1])
        self.z = [c.small[:, 64 + 32 * k:96 + 32 * k] for k in range(4)]
        names = ("lf_z", "lf_abs", "lf_exp", "lf_ln", "lf_done", "lf_sum", "lf_kept")
        (self.zed, self.absed, self.exped, self.lned, self.lf, self.summed, self.kept) = [c.flag(n) for n in names]
        self.chain = c.flag("vector_chain")

    def sync(self, sp):
        self.c.load_panel(sp, self.panel0, None, self.panel0, self.c.dram["e_w_f"], KD * FOX)

    def tensor(self, pe):
        c = self.c
        slot, n = self.panel0 % SLOTS, self.panel0
        pe.wait_ge(c.weights_split.sem, n + 1)
        after(pe, c.banks_freed, self.product0 - (RING_BANKS - 1))
        bank = self.product0 % RING_BANKS
        for i in range(NT):
            for k in range(KD):
                t, w = slice(i * P, (i + 1) * P), slice(k * FOX, (k + 1) * FOX)
                pe.matmul(c.psum[:, bank, i * FOX:(i + 1) * FOX], c.xh[:, k, t], c.wh[:, slot, w],
                          start=(k == 0), stop=False, skip_group_check=True)
                pe.matmul(c.psum[:, bank, i * FOX:(i + 1) * FOX], c.xh[:, k, t], c.wl[:, slot, w],
                          start=False, stop=False, skip_group_check=True)
                mm = pe.matmul(c.psum[:, bank, i * FOX:(i + 1) * FOX], c.xl[:, k, t], c.wh[:, slot, w],
                               start=False, stop=(k == KD - 1), skip_group_check=True)
        mm.then_inc(c.panels_used.sem, 1)

    def scalar(self, act):
        c = self.c
        c.ahead(c.split_high, act, self.panel0, 0, 0, 1)
        act.wait_ge(self.zed.sem, NT)
        act.activation(self.z[1], self.z[0], ACT.Abs).then_inc(self.absed.sem, 1)
        act.wait_ge(self.absed.sem, 1)
        act.activation(self.z[1], self.z[1], ACT.Exp, scale=-1.0).then_inc(self.exped.sem, 1)
        act.wait_ge(self.exped.sem, 1)
        act.activation(self.z[1], self.z[1], ACT.Ln, bias=c.sq["ones"][:, 0:1]).then_inc(self.lned.sem, 1)

    def vector(self, dve):
        c = self.c
        ch = Chain(dve, self.chain)
        bank = self.product0 % RING_BANKS
        c.ahead(c.split_low, dve, self.panel0, 0, 0, 1)
        dve.wait_ge(self.loads.done.sem, self.loads.value())
        dve.wait_ge(c.panels_used.sem, self.panel0 + 1)
        for i in range(NT):
            t = slice(i * FOX, (i + 1) * FOX)
            dve.scalar_tensor_tensor(self.z[0][:, t], c.psum[:, bank, t], c.rstd_tok[:, i:i + 1], self.bf[:],
                                     ALU.mult, ALU.add).then_inc(self.zed.sem, 1)
        dve.wait_ge(self.zed.sem, NT)
        dve.sem_inc(c.banks_freed.sem, 4)
        ch.link(dve.tensor_scalar(self.gq[:], c.col("e_gq"), 1.0 / 8, None, ALU.mult))
        ch.link(dve.tensor_scalar(self.z[2], self.z[0], 0.0, None, ALU.min))
        dve.wait_ge(self.lned.sem, 1)
        dve.tensor_tensor(self.z[3], self.z[2], self.z[1], ALU.subtract).then_inc(self.lf.sem, 1)


class ForgetSums(Stage):
    def __init__(self, c, lf):
        self.c, self.lf = c, lf

    def tensor(self, pe):
        c, s = self.c, self.lf
        lf, tri = s.z[3].rearrange("p (i h) -> p i h", i=NT), s.tri
        pe.wait_ge(s.lf.sem, 1)
        for h in range(FOX):
            after(pe, s.kept, h - 1)
            for j in range(NT):
                mm = pe.matmul(c.psum[:, 4 + h % 2, j * P:S], lf[:, j, h:h + 1].to_broadcast([P, P]), tri[:, 0:S - j * P],
                               start=(j == 0), stop=(j == NT - 1))
            mm.then_inc(s.summed.sem, 1)
        pe.wait_ge(s.kept.sem, FOX - 1)
        for i in range(NT):
            for j in range(i + 1):
                mm = pe.matmul(c.psum[:, 4, i * FOX:(i + 1) * FOX], tri[:, 0:P] if j == i else tri[:, P:2 * P],
                               lf[:, j, :], start=(j == 0), stop=(j == i), skip_group_check=True)
        mm.then_inc(s.summed.sem, 1)

    def scalar(self, act):
        c, s = self.c, self.lf
        s.free(act)
        for h in range(FOX):
            act.wait_ge(s.summed.sem, h + 1)
            act.activation(s.sums[:, h, :], c.psum[:, 4 + h % 2, :], ACT.Copy).then_inc(s.kept.sem, 1)
        act.wait_ge(s.summed.sem, FOX + 1)
        act.activation(s.own[:], c.psum[:, 4, 0:NT * FOX].rearrange("p (i h) -> p i h", i=NT), ACT.Copy).then_inc(
            s.kept.sem, 1)


class PoolAndConv(Stage):
    W = 16

    def __init__(self, c, loads, zc, hgg, zc_stage, hgg_stage, parts, wpool, inv, pads):
        self.c, self.loads, self.zc, self.hgg, self.zs, self.hs = c, loads, zc, hgg, zc_stage, hgg_stage
        self.parts, self.wpool, self.inv, self.pads = parts, wpool, inv, pads
        self.t = [c.arena(f"pool_t{k}", 74 + 2.5 * k, [P, self.W + S]) for k in range(2)]
        self.xg = c.arena("pool_xg", 65, [P, 4, 2 + S])
        self.ready, self.high = c.flag("pc_ready"), c.flag("pc_high")
        self.ready0 = 0
        self.pooled, self.mapped, self.made = c.flag("pooled"), c.flag("pool_mapped"), c.flag("pc_made")
        self.chain = c.flag("vector_chain")

    def gpsimd(self, pool):
        c = self.c
        pool.memset(self.t[0][:, 0:self.W], 0.0).then_inc(self.pads.sem, 1)
        pool.memset(self.t[1][:, 0:self.W], 0.0).then_inc(self.pads.sem, 1)
        pool.memset(self.xg[:, :, 0:2], 0.0).then_inc(self.pads.sem, 1)

    def vector(self, dve):
        c, W = self.c, self.W
        ch = Chain(dve, self.chain)
        dve.wait_ge(self.pads.sem, 4)
        dve.wait_ge(self.loads.done.sem, self.loads.value())
        dve.wait_ge(c.banks_freed.sem, self.zs.product0 + 4)
        for g, w in enumerate(POOLS):
            src, k = self.zc[:, g, :], 0
            for level in range(g + 1):
                dst = self.t[k]
                shift = 1 << level
                ch.link(dve.tensor_tensor(dst[:, W:], src[:, W:], src[:, W - shift:W + S - shift], ALU.add))
                src, k = dst, 1 - k
            mean = self.t[k]
            ch.link(dve.tensor_scalar(mean[:, W:], src[:, W:], 1.0 / w, None, ALU.mult))
            ch.link(dve.tensor_tensor(mean[:, W:2 * W], src[:, W:2 * W], self.inv[:, g, :], ALU.mult))
            dve.tensor_tensor(self.zc[:, g, W:], mean[:, W:], self.zc[:, g, W:], ALU.subtract).then_inc(
                self.pooled.sem, 1)
            dve.wait_ge(self.pooled.sem, g + 1)
        dve.wait_ge(c.banks_freed.sem, self.hs.product0 + 12)
        for t in range(4):
            hd, gb, gc = (self.hgg[:, 4 * q + t, :] for q in range(3))
            x = self.xg[:, t, :]
            ch.link(dve.tensor_tensor(x[:, 2:], gc, hd, ALU.mult))
            ch.link(dve.tensor_scalar(hd, x[:, 0:S], c.col("conv_w", t), None, ALU.mult))
            ch.link(dve.scalar_tensor_tensor(hd, x[:, 1:1 + S], c.col("conv_w", 4 + t), hd, ALU.mult, ALU.add))
            ch.link(dve.scalar_tensor_tensor(hd, x[:, 2:2 + S], c.col("conv_w", 8 + t), hd, ALU.mult, ALU.add))
            dve.tensor_tensor(gb, hd, gb, ALU.mult).then_inc(self.made.sem, 1)
        dve.wait_ge(self.made.sem, 4)
        for g in range(4):
            dve.wait_ge(self.high.sem, g + 1)
            dve.scalar_tensor_tensor(self.parts[1][:, g, :], c.psum[:, 6 + g % 2, :], c.col("s_pool", g),
                                     self.parts[0][:, g, :].bitcast(F32), ALU.mult, ALU.subtract).then_inc(
                self.ready.sem, 1)
        for t in range(4):
            dve.wait_ge(self.high.sem, 4 + t + 1)
            dve.tensor_tensor(self.parts[1][:, 4 + t, :], self.hgg[:, 4 + t, :],
                              self.parts[0][:, 4 + t, :].bitcast(F32), ALU.subtract).then_inc(self.ready.sem, 1)

    def scalar(self, act):
        c = self.c
        for g in range(4):
            act.wait_ge(self.mapped.sem, g + 1)
            act.activation(self.parts[0][:, g, :], c.psum[:, 6 + g % 2, :], ACT.Copy, scale=c.col("s_pool", g)
                           ).then_inc(self.high.sem, 1)
        for t in range(4):
            act.wait_ge(self.made.sem, t + 1)
            act.activation(self.parts[0][:, 4 + t, :], self.hgg[:, 4 + t, :], ACT.Copy).then_inc(self.high.sem, 1)

    def tensor(self, pe):
        c = self.c
        pe.wait_ge(self.loads.done.sem, self.loads.value())
        for g in range(4):
            pe.wait_ge(self.pooled.sem, g + 1)
            after(pe, self.ready, g - 1)
            pe.matmul(c.psum[:, 6 + g % 2, :], self.wpool[:, g, :], self.zc[:, g, self.W:], start=True,
                      stop=True).then_inc(self.mapped.sem, 1)


class Memory(Stage):

    def __init__(self, c, layer, wait, mixer):
        self.c, self.layer, self.held_until, self.mixer = c, layer, wait, mixer
        n = f"mem{layer}_"
        self.m = c.arena(n + "x", 64, [P, KD, MEM])
        self.parts = (c.arena(n + "high", 72, [P, KD, MEM], FR), c.arena(n + "low", 80, [P, KD, MEM], FR))
        self.sq = c.arena(n + "sq", 60, [P, 2, MEM])
        self.sum = c.arena(n + "sum", 62, [P, MEM])
        self.rs = c.arena(n + "rs", 63, [P, MEM])
        names = ("mem_in", "mem_squared", "mem_summed", "mem_stat", "mem_root", "mem_normed", "mem_high", "mem_ready")
        (self.loaded, self.squared, self.summed, self.stat, self.root, self.normed, self.high,
         self.ready) = [c.flag(x) for x in names]
        self.s = [s.reserve(k) for s, k in ((self.loaded, 16), (self.squared, KD), (self.summed, KD + 1),
                                            (self.stat, 1), (self.root, 1), (self.normed, KD + 1), (self.high, KD),
                                            (self.ready, KD))]
        self.ready0 = self.s[7]

    def gpsimd(self, pool):
        self.held_until(pool)
        pool.dma_start(self.m[:], self.c.dram["memT"]).then_inc(self.loaded.sem, 16)
        pool.memset(self.sum[:], 0.0).then_inc(self.summed.sem, 1)
        pool.wait_ge(self.loaded.sem, self.s[0] + 16)
        for k in range(KD):
            pool.tensor_tensor(self.sq[:, k % 2, :], self.m[:, k, :], self.m[:, k, :], ALU.mult).then_inc(
                self.squared.sem, 1)
            pool.wait_ge(self.squared.sem, self.s[1] + k + 1)
            pool.wait_ge(self.summed.sem, self.s[2] + k + 1)
            pool.tensor_tensor(self.sum[:], self.sum[:], self.sq[:, k % 2, :], ALU.add).then_inc(self.summed.sem, 1)

    def tensor(self, pe):
        c = self.c
        pe.wait_ge(self.summed.sem, self.s[2] + KD + 1)
        pe.wait_ge(self.mixer.ready.sem, self.mixer.ready0 + KD)
        pe.matmul(c.psum[:, 6, 0:MEM], c.sq["mean"][:], self.sum[:], start=True, stop=True).then_inc(self.stat.sem, 1)

    def scalar(self, act):
        c = self.c
        act.wait_ge(self.stat.sem, self.s[3] + 1)
        act.activation(self.rs[:], c.psum[:, 6, 0:MEM], ACT.Sqrt, bias=c.eps[:]).then_inc(self.root.sem, 1)
        for k in range(KD):
            act.wait_ge(self.normed.sem, self.s[5] + k + 2)
            act.activation(self.parts[0][:, k, :], self.m[:, k, :], ACT.Copy).then_inc(self.high.sem, 1)

    def vector(self, dve):
        c = self.c
        dve.wait_ge(self.root.sem, self.s[4] + 1)
        dve.reciprocal(self.rs[:], self.rs[:]).then_inc(self.normed.sem, 1)
        dve.wait_ge(self.normed.sem, self.s[5] + 1)
        for k in range(KD):
            dve.scalar_tensor_tensor(self.m[:, k, :], self.m[:, k, :], c.col("g_mem", 8 * self.layer + k), self.rs[:],
                                     ALU.mult, ALU.mult).then_inc(self.normed.sem, 1)
        for k in range(KD):
            dve.wait_ge(self.high.sem, self.s[6] + k + 1)
            dve.tensor_tensor(self.parts[1][:, k, :], self.m[:, k, :], self.parts[0][:, k, :].bitcast(F32),
                              ALU.subtract).then_inc(self.ready.sem, 1)


class MemoryKeys(Stage):

    def __init__(self, c, weights, mem, dest):
        self.c, self.weights, self.mem, self.dest = c, weights, mem, dest
        self.panel0, self.product0 = c.take_panels(4), c.take_products(4)

    def sync(self, sp):
        c = self.c
        for j in range(4):
            n = self.panel0 + j
            c.load_panel(sp, n, None, n, c.dram[self.weights][j], PANEL)

    def tensor(self, pe):
        c = self.c
        ah, al = self.mem.parts
        for j in range(4):
            n, t = self.panel0 + j, self.product0 + j
            after(pe, c.banks_freed, t - (RING_BANKS - 1))
            pe.wait_ge(c.weights_split.sem, n + 1)
            for k in range(KD):
                pe.wait_ge(self.mem.ready.sem, self.mem.ready0 + k + 1)
                w = slice(k * P, (k + 1) * P)
                mm = three(c.nc, c.psum[:, t % RING_BANKS, 0:MEM], c.wh[:, n % SLOTS, w], c.wl[:, n % SLOTS, w],
                           ah[:, k, :], al[:, k, :], k == 0, k == KD - 1)
            mm.then_inc(c.panels_used.sem, 1)

    def scalar(self, act):
        for j in range(4):
            self.c.ahead(self.c.split_high, act, self.panel0, j, 0, 4)

    def vector(self, dve):
        c = self.c
        for j in range(4):
            dve.wait_ge(c.panels_used.sem, self.panel0 + j + 1)
            dve.tensor_copy(self.dest[:, j, :], c.psum[:, (self.product0 + j) % RING_BANKS, 0:MEM]).then_inc(
                c.banks_freed.sem, 1)
            c.ahead(c.split_low, dve, self.panel0, j, 0, 4)


class MemoryAttention(Stage):
    SCALE = 1.0 / float(np.sqrt(P))

    def __init__(self, c, layer, q, keys, values, parts, wait):
        self.c, self.q, self.keys, self.values, self.parts, self.held_until = c, q, keys, values, parts, wait
        n = f"xa{layer}_"
        self.probs = [c.arena(n + f"p{k}", 56 + k, [P, MEM]) for k in range(3)]
        self.pt = [c.arena(n + f"pt{k}", 24 + 4 * k, [P, 2, S]) for k in range(2)]
        names = ("xm_scores", "xm_max", "xm_exp", "xm_sum", "xm_probs", "xm_turned", "xm_copied", "xm_out",
                 "xm_high", "xm_ready")
        (self.scores, self.maxed, self.exped, self.summed, self.probd, self.turned, self.copied, self.out,
         self.high, self.ready) = [c.flag(x) for x in names]
        u = 4 * NT
        self.b = [s.reserve(k) for s, k in ((self.scores, u), (self.maxed, 2 * u), (self.exped, u), (self.summed, u),
                                            (self.probd, u), (self.turned, u), (self.copied, u), (self.out, 4),
                                            (self.high, 4), (self.ready, 4))]
        self.ready0 = self.b[9]

    def tensor(self, pe):
        c, U = self.c, 4 * NT
        self.held_until(pe)
        for s in range(U + 3):
            if s < U:
                h, i = divmod(s, NT)
                if s >= 2:
                    pe.wait_ge(self.exped.sem, self.b[2] + s - 1)
                pe.matmul(c.psum[:, 4 + s % 2, 0:MEM], self.q[:, h, i * P:(i + 1) * P], self.keys[:, h, :],
                          start=True, stop=True).then_inc(self.scores.sem, 1)
            u = s - 2
            if 0 <= u < U:
                pe.wait_ge(self.probd.sem, self.b[4] + u + 1)
                if u >= 2:
                    pe.wait_ge(self.copied.sem, self.b[6] + u - 1)
                for a in range(2):
                    mm = pe.transpose(c.psum[:, (7, 0)[u % 2], a * P:(a + 1) * P],
                                      self.probs[u % 3][:, a * P:(a + 1) * P], c.sq["ident"][:])
                mm.then_inc(self.turned.sem, 1)
            u = s - 3
            if u >= 0 and u % NT == NT - 1:
                h = u // NT
                pe.wait_ge(self.copied.sem, self.b[6] + u + 1)
                if h >= 2:
                    pe.wait_ge(self.ready.sem, self.b[9] + h - 1)
                for a in range(2):
                    mm = pe.matmul(c.psum[:, 1 + h % 2, :], self.values[:, a, h * P:(h + 1) * P],
                                   self.pt[h % 2][:, a, :], start=(a == 0), stop=(a == 1))
                mm.then_inc(self.out.sem, 1)

    def scalar(self, act):
        c, U = self.c, 4 * NT
        self.held_until(act)
        for s in range(U + 4):
            if s < U:
                act.wait_ge(self.maxed.sem, self.b[1] + 2 * s + 2)
                if s >= 3:
                    act.wait_ge(self.turned.sem, self.b[5] + s - 2)
                act.activation(self.probs[s % 3][:], c.psum[:, 4 + s % 2, 0:MEM], ACT.Exp,
                               bias=c.small[:, 16 + s:17 + s], scale=self.SCALE,
                               accum_out=c.small[:, 32 + s:33 + s]).then_inc(self.exped.sem, 1)
            u = s - 2
            if 0 <= u < U:
                h, i = divmod(u, NT)
                act.wait_ge(self.turned.sem, self.b[5] + u + 1)
                if h >= 2 and i == 0:
                    act.wait_ge(self.out.sem, self.b[7] + h - 1)
                act.activation(self.pt[h % 2][:, :, i * P:(i + 1) * P],
                               c.psum[:, (7, 0)[u % 2], 0:MEM].rearrange("p (a n) -> p a n", a=2),
                               ACT.Copy).then_inc(self.copied.sem, 1)
            u = s - 4
            if u >= 0 and u % NT == NT - 1:
                h = u // NT
                act.wait_ge(self.out.sem, self.b[7] + h + 1)
                act.activation(self.parts[0][:, h, :], c.psum[:, 1 + h % 2, :], ACT.Copy).then_inc(self.high.sem, 1)

    def vector(self, dve):
        c, U = self.c, 4 * NT
        self.held_until(dve)
        for s in range(U + 5):
            if s < U:
                dve.wait_ge(self.scores.sem, self.b[0] + s + 1)
                dve.tensor_reduce(c.small[:, s:s + 1], c.psum[:, 4 + s % 2, 0:MEM], AXX, ALU.max).then_inc(
                    self.maxed.sem, 1)
                dve.wait_ge(self.maxed.sem, self.b[1] + 2 * s + 1)
                dve.tensor_scalar(c.small[:, 16 + s:17 + s], c.small[:, s:s + 1], -self.SCALE, None,
                                  ALU.mult).then_inc(self.maxed.sem, 1)
            u = s - 1
            if 0 <= u < U:
                dve.wait_ge(self.exped.sem, self.b[2] + u + 1)
                dve.reciprocal(c.small[:, 48 + u:49 + u], c.small[:, 32 + u:33 + u]).then_inc(self.summed.sem, 1)
                dve.wait_ge(self.summed.sem, self.b[3] + u + 1)
                dve.tensor_scalar(self.probs[u % 3][:], self.probs[u % 3][:], c.small[:, 48 + u:49 + u], None,
                                  ALU.mult).then_inc(self.probd.sem, 1)
            u = s - 5
            if u >= 0 and u % NT == NT - 1:
                self.low(dve, u // NT)

    def low(self, dve, h):
        c = self.c
        dve.wait_ge(self.high.sem, self.b[8] + h + 1)
        dve.tensor_tensor(self.parts[1][:, h, :], c.psum[:, 1 + h % 2, :], self.parts[0][:, h, :].bitcast(F32),
                          ALU.subtract).then_inc(self.ready.sem, 1)


class From:

    def __init__(self, ready, ready0):
        self.ready, self.ready0 = ready, ready0


def plan(c):
    stages = []

    def add(stage):
        stages.append(stage)
        return stage

    def feed_forward(w_in, w_out, source, norm, gain, last=False):
        gated = add(Gated(c, w_in, KF, source, norm, hidden=hidden))
        return add(Residual(c, w_out, hidden, From(gated.ready, gated.ready0), [7, 7, 8], 1, gain, last=last))

    def memory_attention(layer, free, mixed, w_out, mixer_parts, source):
        mem = add(Memory(c, layer, free, source))
        res = add(Residual(c, w_out, mixer_parts, source, [KD], 1, ("g_xa", KD * layer)))
        mk = c.arena(f"mk{layer}", 48, [P, XAH, MEM])
        mv = c.arena(f"mv{layer}", 52, [P, 2, 512])
        q = c.arena(f"xq{layer}", 16, [P, XAH, S])
        keys = add(MemoryKeys(c, f"xa_wk{layer}", mem, mk))
        vals = add(ProjectTokens(c, f"xa_wv{layer}", mem.parts, mem, mv, tiles_=2))
        norm = add(Norm(c, res))
        qs = add(Project(c, f"xa_wq{layer}", XAH, (c.xh, c.xl), res, norm, q))

        def projected(eng):
            eng.wait_ge(c.banks_freed.sem, qs.product0 + XAH)
        items = [(mk[:, h, :], c.col("xa_gk", layer)) for h in range(XAH)]
        add(HeadNorm(c, items, "mean128", MEM, projected))
        items = [(q[:, h, :], c.col("xa_gq", layer)) for h in range(XAH)]
        hn = add(HeadNorm(c, items, "mean128", S, projected))
        parts = (c.arena(f"xo_high{layer}", 0, [P, XAH, S], FR), c.arena(f"xo_low{layer}", 8, [P, XAH, S], FR))

        def normed(eng):
            eng.wait_ge(hn.done.sem, hn.d0 + 2 * XAH)
            eng.wait_ge(c.banks_freed.sem, qs.product0 + XAH)
        att = add(MemoryAttention(c, layer, q, mk, mv, parts, normed))
        res = add(Residual(c, f"xa_wo{layer}", parts, att, [XAH], 2, ("g_ffn", KD * layer)))
        return res, add(Norm(c, res))

    add(Load(c))
    hidden = (c.arena("hidden_high", 0, [P, KF, S], FR), c.arena("hidden_low", 44, [P, KF, S], FR))

    start = add(Prepare(c, ("a_norm", 0)))
    norm = add(Norm(c, start))
    conv_at = len(stages)
    pw1 = add(Gated(c, "pw1", KD, start, norm, conv=True))
    conv = add(Convolution(c, pw1))
    pw1.conv = conv.padded
    stages.insert(conv_at, PadZeros(c, conv.padded, PAD, "pads"))
    res = add(Residual(c, "pw2", conv.parts, conv, [KD], 1, ("ffn_norm", 0), bias="pw2_b"))
    norm = add(Norm(c, res))
    res = feed_forward("ffn_in0", "ffn_out0", res, norm, ("kv_norm", 0))
    norm = add(Norm(c, res))

    kv = add(KeysValues(c, res, norm))
    comp = add(Compress(c, kv))
    q = c.arena("queries", 72, [P, KD, S])
    qp = add(Project(c, "w_q", KD, kv.parts, kv, norm, q, scale=0.125))
    gates = add(Gates(c, kv, norm))
    cmp_att = add(CompressedAttention(c, q, kv, comp, gates, qp))
    distance = c.arena("distance", 24, [P, S])

    def gates_done(pool):
        pool.wait_ge(gates.turned.sem, 1)
    dist = add(Loads(c, [(distance[:], c.dram["distance"])], gates_done, "distance_in"))

    def wait_tensor(pe):
        pe.wait_ge(cmp_att.kept.sem, 8)
        pe.wait_ge(kv.key_copies.sem, 64)
        pe.wait_ge(kv.copied.sem, 2)

    def wait_scalar(act):
        act.wait_ge(dist.done.sem, dist.value())
    att = add(CausalAttention(c, "sparse", "sparse", q, KD, (8, 14, 20), keys=kv.keys, values=kv.values,
                              distance=distance, gates=gates.gates, out=cmp_att.o, wait_tensor=wait_tensor,
                              wait_scalar=wait_scalar, wait_vector=lambda dve: None))
    done = att.v(att.added, KD - 1, att.U - 1)
    parts = (c.arena("o_high", 0, [P, KD, S], FR), c.arena("o_low", 16, [P, KD, S], FR))
    split = add(Split(c, cmp_att.o, KD, parts, 0, lambda pe: pe.wait_ge(att.added.sem, done)))
    res = add(Residual(c, "w_o", parts, From(split.ready, split.r0), [KD], 1, ("ffn_norm", KD)))
    norm = add(Norm(c, res))
    res = feed_forward("ffn_in1", "ffn_out1", res, norm, None)
    norm = add(Norm(c, res))

    start = add(Prepare(c, ("g_mix", 0), norm=norm))
    norm = add(Norm(c, start))
    parts = (c.arena("ey_high", 0, [P, KD, S], FR), c.arena("ey_low", 16, [P, KD, S], FR))
    u, v = c.arena("u", 32, [P, 4, S]), c.arena("v", 40, [P, NT, 512])
    ws, gv, bs = c.arena("w_s", 48, [P, 4, P]), c.arena("g_v", 50, [P, 512]), c.arena("b_s", 52, [P, 4, P])
    qk, vv = c.arena("fox_qk", 54, [P, 8, S]), c.arena("fox_v", 70, [P, NT, 512])
    tri = c.arena("tri", 84, [P, S])
    bf, mask = c.place("b_f", [P, FOX]), c.place("mask", [P, P])
    hidden_read = res.product0 + KD

    def arena_free(pool):
        pool.wait_ge(c.banks_freed.sem, hidden_read)
    loads = add(Loads(c, [(ws[:], c.dram["e_w_s"]), (gv[:], c.dram["e_g_v"].to_broadcast([P, 512])),
                          (bs[:], c.dram["e_b_s"].to_broadcast([P, 4, P])), (tri[:], c.dram["tri"]),
                          (bf[:], c.dram["e_b_f"].to_broadcast([P, FOX])), (mask[:], c.dram["mask"])],
                      arena_free, "even_in"))
    up = add(Project(c, "e_w_u", 4, (c.xh, c.xl), start, norm, u, func=ACT.Gelu_apprx_tanh))
    vp = add(ProjectTokens(c, "e_w_v", (c.xh, c.xl), start, v, norm=norm, func=ACT.Gelu_apprx_tanh))
    qkp = add(Project(c, "e_w_qk", 8, (c.xh, c.xl), start, norm, qk))
    add(ProjectTokens(c, "e_w_vv", (c.xh, c.xl), start, vv, norm=norm))
    sums = c.arena("sums", 32, [P, FOX, S])
    spatial = SpatialGate(c, loads, u, v, up, vp, ws, gv, bs, parts)

    def sums_free(act):
        act.wait_ge(spatial.ready.sem, 4)
    lf = add(LogForget(c, loads, None, bf, tri, sums, sums_free))
    add(spatial)
    add(ForgetSums(c, lf))

    def qk_done(eng):
        eng.wait_ge(c.banks_freed.sem, qkp.product0 + 8)
    items = [(qk[:, t, :], lf.gq[:] if t < 4 else c.col("e_gk")) for t in range(8)]
    hn = add(HeadNorm(c, items, "mean64", S, qk_done))
    o = c.place("fox_o", [P, NT, 512], offset=c.xh_at)

    def fox_tensor(pe):
        pe.wait_ge(hn.done.sem, hn.d0 + 16)
        pe.wait_ge(lf.kept.sem, FOX + 1)
        pe.wait_ge(c.banks_freed.sem, lf.product0 + 4)

    def fox_other(eng):
        eng.wait_ge(hn.done.sem, hn.d0 + 16)
        eng.wait_ge(lf.kept.sem, FOX + 1)
    c.fox_pt = (48, 78, 84)
    att = add(CausalAttention(c, "fox", "fox", qk[:, 0:4, :], 4, (48, 78, 84), keys=qk[:, 4:8, :], values=vv,
                              sums=sums, own_sum=lf.own, mask=mask, out=o, wait_tensor=fox_tensor,
                              wait_scalar=fox_other, wait_vector=fox_other))
    fox_done = att.v(att.added, 3, att.U - 1)
    split = add(Split(c, o, 4, parts, 4, lambda pe: pe.wait_ge(att.added.sem, fox_done)))
    res, norm = memory_attention(0, lambda pool: pool.wait_ge(att.added.sem, fox_done), None, "e_w_out", parts,
                                 From(split.ready, split.r0 - 4))
    res = feed_forward("ffn2_in0", "ffn2_out0", res, norm, ("g_mix", KD))
    norm = add(Norm(c, res))

    parts = (c.arena("oy_high", 0, [P, KD, S], FR), c.arena("oy_low", 16, [P, KD, S], FR))
    hgg = c.arena("hgg", 32, [P, 12, S])
    zc = c.arena("zc", 56, [P, 4, PoolAndConv.W + S])
    wpool, inv = c.arena("w_pool", 80, [P, 4, P]), c.arena("inverse_counts", 82, [P, 4, PoolAndConv.W])
    free1 = res.product0 + KD

    def arena_free1(pool):
        pool.wait_ge(c.banks_freed.sem, free1)
    loads = add(Loads(c, [(wpool[:], c.dram["o_w_pool"]), (inv[:], c.dram["inverse_counts"])], arena_free1,
                      "odd_in"))
    pads = add(PadZeros(c, zc, PoolAndConv.W, "odd_pads"))
    zs = add(Project(c, "o_w_c", 4, (c.xh, c.xl), res, norm, zc, pad=PoolAndConv.W))
    hs = add(Project(c, "o_w_hgg", 12, (c.xh, c.xl), res, norm, hgg))
    pc = add(PoolAndConv(c, loads, zc, hgg, zs, hs, parts, wpool, inv, pads.done))
    res, norm = memory_attention(1, lambda pool: pool.wait_ge(pc.ready.sem, 8), None, "o_w_out", parts, pc)
    res = feed_forward("ffn2_in1", "ffn2_out1", res, norm, None, last=True)
    add(Store(c, res))
    c.last_panel = c.panels
    return stages


def program(nc, dram):
    with ExitStack() as ctx:
        stages = plan(Core(nc, ctx, dram))
        block = ctx.enter_context(nc.Block())

        @block.sync
        def _(sp):
            for stage in stages:
                stage.sync(sp)

        @block.gpsimd
        def _(pool):
            for stage in stages:
                stage.gpsimd(pool)

        @block.scalar
        def _(act):
            for stage in stages:
                stage.scalar(act)

        @block.vector
        def _(dve):
            for stage in stages:
                stage.vector(dve)

        @block.tensor
        def _(pe):
            for stage in stages:
                stage.tensor(pe)


def blocks(w, m=P):
    k, n = w.shape
    return w.reshape(k // P, P, n // m, m).transpose(2, 1, 0, 3).reshape(n // m, P, k // P * m)


def rows(w, per=2):
    k, n = w.shape
    return w.reshape(k // P // per, per, P, n).transpose(0, 2, 1, 3).reshape(k // P // per, P, per * n)


def tiles(v):
    return v.reshape(-1, P).T


def narrow(w):
    k, n = w.shape
    return w.reshape(k // P, P, n).transpose(1, 0, 2).reshape(P, k // P * n)


def twice(a):
    return np.concatenate([a, a], axis=0)


def pairs(a, b):
    return np.stack([blocks(a), blocks(b)], axis=1).reshape(-1, P, PANEL)


def constants():
    p = np.arange(P)[:, None]
    ident = np.eye(P)
    ones = np.ones((P, P))
    squares = np.stack([ident, ones, ones / D, np.kron(np.eye(2), np.ones((HALF, HALF))) / HALF, ones / P])
    slopes = 2.0 ** (-8.0 * (np.arange(HEADS) + 1) / HEADS)
    away = np.arange(S)[None, :] - (S - P) - p
    distance = np.where(away <= 0, away, NEG)
    t = (np.arange(NT)[None, :] * P + p)[:, :, None, None]
    n = np.arange(32)[None, None, None, :]
    dist = t - (n * STRIDE + LCMP - 1)
    cmp_bias = np.where((dist >= 0) & (n < NCMP), -slopes.astype(np.float32)[None, None, :, None] * dist, NEG)
    tri = np.concatenate([(p <= np.arange(P)[None, :]).astype(float)] + [ones] * (NT - 1), axis=1)
    mask = np.where(np.arange(P)[None, :] > p, NEG, 0.0)
    counts = np.stack([1.0 / np.minimum(np.arange(PoolAndConv.W) + 1, w) for w in POOLS])
    inverse = np.broadcast_to(counts[None], (P, len(POOLS), PoolAndConv.W))
    f = {"squares": squares, "distance": distance, "cmp_bias": cmp_bias, "tri": tri, "mask": mask,
         "inverse_counts": inverse}
    f = {k: np.ascontiguousarray(v.astype(np.float32)) for k, v in f.items()}
    return f, np.broadcast_to(slopes.astype(np.float32)[None, :], (P, HEADS)), (p >= LCMP - 1).astype(np.float32)


def lay_out(inputs):
    i = {k: np.asarray(v) for k, v in inputs.items()}
    arrays, slopes, seen = constants()
    dw = i["a_dw_w"][0].reshape(TAPS, KD, P).transpose(2, 1, 0).reshape(P, KD * TAPS)
    table = {
        "a_norm": tiles(i["a_norm"][0]), "pw1_b": tiles(i["a_pw1_b"][0]), "dw_w": dw, "dw_b": tiles(i["a_dw_b"][0]),
        "ln_g": tiles(i["a_ln_g"][0]), "ln_b": tiles(i["a_ln_b"][0]), "pw2_b": tiles(i["a_pw2_b"][0]),
        "kv_norm": tiles(i["kv_norm"]), "b_norm": tiles(i["b_norm"][0]), "ffn_norm": tiles(i["ffn_norm"]),
        "final_norm": tiles(i["final_norm"]), "g_mix": tiles(i["g_mix_2"]), "g_xa": tiles(i["g_xa_2"]),
        "g_mem": tiles(i["g_mem_2"]), "xa_gq": tiles(i["xa_gq_2"]), "xa_gk": tiles(i["xa_gk_2"]),
        "g_ffn": tiles(i["g_ffn_2"]), "e_gq": twice(i["e_g_qn_2"][0][:, None]), "e_gk": twice(i["e_g_kn_2"][0][:, None]),
        "s_pool": tiles(i["o_s_pool_2"][0]), "conv_w": tiles(i["o_conv_w_2"][0]), "slopes": slopes, "seen": seen,
    }
    arrays["cols"] = np.concatenate([table[n] for n, _ in COLUMNS], axis=1)
    arrays["xT"] = i["x"][0].T.reshape(KD, P, S).transpose(1, 0, 2)
    arrays["memT"] = i["mem_2"][0].T.reshape(KD, P, MEM).transpose(1, 0, 2)
    pw1 = i["a_pw1_w"][0]
    arrays["pw1"] = pairs(pw1[:, D:], pw1[:, :D])
    arrays["pw2"] = blocks(i["a_pw2_w"][0])
    for l in range(2):
        w = i["ffn_w_in"][l]
        arrays[f"ffn_in{l}"] = pairs(w[:, :F], w[:, F:])
        arrays[f"ffn_out{l}"] = blocks(i["ffn_w_out"][l])
        arrays[f"ffn2_in{l}"] = pairs(i["w_gate_2"][l], i["w_up_2"][l])
        arrays[f"ffn2_out{l}"] = blocks(i["w_down_2"][l])
        arrays[f"xa_wq{l}"] = blocks(i["xa_wq_2"][l])
        arrays[f"xa_wk{l}"] = blocks(i["xa_wkv_2"][l][:, :512])
        arrays[f"xa_wv{l}"] = rows(i["xa_wkv_2"][l][:, 512:])
        arrays[f"xa_wo{l}"] = blocks(i["xa_wo_2"][l]).reshape(4, 2, P, 512).transpose(0, 2, 1, 3).reshape(4, P, PANEL)
    arrays["w_kv"] = blocks(i["w_kv"])
    arrays["w_q"] = blocks(i["b_w_in"][0][:, :D])
    arrays["w_gates"] = narrow(i["b_w_in"][0][:, D:])
    arrays["w_o"] = blocks(i["b_w_out"][0])
    w1 = [i[n].reshape(LCMP, HALF, HALF).transpose(1, 0, 2).reshape(HALF, LCMP * HALF) for n in ("phi_k_w1", "phi_v_w1")]
    arrays["phi_w1"] = twice(np.stack(w1, axis=1))
    arrays["phi_w2"] = twice(np.stack([i["phi_k_w2"], i["phi_v_w2"]], axis=1))
    arrays["cmp_pos"] = twice(np.stack([i["cmp_pos_k"].T, i["cmp_pos_v"].T], axis=1))
    e = i["e_w_in_2"][0]
    arrays["e_w_u"], arrays["e_w_v"] = blocks(e[:, :512]), rows(e[:, 512:1024])
    arrays["e_w_qk"], arrays["e_w_vv"] = blocks(e[:, 1024:2048]), rows(e[:, 2048:2560])
    arrays["e_w_f"] = narrow(e[:, 2560:])
    arrays["e_b_f"] = i["e_b_f_2"]
    arrays["e_g_v"] = i["e_g_v_2"]
    arrays["e_w_s"] = i["e_w_s_2"][0].transpose(2, 0, 1)
    arrays["e_b_s"] = i["e_b_s_2"]
    arrays["e_w_out"] = blocks(i["e_w_out_2"][0])
    o = i["o_w_in_2"][0]
    arrays["o_w_c"], arrays["o_w_hgg"] = blocks(o[:, :512]), blocks(o[:, 512:])
    arrays["o_w_pool"] = i["o_w_pool_2"][0].transpose(1, 0, 2)
    arrays["o_w_out"] = blocks(i["o_w_out_2"][0])
    return {k: np.ascontiguousarray(v) for k, v in arrays.items()}


def kernel(**inputs):
    import concourse.bacc as bacc
    from concourse.bass_utils import run_bass_kernel_spmd

    arrays = lay_out(inputs)
    nc = bacc.Bacc("TRN2", target_bir_lowering=False, num_devices=1)
    dram = {n: nc.dram_tensor(n, a.shape, mybir.dt.from_np(a.dtype), kind="ExternalInput").ap()
            for n, a in arrays.items()}
    dram["out"] = nc.dram_tensor("out", [KD, P, S], F32, kind="ExternalOutput").ap()
    program(nc, dram)
    result = run_bass_kernel_spmd(nc, [arrays], core_ids=[0]).results[0]["out"]
    return np.ascontiguousarray(result.reshape(D, S).T)[None]
```

```python
from contextlib import ExitStack

import numpy as np
import concourse.bass as bass
from concourse import mybir

F32 = mybir.dt.float32
FR = mybir.dt.float32r
ALU = mybir.AluOpType
ACT = mybir.ActivationFunctionType
AXX = mybir.AxisListType.X

P = 128
S = 512
NT = S // P
D = 1024
KD = D // P
F = 2816
KF = F // P
HALF = 64
HEADS = 16
FOX = 8
XAH = 4
MEM = 256
TAPS = 31
NCMP = 31
LCMP = 32
STRIDE = 16
EPS = 1e-6
NEG = -1e30
BIG = 3e38
POOLS = (2, 4, 8, 16)
PAD = TAPS - 1

SLOTS = 4
PANEL = 1024
ARENA = 88
RING_BANKS = 4

COLUMNS = [
    ("a_norm", KD), ("pw1_b", 2 * KD), ("dw_w", KD * TAPS), ("dw_b", KD), ("ln_g", KD), ("ln_b", KD),
    ("pw2_b", KD), ("kv_norm", KD), ("b_norm", KD), ("ffn_norm", 2 * KD), ("final_norm", KD),
    ("g_mix", 2 * KD), ("g_xa", 2 * KD), ("g_mem", 2 * KD), ("xa_gq", 2), ("xa_gk", 2), ("g_ffn", 2 * KD),
    ("e_gq", 1), ("e_gk", 1), ("s_pool", 4), ("conv_w", 12), ("slopes", HEADS), ("seen", 1), ("halves", 2),
]
AT = {}
_n = 0
for _name, _w in COLUMNS:
    AT[_name] = _n
    _n += _w
NCOLS = _n
SQUARES = ["ident", "ones", "mean", "mean64", "mean128"]


class Signal:

    def __init__(self, sem):
        self.sem, self.total = sem, 0

    def reserve(self, n):
        base = self.total
        self.total += n
        return base


def after(eng, signal, value):
    if isinstance(value, int) and value <= 0:
        return
    eng.wait_ge(signal.sem, value)


def repeat(eng, n, body, straight=False, peel=0):
    if straight or n - peel == 1:
        peel = n
    for i in range(peel):
        body(i)
    if peel < n:
        with eng.Fori(peel, n) as i:
            body(i)


class Core:

    def __init__(self, nc, ctx, dram):
        self.nc, self.dram = nc, dram
        self.at = 16512
        self.ctx = ctx
        self.flags = {}
        self.x = self.place("x", [P, KD, S])
        self.xh_at = self.at
        self.xh = self.place("xh", [P, KD, S], FR)
        self.xl_at = self.at
        self.xl = self.place("xl", [P, KD, S], FR)
        self.raw = self.place("raw", [P, SLOTS, PANEL])
        self.wh = self.place("wh", [P, SLOTS, PANEL], FR)
        self.wl = self.place("wl", [P, SLOTS, PANEL], FR)
        self.rstd = self.place("rstd", [P, S])
        self.rstd_tok = self.place("rstd_tok", [P, NT])
        self.root_tok = self.place("root_tok", [P, NT])
        self.ssq = self.place("ssq", [P, S])
        self.square_at = self.at
        self.square = self.place("square", [P, 2, S])
        self.pre = self.place("pre", [P, 2, S])
        self.up_at = self.at
        self.up = self.place("up", [P, 2, S])
        self.cols = self.place("cols", [P, NCOLS])
        self.sq = {n: self.place(n, [P, P]) for n in SQUARES}
        self.small = self.place("small", [P, 256])
        self.eps = self.place("eps", [P, 1])
        self.arena0 = self.at
        self.at += ARENA * 1024
        self.psum = ctx.enter_context(nc.psum_tensor("psum", [P, 8, S], F32))
        self.landed = [Signal(ctx.enter_context(nc.semaphore(f"landed{i}"))) for i in range(SLOTS)]
        self.weights_high = self.flag("weights_high")
        self.weights_split = self.flag("weights_split")
        self.panels_used = self.flag("panels_used")
        self.banks_freed = self.flag("banks_freed")
        self.consts = self.flag("consts")
        self.panels = SLOTS
        self.products = RING_BANKS
        self.last_panel = None

    def place(self, name, shape, dtype=F32, offset=None):
        size = int(np.prod(shape[1:])) * 4
        if offset is None:
            offset = self.at
            self.at = (offset + size + 31) // 32 * 32
            assert self.at <= 229344, (name, self.at)
        assert offset + size <= 229344, (name, offset + size - 229344)
        return self.nc.alloc_sbuf_tensor_at(name, shape, dtype, offset=offset)

    def arena(self, name, kib, shape, dtype=F32):
        return self.place(name, shape, dtype, offset=int(self.arena0 + kib * 1024))

    def flag(self, name):
        if name not in self.flags:
            self.flags[name] = Signal(self.ctx.enter_context(self.nc.semaphore(name)))
        return self.flags[name]

    def col(self, name, i=0):
        return self.cols[:, bass.ds(AT[name] + i, 1)]

    def take_panels(self, n):
        base, self.panels = self.panels, self.panels + n
        return base

    def take_products(self, n):
        base, self.products = self.products, self.products + n
        return base

    def load_panel(self, sp, n0, lap, n, source, width):
        slot = n0 % SLOTS
        after(sp, self.weights_split, n - (SLOTS - 1))
        sp.dma_start(self.raw[:, slot, 0:width], source).then_inc(self.landed[slot].sem, 16)

    def split_high(self, act, n0, lap, n):
        slot = n0 % SLOTS
        act.wait_ge(self.landed[slot].sem, 16 * lap)
        after(act, self.panels_used, n - (SLOTS - 1))
        self.nc.scalar.activation(self.wh[:, slot, :], self.raw[:, slot, :], ACT.Copy).then_inc(
            self.weights_high.sem, 1)

    def split_low(self, dve, n0, lap, n):
        slot = n0 % SLOTS
        dve.wait_ge(self.weights_high.sem, n + 1)
        self.nc.vector.tensor_tensor(self.wl[:, slot, :], self.raw[:, slot, :],
                                     self.wh[:, slot, :].bitcast(F32), ALU.subtract).then_inc(
            self.weights_split.sem, 1)

    def ahead(self, split, eng, base, j, i, per):
        m = base + j + SLOTS
        if isinstance(i, int):
            m += i * per
            if m < self.last_panel:
                split(eng, m, m // SLOTS, m)
        else:
            split(eng, m, m // SLOTS + i * (per // SLOTS), m + i * per)


def three(nc, out, ah, al, bh, bl, start, stop):
    nc.tensor.matmul(out, ah, bh, start=start, stop=False)
    nc.tensor.matmul(out, ah, bl, start=False, stop=False)
    return nc.tensor.matmul(out, al, bh, start=False, stop=stop)


class Stage:

    def sync(self, sp):
        pass

    def gpsimd(self, pool):
        pass

    def scalar(self, act):
        pass

    def vector(self, dve):
        pass

    def tensor(self, pe):
        pass


class Load(Stage):

    def __init__(self, c):
        self.c = c
        self.cols_in = c.flag("cols_in")
        c.x_in = [c.flag(f"x_in{q}") for q in range(KD // 2)]
        self.eps_set = c.flag("eps_set")

    def sync(self, sp):
        c = self.c
        sp.dma_start(c.cols[:], c.dram["cols"]).then_inc(self.cols_in.sem, 16)
        for q, arrived in enumerate(c.x_in):
            at = slice(2 * q, 2 * q + 2)
            sp.dma_start(c.x[:, at, :], c.dram["xT"][:, at, :]).then_inc(arrived.sem, 16)

    def gpsimd(self, pool):
        c = self.c
        pool.memset(c.eps[:], EPS).then_inc(self.eps_set.sem, 1)
        for k, n in enumerate(SQUARES):
            pool.dma_start(c.sq[n][:], c.dram["squares"][k]).then_inc(c.consts.sem, 16)

    def scalar(self, act):
        act.sem_inc(self.c.weights_high.sem, SLOTS)
        act.wait_ge(self.cols_in.sem, 16)
        act.wait_ge(self.eps_set.sem, 1)

    def vector(self, dve):
        dve.sem_inc(self.c.weights_split.sem, SLOTS)
        dve.sem_inc(self.c.banks_freed.sem, RING_BANKS)
        dve.wait_ge(self.cols_in.sem, 16)

    def tensor(self, pe):
        pe.sem_inc(self.c.panels_used.sem, SLOTS)


class FirstPanels(Stage):

    def __init__(self, c):
        self.c = c

    def scalar(self, act):
        for n in range(SLOTS, 2 * SLOTS):
            self.c.split_high(act, n, 1, n)
        act.wait_ge(self.c.consts.sem, 16 * len(SQUARES))

    def vector(self, dve):
        for n in range(SLOTS, 2 * SLOTS):
            self.c.split_low(dve, n, 1, n)
        dve.wait_ge(self.c.consts.sem, 16 * len(SQUARES))

    def tensor(self, pe):
        pe.wait_ge(self.c.consts.sem, 16 * len(SQUARES))


class Prepare(Stage):

    def __init__(self, c, gain, norm=None):
        self.c, self.gain, self.norm = c, gain, norm
        self.high, self.ready = c.flag("x_high"), c.flag("x_ready")
        self.high0, self.ready0 = self.high.reserve(KD), self.ready.reserve(KD)
        self.squared, self.summed = c.flag("squared"), c.flag("summed")
        self.squared0, self.summed0 = self.squared.reserve(KD), self.summed.reserve(KD + 1)
        self.x_new = c.flag("x_new")
        self.x_new0 = self.x_new.reserve(KD) if norm else 0

    def gpsimd(self, pool):
        c = self.c
        if self.norm:
            pool.wait_ge(self.norm.stat.sem, self.norm.stat0 + 1)
        pool.memset(c.ssq[:], 0.0).then_inc(self.summed.sem, 1)
        for m in range(KD):
            pool.wait_ge(self.summed.sem, self.summed0 + 1 + m)
            pool.wait_ge(self.squared.sem, self.squared0 + m + 1)
            pool.tensor_tensor(c.ssq[:], c.ssq[:], c.square[:, m % 2, :], ALU.add).then_inc(self.summed.sem, 1)

    def scalar(self, act):
        c = self.c
        for m in range(KD):
            self.arrived(act, m)
            c.nc.scalar.activation(c.xh[:, m, :], c.x[:, m, :], ACT.Copy, scale=c.col(*self.at(m))).then_inc(
                self.high.sem, 1)
            after(act, self.summed, self.summed0 + m)
            act.activation(c.square[:, m % 2, :], c.x[:, m, :], ACT.Square).then_inc(self.squared.sem, 1)

    def arrived(self, eng, m):
        if self.norm:
            eng.wait_ge(self.x_new.sem, self.x_new0 + m + 1)
        else:
            eng.wait_ge(self.c.x_in[m // 2].sem, 16)

    def at(self, m):
        return self.gain[0], self.gain[1] + m

    def vector(self, dve):
        c = self.c
        for m in range(KD):
            if self.norm:
                if m == 0:
                    dve.wait_ge(self.norm.done.sem, self.norm.done0 + 1)
                c.nc.vector.scalar_tensor_tensor(c.x[:, m, :], c.x[:, m, :], c.col("final_norm", m), c.rstd[:],
                                                 ALU.mult, ALU.mult).then_inc(self.x_new.sem, 1)
                if m >= 2:
                    self.low(dve, m - 2)
        for m in range(KD - 2 if self.norm else 0, KD):
            self.low(dve, m)

    def low(self, dve, m):
        c = self.c
        dve.wait_ge(self.high.sem, self.high0 + m + 1)
        c.nc.vector.scalar_tensor_tensor(c.xl[:, m, :], c.x[:, m, :], c.col(*self.at(m)),
                                         c.xh[:, m, :].bitcast(F32), ALU.mult, ALU.subtract).then_inc(
            self.ready.sem, 1)


class Norm(Stage):

    def __init__(self, c, source, now=False):
        self.c, self.source, self.now, self.step = c, source, now, 0
        c.last_norm = self
        self.stat, self.root, self.done = c.flag("stat"), c.flag("root_s"), c.flag("rstd_s")
        self.spread = c.flag("rstd_spread")
        self.stat0, self.root0, self.done0 = self.stat.reserve(1), self.root.reserve(1), self.done.reserve(2)
        self.spread0 = self.spread.reserve(1)

    def late(self, pe, j):
        if j == 0 and self.step == 0:
            self.sums(pe)
        elif j == 1 and self.step == 1:
            self.along(pe)

    def sums(self, pe):
        c, s = self.c, self.source
        self.step = 1
        pe.wait_ge(s.summed.sem, s.summed0 + KD + 1)
        after(pe, self.root, self.root0)
        for i in range(NT):
            mm = pe.matmul(c.psum[:, 5, i:i + 1], c.ssq[:, i * P:(i + 1) * P], c.sq["mean"][:, 0:1],
                           start=(i == 0), stop=(i == NT - 1), skip_group_check=True)
        mm.then_inc(self.stat.sem, 1)

    def along(self, pe):
        c = self.c
        self.step = 2
        pe.wait_ge(self.done.sem, self.done0 + 1)
        for i in range(NT):
            mm = pe.matmul(c.psum[:, 4, i * P:(i + 1) * P], c.rstd_tok[:, i:i + 1].to_broadcast([P, P]),
                           c.sq["ident"][:], start=True, stop=True, skip_group_check=True)
        mm.then_inc(self.spread.sem, 1)

    def tensor(self, pe):
        if self.now:
            self.sums(pe)
            self.along(pe)

    def scalar(self, act):
        c = self.c
        act.wait_ge(self.stat.sem, self.stat0 + 1)
        after(act, self.done, self.done0)
        c.nc.scalar.activation(c.root_tok[:], c.psum[:, 5, 0:NT], ACT.Sqrt, bias=c.eps[:]).then_inc(self.root.sem, 1)

    def vector(self, dve):
        c = self.c
        dve.wait_ge(self.root.sem, self.root0 + 1)
        dve.reciprocal(c.rstd_tok[:], c.root_tok[:]).then_inc(self.done.sem, 1)
        dve.wait_ge(self.spread.sem, self.spread0 + 1)
        dve.tensor_copy(c.rstd[:], c.psum[:, 4, :]).then_inc(self.done.sem, 1)
        dve.wait_ge(self.done.sem, self.done0 + 2)


class Gated(Stage):

    def __init__(self, c, weights, pairs, source, norm, hidden=None, conv=None):
        self.c, self.weights, self.pairs, self.source, self.norm = c, weights, pairs, source, norm
        self.hidden, self.conv, self.taps = hidden, conv, None
        self.panel0, self.product0 = c.take_panels(2 * pairs), c.take_products(2 * pairs)
        self.gated = c.flag("gated")
        self.made = c.flag("made")
        self.high = c.flag("hidden_high")
        self.ready = c.flag("hidden_ready")
        self.gated0, self.made0 = self.gated.reserve(pairs), self.made.reserve(pairs)
        if hidden:
            self.high0, self.ready0 = self.high.reserve(pairs), self.ready.reserve(pairs)

    def sync(self, sp):
        c, w = self.c, self.c.dram[self.weights]

        def four(i):
            for j in range(4):
                n0 = self.panel0 + j
                c.load_panel(sp, n0, None, n0 + 4 * i, w[bass.ds(4 * i + j, 1)].rearrange("a p n -> (a p) n"), PANEL)
        repeat(sp, self.pairs // 2, four)

    def tensor(self, pe):
        c = self.c

        def four(i):
            for j in range(4):
                n0, t0 = self.panel0 + j, self.product0 + j
                after(pe, c.banks_freed, t0 + 4 * i - (RING_BANKS - 1))
                pe.wait_ge(c.weights_split.sem, n0 + 4 * i + 1)
                out = c.psum[:, t0 % RING_BANKS, :]
                slot = n0 % SLOTS
                for k in range(KD):
                    if j == 0:
                        pe.wait_ge(self.source.ready.sem, self.source.ready0 + k + 1)
                    w = slice(k * P, (k + 1) * P)
                    mm = three(c.nc, out, c.wh[:, slot, w], c.wl[:, slot, w], c.xh[:, k, :], c.xl[:, k, :],
                               k == 0, k == KD - 1)
                mm.then_inc(c.panels_used.sem, 1)
                if isinstance(i, int):
                    self.norm.late(pe, j)
        repeat(pe, self.pairs // 2, four, peel=1)

    def scalar(self, act):
        c = self.c

        act.preload_act_table(ACT.Sigmoid if self.conv else ACT.Silu)

        def four(i):
            for r in range(2):
                c.ahead(c.split_high, act, self.panel0, 2 * r, i, 4)
                act.wait_ge(c.banks_freed.sem, self.product0 + 2 * r + 1 + 4 * i)
                func = ACT.Sigmoid if self.conv else ACT.Silu
                more = {"bias": c.col("pw1_b", KD + r + 2 * i)} if self.conv else {}
                c.nc.scalar.activation(c.pre[:, r, :], c.pre[:, r, :], func, **more).then_inc(self.gated.sem, 1)
                c.ahead(c.split_high, act, self.panel0, 2 * r + 1, i, 4)
                if self.taps:
                    self.taps.diagonals(act, 8)
                    if i >= 1:
                        self.taps.scale_taps(act, 6)
                if self.hidden:
                    act.wait_ge(self.made.sem, self.made0 + r + 1 + 2 * i)
                    c.nc.scalar.activation(self.hidden[0][:, bass.ds(2 * i + r, 1), :],
                                           c.up[:, r:r + 1, :], ACT.Copy).then_inc(self.high.sem, 1)
        repeat(act, self.pairs // 2, four, straight=bool(self.taps))

    def vector(self, dve):
        c = self.c
        dve.wait_ge(self.norm.done.sem, self.norm.done0 + 2)

        def four(i):
            for r in range(2):
                dve.wait_ge(c.panels_used.sem, self.panel0 + 2 * r + 1 + 4 * i)
                bank = (self.product0 + 2 * r) % RING_BANKS
                dve.tensor_tensor(c.pre[:, r, :], c.psum[:, bank, :], c.rstd[:], ALU.mult).then_inc(
                    c.banks_freed.sem, 1)
                c.ahead(c.split_low, dve, self.panel0, 2 * r, i, 4)
                if self.taps:
                    self.taps.some(dve, 5, i)
                dve.wait_ge(c.panels_used.sem, self.panel0 + 2 * r + 2 + 4 * i)
                bank = (self.product0 + 2 * r + 1) % RING_BANKS
                dve.tensor_tensor(c.up[:, r, :], c.psum[:, bank, :], c.rstd[:], ALU.mult).then_inc(
                    c.banks_freed.sem, 1)
                c.ahead(c.split_low, dve, self.panel0, 2 * r + 1, i, 4)
                dve.wait_ge(c.banks_freed.sem, self.product0 + 2 * r + 2 + 4 * i)
                dve.wait_ge(self.gated.sem, self.gated0 + r + 1 + 2 * i)
                if self.conv:
                    dve.scalar_tensor_tensor(self.conv[:, bass.ds(2 * i + r, 1), PAD:PAD + S],
                                             c.up[:, r:r + 1, :], c.col("pw1_b", r + 2 * i), c.pre[:, r:r + 1, :],
                                             ALU.add, ALU.mult).then_inc(self.made.sem, 1)
                    self.taps.some(dve, 5, i)
                else:
                    dve.tensor_tensor(c.up[:, r, :], c.up[:, r, :], c.pre[:, r, :], ALU.mult).then_inc(
                        self.made.sem, 1)
                    dve.wait_ge(self.high.sem, self.high0 + r + 1 + 2 * i)
                    at = bass.ds(2 * i + r, 1)
                    dve.tensor_tensor(self.hidden[1][:, at, :], c.up[:, r:r + 1, :],
                                      self.hidden[0][:, at, :].bitcast(F32), ALU.subtract).then_inc(self.ready.sem, 1)
        repeat(dve, self.pairs // 2, four, straight=bool(self.taps))


class Residual(Stage):

    def __init__(self, c, weights, act_parts, source, cuts, pack, gain, bias=None, last=False):
        self.c, self.weights, self.parts, self.source = c, weights, act_parts, source
        self.cuts, self.pack, self.gain, self.bias, self.last = cuts, pack, gain, bias, last
        self.norm = c.last_norm
        self.per = KD * len(cuts) // pack
        self.panel0, self.product0 = c.take_panels(self.per), c.take_products(KD)
        self.body = 4 * pack if len(cuts) == 1 else 4
        self.turns = KD // self.body
        self.body_panels = self.body * len(cuts) // pack
        self.within = c.flag("within_panel")
        self.within0 = self.within.reserve(KD - KD // pack)
        self.high, self.ready = c.flag("x_high"), c.flag("x_ready")
        self.squared, self.summed = c.flag("squared"), c.flag("summed")
        if gain:
            self.high0, self.ready0 = self.high.reserve(KD), self.ready.reserve(KD)
        if not last:
            self.squared0, self.summed0 = self.squared.reserve(KD), self.summed.reserve(KD + 1)

    def sync(self, sp):
        c, w = self.c, self.c.dram[self.weights]

        def turn(i):
            for j in range(self.body_panels):
                n0 = self.panel0 + j
                if len(self.cuts) == 1:
                    width = self.cuts[0] * self.pack * P
                    src = w[bass.ds(self.body_panels * i + j, 1)].rearrange("a p n -> (a p) n")
                else:
                    m, q = divmod(j, len(self.cuts))
                    lo = sum(self.cuts[:q]) * P
                    width = self.cuts[q] * P
                    src = w[bass.ds(self.body * i + m, 1), :, lo:lo + width].rearrange("a p n -> (a p) n")
                c.load_panel(sp, n0, None, n0 + self.body_panels * i, src, width)
        repeat(sp, self.turns, turn, straight=self.last)

    def tensor(self, pe):
        c = self.c
        ah, al = self.parts

        def turn(i):
            for m in range(self.body):
                t0 = self.product0 + m
                after(pe, c.banks_freed, t0 + self.body * i - (RING_BANKS - 1))
                out = c.psum[:, t0 % RING_BANKS, :]
                for q, blocks in enumerate(self.cuts):
                    j = (m * len(self.cuts) + q) // self.pack
                    n0 = self.panel0 + j
                    slot = n0 % SLOTS
                    if m % self.pack == 0:
                        pe.wait_ge(c.weights_split.sem, n0 + self.body_panels * i + 1)
                    for b in range(blocks):
                        k = sum(self.cuts[:q]) + b
                        if m == 0:
                            pe.wait_ge(self.source.ready.sem, self.source.ready0 + k + 1)
                        at = ((m % self.pack) * blocks + b) * P
                        mm = three(c.nc, out, c.wh[:, slot, at:at + P], c.wl[:, slot, at:at + P],
                                   ah[:, k, :], al[:, k, :], k == 0, k == sum(self.cuts) - 1)
                    if m % self.pack == self.pack - 1:
                        mm.then_inc(c.panels_used.sem, 1)
                    else:
                        mm.then_inc(self.within.sem, 1)
        repeat(pe, self.turns, turn, straight=self.last)

    def panels_of(self, m):
        if self.pack > 1:
            return [m // self.pack] if m % self.pack == self.pack - 1 else []
        return [m * len(self.cuts) + q for q in range(len(self.cuts))]

    def gpsimd(self, pool):
        c = self.c
        if self.last:
            return
        pool.wait_ge(self.norm.stat.sem, self.norm.stat0 + 1)
        pool.memset(c.ssq[:], 0.0).then_inc(self.summed.sem, 1)

        def turn(i):
            for m in range(self.body):
                at = bass.ds(self.body * i + m, 1)
                pool.wait_ge(c.banks_freed.sem, self.product0 + m + 1 + self.body * i)
                pool.wait_ge(self.summed.sem, self.summed0 + m + self.body * i)
                pool.tensor_tensor(c.square[:, m % 2, :].rearrange("p (a n) -> p a n", a=1), c.x[:, at, :],
                                   c.x[:, at, :], ALU.mult).then_inc(self.squared.sem, 1)
                pool.wait_ge(self.summed.sem, self.summed0 + 1 + m + self.body * i)
                pool.wait_ge(self.squared.sem, self.squared0 + m + 1 + self.body * i)
                pool.tensor_tensor(c.ssq[:], c.ssq[:], c.square[:, m % 2, :], ALU.add).then_inc(self.summed.sem, 1)
        repeat(pool, self.turns, turn)

    def scalar(self, act):
        c = self.c

        def turn(i):
            for m in range(self.body):
                if self.gain:
                    at = bass.ds(self.body * i + m, 1)
                    act.wait_ge(c.banks_freed.sem, self.product0 + m + 1 + self.body * i)
                    c.nc.scalar.activation(c.xh[:, at, :], c.x[:, at, :], ACT.Copy,
                                           scale=c.col(self.gain[0], self.gain[1] + m + self.body * i)).then_inc(
                        self.high.sem, 1)
                for j in self.panels_of(m):
                    c.ahead(c.split_high, act, self.panel0, j, i, self.body_panels)
        repeat(act, self.turns, turn, straight=self.last)

    def vector(self, dve):
        c = self.c

        def turn(i):
            for m in range(self.body):
                at = bass.ds(self.body * i + m, 1)
                last = (m // self.pack * len(self.cuts)) + len(self.cuts)
                if m % self.pack == self.pack - 1:
                    dve.wait_ge(c.panels_used.sem, self.panel0 + last + self.body_panels * i)
                else:
                    dve.wait_ge(self.within.sem, self.within0 + m // self.pack + 1)
                bank = (self.product0 + m) % RING_BANKS
                out = c.psum[:, bank:bank + 1, :]
                if self.bias:
                    dve.scalar_tensor_tensor(c.x[:, at, :], out, c.col(self.bias, m + self.body * i), c.x[:, at, :],
                                             ALU.add, ALU.add).then_inc(c.banks_freed.sem, 1)
                else:
                    dve.tensor_tensor(c.x[:, at, :], out, c.x[:, at, :], ALU.add).then_inc(c.banks_freed.sem, 1)
                for j in self.panels_of(m):
                    c.ahead(c.split_low, dve, self.panel0, j, i, self.body_panels)
                if self.gain:
                    dve.wait_ge(self.high.sem, self.high0 + m + 1 + self.body * i)
                    dve.scalar_tensor_tensor(c.xl[:, at, :], c.x[:, at, :],
                                             c.col(self.gain[0], self.gain[1] + m + self.body * i),
                                             c.xh[:, at, :].bitcast(F32), ALU.mult, ALU.subtract).then_inc(
                        self.ready.sem, 1)
        repeat(dve, self.turns, turn, straight=self.last)


class Store(Stage):

    def __init__(self, c, source):
        self.c, self.source = c, source
        self.out_done = c.flag("out_done")

    def gpsimd(self, pool):
        c = self.c
        for m in range(KD):
            pool.wait_ge(c.banks_freed.sem, self.source.product0 + m + 1)
            pool.dma_start(c.dram["out"][m], c.x[:, m, :]).then_inc(self.out_done.sem, 16)
        pool.wait_ge(self.out_done.sem, 16 * KD)


class Chain:

    def __init__(self, eng, signal):
        self.eng, self.flag = eng, signal

    def link(self, ins):
        ins.then_inc(self.flag.sem, 1)
        self.flag.total += 1
        self.eng.wait_ge(self.flag.sem, self.flag.total)


class Convolution(Stage):
    POOL_TILES, DVE_TILES, PE_TILES = (0, 1), (2, 3, 4, 5), (6, 7)
    SCALED = 5

    def __init__(self, c, source):
        self.c, self.source = c, source
        self.padded = c.arena("conv_in", 0, [P, KD, PAD + S])
        self.out = c.arena("conv_out", 17, [P, KD, S])
        self.parts = (c.arena("conv_high", 34, [P, KD, S], FR), c.arena("conv_low", 50, [P, KD, S], FR))
        self.diag = c.arena("tap_diagonals", 34, [P, len(self.PE_TILES) * TAPS, P])
        self.sq = c.arena("conv_square", 66, [P, 4, S])
        self.root = c.arena("conv_root", 74, [P, S])
        self.rs = c.arena("conv_rstd", 76, [P, S])
        self.scaled = c.arena("scaled_taps", 78, [P, self.SCALED, S])
        self.scale_done = c.flag("tap_scaled")
        self.pads = c.flag("pads")
        self.tapped = c.flag("tapped")
        self.pool_tapped = c.flag("pool_tapped")
        self.diags = c.flag("diagonals")
        self.pe_tapped = c.flag("pe_tapped")
        self.moved = c.flag("taps_moved")
        self.ln_stat, self.centred = c.flag("ln_stat"), c.flag("centred")
        self.sq_done, self.sq_used, self.ln_root = c.flag("sq_done"), c.flag("sq_used"), c.flag("ln_root")
        self.ln_scaled, self.silu_done = c.flag("ln_scaled"), c.flag("silu_done")
        self.high, self.ready = c.flag("conv_high_s"), c.flag("conv_ready")
        self.ready0 = 0
        self.next_tap = self.next_diag = self.next_scaled = 0

    def some(self, dve, count, turn):
        c = self.c
        for _ in range(count):
            pair, n = divmod(self.next_tap, 2 * TAPS)
            if pair >= len(self.DVE_TILES) // 2 or self.DVE_TILES[2 * pair + 1] >= 2 * turn:
                return
            k, m = n // 2, self.DVE_TILES[2 * pair + n % 2]
            out, taps, w = self.out[:, m, :], self.padded[:, m, k:k + S], c.col("dw_w", m * TAPS + k)
            if n == 0:
                dve.wait_ge(self.pads.sem, 1)
                dve.wait_ge(self.source.made.sem, self.source.made0 + self.DVE_TILES[2 * pair + 1] + 1)
            if k == 0:
                dve.tensor_scalar(out, taps, w, c.col("dw_b", m), ALU.mult, ALU.add).then_inc(self.tapped.sem, 1)
            else:
                dve.wait_ge(self.tapped.sem, self.next_tap - 1)
                dve.scalar_tensor_tensor(out, taps, w, out, ALU.mult, ALU.add).then_inc(self.tapped.sem, 1)
            self.next_tap += 1

    def scale_taps(self, act, count):
        c = self.c
        for _ in range(count):
            n = self.next_scaled
            if n >= 2 * TAPS:
                return
            k, m = n // 2, self.POOL_TILES[n % 2]
            if n == 0:
                act.wait_ge(self.pads.sem, 1)
                act.wait_ge(self.source.made.sem, self.source.made0 + self.POOL_TILES[1] + 1)
            after(act, self.pool_tapped, n - self.SCALED + 1)
            act.activation(self.scaled[:, n % self.SCALED, :], self.padded[:, m, k:k + S], ACT.Copy,
                           scale=c.col("dw_w", m * TAPS + k)).then_inc(self.scale_done.sem, 1)
            self.next_scaled += 1

    def diagonals(self, act, count):
        for _ in range(count):
            if self.next_diag < len(self.PE_TILES) * TAPS:
                d = self.next_diag
                act.activation(self.diag[:, d, :], self.c.sq["ident"][:], ACT.Copy,
                               scale=self.c.col("dw_w", self.PE_TILES[0] * TAPS + d)).then_inc(self.diags.sem, 1)
                self.next_diag += 1

    def gpsimd(self, pool):
        c = self.c
        for n in range(2 * TAPS):
            m = self.POOL_TILES[n % 2]
            out, tap = self.out[:, m, :], self.scaled[:, n % self.SCALED, :]
            pool.wait_ge(self.scale_done.sem, n + 1)
            if n < 2:
                pool.tensor_scalar(out, tap, c.col("dw_b", m), None, ALU.add).then_inc(self.pool_tapped.sem, 1)
            else:
                pool.wait_ge(self.pool_tapped.sem, n - 1)
                pool.tensor_tensor(out, out, tap, ALU.add).then_inc(self.pool_tapped.sem, 1)

    def vector(self, dve):
        c = self.c
        self.some(dve, 4 * TAPS, 4)
        for k, m in enumerate(self.PE_TILES):
            dve.wait_ge(self.pe_tapped.sem, k + 1)
            dve.tensor_scalar(self.out[:, m, :], c.psum[:, 4 + k, :], c.col("dw_b", m), None, ALU.add).then_inc(
                self.moved.sem, 1)
        dve.wait_ge(self.ln_stat.sem, 1)
        for m in range(KD):
            dve.tensor_tensor(self.out[:, m, :], self.out[:, m, :], c.psum[:, 6, :], ALU.subtract).then_inc(
                self.centred.sem, 1)
        dve.wait_ge(self.ln_root.sem, 1)
        dve.reciprocal(self.rs[:], self.root[:]).then_inc(self.centred.sem, 1)
        dve.wait_ge(self.centred.sem, KD + 1)
        dve.wait_ge(self.sq_done.sem, KD)
        for m in range(KD):
            dve.scalar_tensor_tensor(self.out[:, m, :], self.out[:, m, :], c.col("ln_g", m), self.rs[:],
                                     ALU.mult, ALU.mult).then_inc(self.ln_scaled.sem, 1)
            if m >= 2:
                self.low(dve, m - 2)
        self.low(dve, KD - 2)
        self.low(dve, KD - 1)

    def low(self, dve, m):
        dve.wait_ge(self.high.sem, m + 1)
        dve.tensor_tensor(self.parts[1][:, m, :], self.out[:, m, :], self.parts[0][:, m, :].bitcast(F32),
                          ALU.subtract).then_inc(self.ready.sem, 1)

    def scalar(self, act):
        c = self.c
        self.scale_taps(act, 2 * TAPS)
        act.preload_act_table(ACT.Sqrt)
        for m in range(KD):
            act.wait_ge(self.centred.sem, m + 1)
            after(act, self.sq_used, m - 3)
            act.activation(self.sq[:, m % 4, :], self.out[:, m, :], ACT.Square).then_inc(self.sq_done.sem, 1)
        act.wait_ge(self.ln_stat.sem, 2)
        act.activation(self.root[:], c.psum[:, 7, :], ACT.Sqrt, bias=c.eps[:]).then_inc(self.ln_root.sem, 1)
        act.preload_act_table(ACT.Silu)
        for m in range(KD + 1):
            if m < KD:
                act.wait_ge(self.ln_scaled.sem, m + 1)
                act.activation(self.out[:, m, :], self.out[:, m, :], ACT.Silu, bias=c.col("ln_b", m)).then_inc(
                    self.silu_done.sem, 1)
            if m >= 1:
                act.wait_ge(self.silu_done.sem, m)
                act.activation(self.parts[0][:, m - 1, :], self.out[:, m - 1, :], ACT.Copy).then_inc(self.high.sem, 1)

    def tensor(self, pe):
        c = self.c
        pe.wait_ge(self.source.norm.done.sem, self.source.norm.done0 + 2)
        pe.wait_ge(self.source.made.sem, self.source.made0 + KD)
        for k, m in enumerate(self.PE_TILES):
            pe.wait_ge(self.diags.sem, (k + 1) * TAPS)
            for t in range(TAPS):
                mm = pe.matmul(c.psum[:, 4 + k, :], self.diag[:, k * TAPS + t, :], self.padded[:, m, t:t + S],
                               start=(t == 0), stop=(t == TAPS - 1))
            mm.then_inc(self.pe_tapped.sem, 1)
        for m in range(KD):
            if m in self.DVE_TILES:
                pe.wait_ge(self.tapped.sem, 2 * TAPS * (self.DVE_TILES.index(m) // 2 + 1))
            elif m in self.POOL_TILES:
                pe.wait_ge(self.pool_tapped.sem, 2 * TAPS)
            else:
                pe.wait_ge(self.moved.sem, m - self.PE_TILES[0] + 1)
            mm = pe.matmul(c.psum[:, 6, :], c.sq["mean"][:], self.out[:, m, :], start=(m == 0), stop=(m == KD - 1))
        mm.then_inc(self.ln_stat.sem, 1)
        for m in range(KD):
            pe.wait_ge(self.sq_done.sem, m + 1)
            pe.matmul(c.psum[:, 7, :], c.sq["mean"][:], self.sq[:, m % 4, :], start=(m == 0),
                      stop=(m == KD - 1)).then_inc((self.ln_stat if m == KD - 1 else self.sq_used).sem, 1)


class PadZeros(Stage):
    def __init__(self, c, buffer, width, signal):
        self.buffer, self.width, self.done = buffer, width, c.flag(signal)

    def gpsimd(self, pool):
        pool.memset(self.buffer[:, :, 0:self.width], 0.0).then_inc(self.done.sem, 1)


class Project(Stage):

    def __init__(self, c, weights, count, parts, source, norm, dest, scale=None, func=None, pad=0, first=0):
        self.c, self.weights, self.count, self.parts, self.source = c, weights, count, parts, source
        self.norm, self.dest, self.scale, self.func, self.pad, self.first = norm, dest, scale, func, pad, first
        self.panel0, self.product0 = c.take_panels(count), c.take_products(count)
        self.acted = c.flag("acted")
        self.acted0 = self.acted.reserve(count) if func else 0

    def sync(self, sp):
        c, w = self.c, self.c.dram[self.weights]

        def four(i):
            for j in range(4):
                n0 = self.panel0 + j
                c.load_panel(sp, n0, None, n0 + 4 * i, w[bass.ds(self.first + 4 * i + j, 1)].rearrange("a p n -> (a p) n"), PANEL)
        repeat(sp, self.count // 4, four)

    def tensor(self, pe):
        c = self.c
        ah, al = self.parts

        def four(i):
            for j in range(4):
                n0, t0 = self.panel0 + j, self.product0 + j
                slot = n0 % SLOTS
                after(pe, c.banks_freed, t0 + 4 * i - (RING_BANKS - 1))
                pe.wait_ge(c.weights_split.sem, n0 + 4 * i + 1)
                for k in range(KD):
                    if j == 0:
                        pe.wait_ge(self.source.ready.sem, self.source.ready0 + k + 1)
                    w = slice(k * P, (k + 1) * P)
                    mm = three(c.nc, c.psum[:, t0 % RING_BANKS, :], c.wh[:, slot, w], c.wl[:, slot, w],
                               ah[:, k, :], al[:, k, :], k == 0, k == KD - 1)
                mm.then_inc(c.panels_used.sem, 1)
                if isinstance(i, int):
                    self.norm.late(pe, j)
        repeat(pe, self.count // 4, four, peel=1)

    def scalar(self, act):
        c = self.c
        if self.func:
            act.preload_act_table(self.func)

        def four(i):
            for j in range(4):
                c.ahead(c.split_high, act, self.panel0, j, i, 4)
                if self.func:
                    act.wait_ge(c.banks_freed.sem, self.product0 + j + 1 + 4 * i)
                    d = self.dest[:, bass.ds(4 * i + j, 1), self.pad:self.pad + S]
                    act.activation(d, d, self.func).then_inc(self.acted.sem, 1)
        repeat(act, self.count // 4, four)

    def vector(self, dve):
        c = self.c
        dve.wait_ge(self.norm.done.sem, self.norm.done0 + 2)

        def four(i):
            for j in range(4):
                dve.wait_ge(c.panels_used.sem, self.panel0 + j + 1 + 4 * i)
                bank = (self.product0 + j) % RING_BANKS
                d = self.dest[:, bass.ds(4 * i + j, 1), self.pad:self.pad + S]
                r = c.rstd[:].rearrange("p (a n) -> p a n", a=1)
                if self.scale:
                    dve.scalar_tensor_tensor(d, c.psum[:, bank:bank + 1, :], self.scale, r, ALU.mult,
                                             ALU.mult).then_inc(c.banks_freed.sem, 1)
                else:
                    dve.tensor_tensor(d, c.psum[:, bank:bank + 1, :], r, ALU.mult).then_inc(c.banks_freed.sem, 1)
                c.ahead(c.split_low, dve, self.panel0, j, i, 4)
        repeat(dve, self.count // 4, four)


class ProjectTokens(Stage):

    def __init__(self, c, weights, parts, source, dest, tiles_=NT, norm=None, func=None):
        self.c, self.weights, self.parts, self.source = c, weights, parts, source
        self.dest, self.tiles, self.norm, self.func = dest, tiles_, norm, func
        self.panel0, self.product0 = c.take_panels(4), c.take_products(4)
        self.acted = c.flag("acted")
        self.acted0 = self.acted.reserve(tiles_) if func else 0

    def sync(self, sp):
        c, w = self.c, self.c.dram[self.weights]
        for j in range(4):
            n = self.panel0 + j
            c.load_panel(sp, n, None, n, w[j], PANEL)

    def tensor(self, pe):
        c = self.c
        ah, al = self.parts
        after(pe, c.banks_freed, self.product0)
        for j in range(4):
            n = self.panel0 + j
            slot = n % SLOTS
            pe.wait_ge(c.weights_split.sem, n + 1)
            for b in range(2):
                k = 2 * j + b
                pe.wait_ge(self.source.ready.sem, self.source.ready0 + k + 1)
                for i in range(self.tiles):
                    t = slice(i * P, (i + 1) * P)
                    w = slice(b * 512, (b + 1) * 512)
                    mm = three(c.nc, c.psum[:, (self.product0 + i) % RING_BANKS, :], ah[:, k, t], al[:, k, t],
                               c.wh[:, slot, w], c.wl[:, slot, w], k == 0, k == KD - 1)
            mm.then_inc(c.panels_used.sem, 1)

    def scalar(self, act):
        c = self.c
        for j in range(4):
            c.ahead(c.split_high, act, self.panel0, j, 0, 4)
        for i in range(self.tiles):
            if self.func:
                act.wait_ge(c.banks_freed.sem, self.product0 + i + 1)
                act.activation(self.dest[:, i, :], self.dest[:, i, :], self.func).then_inc(self.acted.sem, 1)

    def vector(self, dve):
        c = self.c
        for j in range(4):
            c.ahead(c.split_low, dve, self.panel0, j, 0, 4)
        dve.wait_ge(c.panels_used.sem, self.panel0 + 4)
        if self.norm:
            dve.wait_ge(self.norm.done.sem, self.norm.done0 + 2)
        for i in range(self.tiles):
            bank = (self.product0 + i) % RING_BANKS
            if self.norm:
                dve.tensor_scalar(self.dest[:, i, :], c.psum[:, bank, :], c.rstd_tok[:, i:i + 1], None,
                                  ALU.mult).then_inc(c.banks_freed.sem, 1)
            else:
                dve.tensor_copy(self.dest[:, i, :], c.psum[:, bank, :]).then_inc(c.banks_freed.sem, 1)
        if self.tiles < RING_BANKS:
            dve.wait_ge(c.banks_freed.sem, self.product0 + self.tiles)
            dve.sem_inc(c.banks_freed.sem, RING_BANKS - self.tiles)


class HeadSquares(Stage):

    def __init__(self, sums):
        self.sums = sums

    def scalar(self, act):
        self.sums.square_all(act)


class HeadSums(Stage):

    def __init__(self, c, name, tiles, heads, width, wait, buffers):
        self.buffers = buffers
        self.c, self.tiles, self.heads, self.width, self.held_until = c, tiles, heads, width, wait
        n, self.nt = len(tiles), width // P
        self.mean = c.sq["mean64"][:, 0:P:HALF] if heads == 2 else c.sq["mean128"][:, 0:1]
        self.r = c.place(name, [P, n * self.nt * heads])
        self.squares, self.stat = c.flag("hn_square"), c.flag("hn_stat")
        self.root, self.done = c.flag("hn_root"), c.flag("hn_inverse")
        self.s0, self.t0 = self.squares.reserve(n), self.stat.reserve(n)
        self.r0, self.d0 = self.root.reserve(1), self.done.reserve(1)

    def at(self, t, i):
        a = (t * self.nt + i) * self.heads
        return slice(a, a + self.heads)

    def tensor(self, pe):
        c = self.c
        after(pe, self.root, self.r0)
        for t in range(len(self.tiles)):
            pe.wait_ge(self.squares.sem, self.s0 + t + 1)
            for i in range(self.nt):
                mm = pe.matmul(c.psum[:, 7, self.at(t, i)], self.buffers[t][:, i * P:(i + 1) * P], self.mean,
                               start=True, stop=True, skip_group_check=True)
            mm.then_inc(self.stat.sem, 1)

    def square_all(self, act):
        self.held_until(act)
        for t, z in enumerate(self.tiles):
            act.activation(self.buffers[t][:, 0:self.width], z, ACT.Square).then_inc(self.squares.sem, 1)

    def scalar(self, act):
        c = self.c
        act.wait_ge(self.stat.sem, self.t0 + len(self.tiles))
        act.activation(self.r[:], c.psum[:, 7, 0:len(self.tiles) * self.nt * self.heads], ACT.Sqrt,
                       bias=c.eps[:]).then_inc(self.root.sem, 1)

    def vector(self, dve):
        dve.wait_ge(self.root.sem, self.r0 + 1)
        dve.reciprocal(self.r[:], self.r[:]).then_inc(self.done.sem, 1)


class HeadScale(Stage):

    def __init__(self, c, sums, gains):
        self.c, self.sums, self.gains = c, sums, gains
        self.spread, self.done = c.flag("hn_spread"), c.flag("hn_done")
        self.wide = c.flag("hn_wide")
        n = len(sums.tiles)
        self.s0, self.d0 = self.spread.reserve(n), self.done.reserve(n)
        self.w0 = self.wide.reserve(n) if sums.heads == 2 else 0

    def scalar(self, act):
        c, s = self.c, self.sums
        if s.heads == 1:
            return
        act.wait_ge(s.done.sem, s.d0 + 1)
        for t in range(len(s.tiles)):
            after(act, self.spread, self.s0 + t - 1 if t >= 2 else 0)
            r = s.r[:, s.at(t, 0).start:s.at(t, s.nt - 1).stop].rearrange("p (h a) -> p h a", a=1)
            act.activation(c.up[:, t % 2, :].rearrange("p (h a) -> p h a", a=HALF),
                           r.to_broadcast([P, 2 * s.nt, HALF]), ACT.Copy).then_inc(self.wide.sem, 1)

    def tensor(self, pe):
        c, s = self.c, self.sums
        pe.wait_ge(s.done.sem, s.d0 + 1)
        for t in range(len(s.tiles)):
            after(pe, self.done, self.d0 + t - 1)
            if s.heads == 2:
                pe.wait_ge(self.wide.sem, self.w0 + t + 1)
            for i in range(s.nt):
                r = c.up[:, t % 2, i * P:(i + 1) * P] if s.heads == 2 else s.r[:, s.at(t, i)].to_broadcast([P, P])
                mm = pe.matmul(c.psum[:, 5 + t % 2, i * P:(i + 1) * P], r, c.sq["ident"][:], start=True, stop=True,
                               skip_group_check=True)
            mm.then_inc(self.spread.sem, 1)

    def vector(self, dve):
        s = self.sums
        for t, z in enumerate(s.tiles):
            dve.wait_ge(self.spread.sem, self.s0 + t + 1)
            dve.scalar_tensor_tensor(z, z, self.gains[t], self.c.psum[:, 5 + t % 2, 0:s.width], ALU.mult,
                                     ALU.mult).then_inc(self.done.sem, 1)


class Split(Stage):

    def __init__(self, c, source, count, parts, first, waits):
        self.c, self.from_, self.count, self.parts, self.first, self.waits = c, source, count, parts, first, waits
        self.turned, self.high = c.flag("o_turned"), c.flag("o_high")
        self.ready = c.flag("o_ready")
        self.t0, self.h0, self.r0 = self.turned.reserve(count), self.high.reserve(count), self.ready.reserve(count)

    def tensor(self, pe):
        c = self.c
        self.waits(pe)
        for m in range(self.count):
            after(pe, self.ready, self.r0 + m - 1 if m >= 2 else 0)
            for i in range(NT):
                mm = pe.transpose(c.psum[:, 6 + m % 2, i * P:(i + 1) * P], self.from_[:, i, m * P:(m + 1) * P],
                                  c.sq["ident"][:])
            mm.then_inc(self.turned.sem, 1)

    def scalar(self, act):
        c = self.c
        for m in range(self.count):
            act.wait_ge(self.turned.sem, self.t0 + m + 1)
            act.activation(self.parts[0][:, self.first + m, :], c.psum[:, 6 + m % 2, :], ACT.Copy).then_inc(
                self.high.sem, 1)

    def vector(self, dve):
        c = self.c
        for m in range(self.count):
            dve.wait_ge(self.high.sem, self.h0 + m + 1)
            dve.tensor_tensor(self.parts[1][:, self.first + m, :], c.psum[:, 6 + m % 2, :],
                              self.parts[0][:, self.first + m, :].bitcast(F32), ALU.subtract).then_inc(
                self.ready.sem, 1)


class KeysValues(Stage):
    PARTS = 6

    def __init__(self, c, source, norm):
        self.c, self.source, self.norm = c, source, norm
        self.panel0, self.product0 = c.take_panels(self.PARTS), c.take_products(self.PARTS)
        c.take_products(2)
        self.parts = (c.arena("xb_high", 0, [P, KD, S], FR), c.arena("xb_low", 16, [P, KD, S], FR))
        self.cmp = c.arena("kv_cmp", 56, [P, 2, S])
        self.keys = c.arena("keys", 60, [P, 4, S])
        self.values = c.arena("values", 68, [P, 2, NT, P])
        self.vt = c.pre
        self.high, self.ready = c.flag("xb_high_s"), c.flag("xb_ready")
        self.ready0 = 0
        self.key_copies = c.flag("key_copies")
        self.written = c.flag("kv_written")
        self.turned = c.flag("v_turned")
        self.copied = c.flag("v_copied")

    def sync(self, sp):
        c = self.c
        for j in range(self.PARTS):
            n = self.panel0 + j
            c.load_panel(sp, n, None, n, c.dram["w_kv"][j], PANEL)

    def tensor(self, pe):
        c = self.c
        for j in range(self.PARTS):
            n, t = self.panel0 + j, self.product0 + j
            slot = n % SLOTS
            after(pe, c.banks_freed, t - (RING_BANKS - 1))
            pe.wait_ge(c.weights_split.sem, n + 1)
            for k in range(KD):
                pe.wait_ge(self.source.ready.sem, self.source.ready0 + k + 1)
                w = slice(k * P, (k + 1) * P)
                mm = three(c.nc, c.psum[:, t % RING_BANKS, :], c.wh[:, slot, w], c.wl[:, slot, w],
                           c.xh[:, k, :], c.xl[:, k, :], k == 0, k == KD - 1)
            mm.then_inc(c.panels_used.sem, 1)
            self.norm.late(pe, j)
        for b in range(2):
            after(pe, c.banks_freed, self.product0 + 4 + 2 * b)
            for i in range(NT):
                mm = pe.transpose(c.psum[:, 6 + b, i * P:(i + 1) * P], self.vt[:, b, i * P:(i + 1) * P],
                                  c.sq["ident"][:])
            mm.then_inc(self.turned.sem, 1)

    def scalar(self, act):
        c = self.c
        for j in range(KD):
            if j < self.PARTS:
                c.ahead(c.split_high, act, self.panel0, j, 0, self.PARTS)
            act.activation(self.parts[0][:, j, :], c.x[:, j, :], ACT.Copy, scale=c.col("b_norm", j)).then_inc(
                self.high.sem, 1)
        for b in range(2):
            act.wait_ge(self.turned.sem, b + 1)
            act.activation(self.values[:, b], c.psum[:, 6 + b, :].rearrange("p (t n) -> p t n", t=NT),
                           ACT.Copy).then_inc(self.copied.sem, 1)

    def low(self, dve, m):
        c = self.c
        dve.wait_ge(self.high.sem, m + 1)
        dve.scalar_tensor_tensor(self.parts[1][:, m, :], c.x[:, m, :], c.col("b_norm", m),
                                 self.parts[0][:, m, :].bitcast(F32), ALU.mult, ALU.subtract).then_inc(
            self.ready.sem, 1)

    def vector(self, dve):
        c = self.c
        dve.wait_ge(self.norm.done.sem, self.norm.done0 + 2)
        for j in range(self.PARTS):
            dve.wait_ge(c.panels_used.sem, self.panel0 + j + 1)
            bank = c.psum[:, (self.product0 + j) % RING_BANKS, :]
            if j < 2:
                dve.tensor_tensor(self.cmp[:, j, :], bank, c.rstd[:], ALU.mult).then_inc(c.banks_freed.sem, 1)
            elif j % 2 == 0:
                b = j // 2 - 1
                dve.tensor_tensor(self.keys[0:64, 2 * b, :], bank[0:64], c.rstd[0:64, :], ALU.mult).then_inc(
                    self.written.sem, 1)
                dve.tensor_tensor(self.keys[64:128, 2 * b + 1, :], bank[64:128], c.rstd[64:128, :],
                                  ALU.mult).then_inc(c.banks_freed.sem, 1)
            else:
                b = j // 2 - 1
                dve.tensor_tensor(self.vt[:, b, :], bank, c.rstd[:], ALU.mult).then_inc(c.banks_freed.sem, 1)
            c.ahead(c.split_low, dve, self.panel0, j, 0, self.PARTS)
            self.low(dve, j)
        dve.wait_ge(c.banks_freed.sem, self.product0 + self.PARTS)
        dve.sem_inc(c.banks_freed.sem, 2)
        self.low(dve, 6)
        self.low(dve, 7)

    def gpsimd(self, pool):
        c = self.c
        for b in range(2):
            pool.wait_ge(self.written.sem, b + 1)
            pool.wait_ge(c.banks_freed.sem, self.product0 + 3 + 2 * b)
            pool.dma_start(self.keys[64:128, 2 * b, :], self.keys[0:64, 2 * b, :]).then_inc(self.key_copies.sem, 16)
            pool.dma_start(self.keys[0:64, 2 * b + 1, :], self.keys[64:128, 2 * b + 1, :]).then_inc(
                self.key_copies.sem, 16)


class CompressBlocks(Stage):

    def __init__(self, comp):
        self.comp = comp

    def gpsimd(self, pool):
        self.comp.load(pool)

    def vector(self, dve):
        self.comp.blocks(dve)


class Compress(Stage):

    def __init__(self, c, kv):
        self.c, self.kv = c, kv
        self.w1 = c.arena("phi_w1", 32, [P, 2, LCMP * HALF])
        self.blk = c.arena("cmp_blocks", 48, [P, 2, LCMP, 32])
        self.pos = c.place("cmp_pos", [P, 2, LCMP])
        self.w2 = c.place("phi_w2", [P, 2, HALF])
        self.vc = c.arena("cmp_values", 56, [P, 2, 4 * HALF])
        self.kc = c.arena("cmp_keys", 58, [P, 2, 32])
        self.hid = c.arena("cmp_hidden", 58.25, [P, 2, 32])
        self.loaded, self.cleared = c.flag("phi_loaded"), c.flag("cmp_cleared")
        self.blocked, self.hidden, self.silued = c.flag("blocked"), c.flag("phi_hidden"), c.flag("phi_silu")
        self.mapped, self.kept = c.flag("phi_mapped"), c.flag("cmp_kept")

    def load(self, pool):
        c = self.c
        pool.wait_ge(c.banks_freed.sem, self.kv.source.product0 + KD)
        for t, n in ((self.w1, "phi_w1"), (self.pos, "cmp_pos"), (self.w2, "phi_w2")):
            pool.dma_start(t[:], c.dram[n]).then_inc(self.loaded.sem, 16)
        pool.wait_ge(self.blocked.sem, 4)
        pool.memset(self.kc[:], 0.0).then_inc(self.cleared.sem, 1)
        pool.memset(self.vc[:], 0.0).then_inc(self.cleared.sem, 1)

    def blocks(self, dve):
        c = self.c
        dve.wait_ge(self.loaded.sem, 48)
        dve.wait_ge(c.banks_freed.sem, self.kv.product0 + 2)
        for j in range(2):
            v = self.kv.cmp[:, j, :].rearrange("p (n l) -> p l n", l=STRIDE)
            for h in range(2):
                dve.tensor_tensor(self.blk[:, j, h * STRIDE:(h + 1) * STRIDE, 0:NCMP], v[:, :, h:h + NCMP],
                                  self.pos[:, j, h * STRIDE:(h + 1) * STRIDE].rearrange(
                                      "p (l a) -> p l a", a=1).to_broadcast([P, STRIDE, NCMP]),
                                  ALU.add).then_inc(self.blocked.sem, 1)

    def vector(self, dve):
        c = self.c
        dve.wait_ge(self.cleared.sem, 2)
        dve.wait_ge(self.mapped.sem, 1)
        for g in range(2):
            dve.tensor_copy(self.kc[:, g, 0:NCMP], c.psum[:, 6 - g, 0:NCMP]).then_inc(self.kept.sem, 1)
        dve.wait_ge(self.mapped.sem, 2)
        for g in range(2):
            for h in range(4):
                q = slice(32 * h, 32 * h + NCMP)
                dve.tensor_copy(self.vc[q, g, h * HALF:(h + 1) * HALF],
                                c.psum[q, 7 - 3 * g, h * HALF:(h + 1) * HALF]).then_inc(self.kept.sem, 1)

    def scalar(self, act):
        act.wait_ge(self.hidden.sem, 1)
        act.activation(self.hid[:, :, 0:NCMP], self.c.psum[:, 4, 0:64].rearrange("p (a n) -> p a n", a=2)[:, :, 0:NCMP],
                       ACT.Silu).then_inc(self.silued.sem, 1)

    def tensor(self, pe):
        c = self.c
        halves = [slice(0, 64), slice(64, 128)]
        for j in range(2):
            pe.wait_ge(self.blocked.sem, 2 * j + 2)
            for l in range(LCMP):
                for q in halves:
                    mm = pe.matmul(c.psum[q, 4, j * 32:j * 32 + NCMP], self.w1[q, j, l * HALF:(l + 1) * HALF],
                                   self.blk[q, j, l, 0:NCMP], start=(l == 0), stop=(l == LCMP - 1),
                                   skip_group_check=True)
        mm.then_inc(self.hidden.sem, 1)
        pe.wait_ge(self.silued.sem, 1)
        pe.wait_ge(self.gates.kept.sem, 1)
        after(pe, self.kv.copied, 2)
        for g, q in enumerate(halves):
            for o in halves:
                mm = pe.matmul(c.psum[o, 6 - g, 0:NCMP], self.w2[q, 0, :], self.hid[q, 0, 0:NCMP],
                               start=True, stop=True, skip_group_check=True)
        mm.then_inc(self.mapped.sem, 1)
        for g, q in enumerate(halves):
            for h in range(4):
                mm = pe.matmul(c.psum[32 * h:32 * h + NCMP, 7 - 3 * g, h * HALF:(h + 1) * HALF],
                               self.hid[q, 1, 0:NCMP], self.w2[q, 1, :], start=True, stop=True,
                               skip_group_check=True)
        mm.then_inc(self.mapped.sem, 1)


class Gates(Stage):
    N = 3 * HEADS

    def __init__(self, c, source, norm):
        self.c, self.source, self.norm = c, source, norm
        self.panel0, self.product0 = c.take_panels(1), c.take_products(1)
        c.take_products(3)
        self.gates = c.arena("gates", 59, [P, NT, self.N])
        self.done, self.turned, self.kept = c.flag("gates_done"), c.flag("gates_turned"), c.flag("gates_kept")

    def sync(self, sp):
        c = self.c
        c.load_panel(sp, self.panel0, None, self.panel0, c.dram["w_gates"], KD * self.N)

    def tensor(self, pe):
        c = self.c
        ah, al = self.source.parts
        n, slot = self.panel0, self.panel0 % SLOTS
        after(pe, c.banks_freed, self.product0 - (RING_BANKS - 1))
        pe.wait_ge(c.weights_split.sem, n + 1)
        for k in range(KD):
            w = slice(k * self.N, (k + 1) * self.N)
            mm = three(c.nc, c.psum[0:self.N, self.product0 % RING_BANKS, :], c.wh[:, slot, w], c.wl[:, slot, w],
                       ah[:, k, :], al[:, k, :], k == 0, k == KD - 1)
        mm.then_inc(c.panels_used.sem, 1)
        pe.wait_ge(self.done.sem, 1)
        for i in range(NT):
            mm = pe.transpose(c.psum[:, 5, i * 64:i * 64 + self.N], c.pre[0:self.N, 0, i * P:(i + 1) * P],
                              c.sq["ident"][0:self.N, 0:self.N])
        mm.then_inc(self.turned.sem, 1)

    def scalar(self, act):
        c = self.c
        c.ahead(c.split_high, act, self.panel0, 0, 0, 1)
        act.wait_ge(c.banks_freed.sem, self.product0 + 1)
        act.activation(c.pre[0:self.N, 0, :], c.pre[0:self.N, 0, :], ACT.Sigmoid).then_inc(self.done.sem, 1)

    def vector(self, dve):
        c = self.c
        n = slice(0, self.N)
        dve.wait_ge(c.panels_used.sem, self.panel0 + 1)
        dve.tensor_tensor(c.pre[n, 0, :], c.psum[n, self.product0 % RING_BANKS, :], c.rstd[n, :],
                          ALU.mult).then_inc(c.banks_freed.sem, 1)
        dve.wait_ge(c.banks_freed.sem, self.product0 + 1)
        dve.sem_inc(c.banks_freed.sem, 3)
        c.ahead(c.split_low, dve, self.panel0, 0, 0, 1)
        dve.wait_ge(self.turned.sem, 1)
        dve.tensor_copy(self.gates[:], c.psum[:, 5, 0:256].rearrange("p (i n) -> p i n", i=NT)[:, :, 0:self.N]
                        ).then_inc(self.kept.sem, 1)


class CompressedAttention(Stage):

    def __init__(self, c, q, kv, comp, gates, project):
        self.c, self.q, self.kv, self.comp, self.gates, self.project = c, q, kv, comp, gates, project
        self.bias = c.arena("cmp_bias", 48, [P, NT, HEADS, 32])
        self.o = c.arena("o", 32, [P, NT, D])
        self.t = c.arena("cmp_scores", 0, [P, 2, 256])
        self.prob = c.arena("cmp_probs", 8, [P, 4, 256])
        self.pt = c.arena("cmp_probs_turned", 4, [P, 2, 256])
        self.m = c.arena("cmp_small", 6, [P, 8, 32])
        names = ("cs_loaded", "cs_scores", "cs_scored", "cs_exp", "cs_prob", "cs_turned", "cs_copied", "cs_out",
                 "cs_kept")
        (self.loaded, self.scores, self.scored, self.exped, self.probs, self.turned, self.copied, self.out,
         self.kept) = [c.flag(n) for n in names]
        self.chain = c.flag("vector_chain")

    def gpsimd(self, pool):
        c = self.c
        pool.wait_ge(self.comp.hidden.sem, 1)
        pool.dma_start(self.bias[:], c.dram["cmp_bias"]).then_inc(self.loaded.sem, 16)

    def tensor(self, pe):
        c = self.c
        pe.wait_ge(self.comp.kept.sem, 10)
        pe.wait_ge(self.gates.turned.sem, 1)
        pe.wait_ge(self.gates.kept.sem, 1)
        pe.wait_ge(c.banks_freed.sem, self.project.product0 + KD)
        for s in range(8 + 3):
            if s < 8:
                g, i = divmod(s, NT)
                after(pe, self.scored, s - 1)
                for h in range(8):
                    half = slice(64 * (h % 2), 64 * (h % 2) + 64)
                    mm = pe.matmul(c.psum[:, 4 + h % 2 + 2 * (s % 2), h * 32:(h + 1) * 32],
                                   self.q[half, 4 * g + h // 2, i * P:(i + 1) * P], self.comp.kc[half, g, :],
                                   start=True, stop=True, skip_group_check=True)
                mm.then_inc(self.scores.sem, 1)
            u = s - 2
            if 0 <= u < 8:
                pe.wait_ge(self.probs.sem, u + 1)
                after(pe, self.copied, u - 1)
                for a in range(2):
                    mm = pe.transpose(c.psum[:, 2 * (u % 2), a * P:(a + 1) * P], self.prob[:, u % 4, a * P:(a + 1) * P],
                                      c.sq["ident"][:])
                mm.then_inc(self.turned.sem, 1)
            u = s - 3
            if u >= 0:
                pe.wait_ge(self.copied.sem, u + 1)
                after(pe, self.kept, u - 1)
                for a in range(2):
                    mm = pe.matmul(c.psum[:, 1 + 2 * (u % 2), a * 256:(a + 1) * 256],
                                   self.pt[:, u % 2, a * P:(a + 1) * P], self.comp.vc[:, u // NT, :], start=True,
                                   stop=True, skip_group_check=True)
                mm.then_inc(self.out.sem, 1)

    def scalar(self, act):
        act.preload_act_table(ACT.Exp)
        for s in range(8 + 2):
            if s < 8:
                act.wait_ge(self.scored.sem, s + 1)
                after(act, self.turned, s - 3)
                act.activation(self.prob[:, s % 4, :], self.t[:, s % 2, :], ACT.Exp).then_inc(self.exped.sem, 1)
            u = s - 2
            if u >= 0:
                act.wait_ge(self.turned.sem, u + 1)
                after(act, self.out, u - 1)
                act.activation(self.pt[:, u % 2, :], self.c.psum[:, 2 * (u % 2), 0:256], ACT.Copy).then_inc(
                    self.copied.sem, 1)

    def vector(self, dve):
        self.ch = Chain(dve, self.chain)
        dve.wait_ge(self.loaded.sem, 16)
        dve.wait_ge(self.gates.kept.sem, 1)
        for s in range(8 + 4):
            if s < 8:
                self.score(dve, s)
            if 0 <= s - 1 < 8:
                self.share(dve, s - 1)
            u = s - 4
            if u >= 0:
                dve.wait_ge(self.out.sem, u + 1)
                g, i = divmod(u, NT)
                dve.tensor_copy(self.o[:, i, g * 512:(g + 1) * 512], self.c.psum[:, 1 + 2 * (u % 2), :]).then_inc(
                    self.kept.sem, 1)

    def heads(self, buffer):
        return buffer.rearrange("p (h n) -> p h n", h=8)

    def row(self, k, u):
        return self.m[:, 4 * (u % 2) + k, 0:8]

    def wide(self, k, u):
        return self.row(k, u).rearrange("p (h a) -> p h a", a=1).to_broadcast([P, 8, 32])

    def score(self, dve, u):
        c, (g, i), t = self.c, divmod(u, NT), self.heads(self.t[:, u % 2, :])
        dve.wait_ge(self.scores.sem, u + 1)
        after(dve, self.exped, u - 1)
        for a in range(2):
            s = c.psum[:, 4 + a + 2 * (u % 2), 0:256].rearrange("p (h n) -> p h n", h=8)[:, a:8:2, :]
            self.ch.link(dve.tensor_tensor(t[:, a:8:2, :], s, self.bias[:, i, 8 * g + a:8 * g + 8:2, :], ALU.add))
        self.ch.link(dve.tensor_reduce(self.row(0, u), t, AXX, ALU.max))
        dve.tensor_tensor(t, t, self.wide(0, u), ALU.subtract).then_inc(self.scored.sem, 1)

    def share(self, dve, u):
        c, (g, i), p = self.c, divmod(u, NT), self.heads(self.prob[:, u % 4, :])
        dve.wait_ge(self.exped.sem, u + 1)
        self.ch.link(dve.tensor_reduce(self.row(1, u), p, AXX, ALU.add))
        self.ch.link(dve.reciprocal(self.row(2, u), self.row(1, u)))
        self.ch.link(dve.tensor_tensor(self.row(3, u), self.row(2, u), self.gates.gates[:, i, 8 * g:8 * g + 8],
                                       ALU.mult))
        if i == 0:
            self.ch.link(dve.tensor_scalar(self.row(3, u), self.row(3, u), c.col("seen"), None, ALU.mult))
        dve.tensor_tensor(p, p, self.wide(3, u), ALU.mult).then_inc(self.probs.sem, 1)


class StackQueries(Stage):

    def __init__(self, c, q, project):
        self.c, self.q, self.project = c, q, project
        self.twice = (c.place("queries_even", [P, KD, S], FR, offset=c.xh_at),
                      c.place("queries_odd", [P, KD, S], FR, offset=c.xl_at))
        self.low = c.arena("queries_low", 12, [P, KD, S])
        self.high_done, self.low_done, self.copied = c.flag("q_high"), c.flag("q_low"), c.flag("q_copied")

    def rows(self):
        for h in range(2):
            yield h, slice(64 * h, 64 * h + 64), slice(64 - 64 * h, 128 - 64 * h)

    def scalar(self, act):
        act.wait_ge(self.c.banks_freed.sem, self.project.product0 + KD)
        for h, own, _ in self.rows():
            act.activation(self.twice[h][own], self.q[own], ACT.Copy).then_inc(self.high_done.sem, 1)

    def vector(self, dve):
        for h, own, _ in self.rows():
            dve.wait_ge(self.high_done.sem, h + 1)
            dve.tensor_tensor(self.low[own], self.q[own], self.twice[h][own].bitcast(F32), ALU.subtract).then_inc(
                self.low_done.sem, 1)

    def gpsimd(self, pool):
        for h, own, other in self.rows():
            pool.wait_ge(self.high_done.sem, h + 1)
            pool.dma_start(self.twice[h][other], self.twice[h][own]).then_inc(self.copied.sem, 16)


class StackKeys(Stage):

    def __init__(self, c, kv, after_stage):
        self.c, self.kv, self.after = c, kv, after_stage
        self.even = c.arena("keys_even", 60, [P, 4, S], FR)
        self.odd = c.arena("keys_odd", 48, [P, 4, S], FR)
        self.high, self.done = c.flag("k_high"), c.flag("k_stacked")

    def scalar(self, act):
        act.wait_ge(self.kv.key_copies.sem, 64)
        act.wait_ge(self.after.kept.sem, 8)
        for k in range(4):
            act.activation(self.odd[:, k, :], self.kv.keys[:, k, :], ACT.Copy).then_inc(self.high.sem, 1)
        for k in range(4):
            act.wait_ge(self.done.sem, 2 * k + 1)
            act.activation(self.even[0:64, k, :], self.kv.keys[0:64, k, :], ACT.Copy).then_inc(self.high.sem, 1)

    def vector(self, dve):
        for k in range(4):
            keys = self.kv.keys[:, k, :]
            dve.wait_ge(self.high.sem, k + 1)
            dve.tensor_tensor(self.odd[0:64, k, :], keys[0:64], self.odd[0:64, k, :].bitcast(F32),
                              ALU.subtract).then_inc(self.done.sem, 1)
            dve.tensor_tensor(self.even[64:128, k, :], keys[64:128], self.odd[64:128, k, :].bitcast(F32),
                              ALU.subtract).then_inc(self.done.sem, 1)


class CausalAttention(Stage):
    RING, PROBS = 4, 8
    SCORE_BANKS, TURN_BANKS = (4, 5, 6, 3), (7, 0)
    LAG = 4

    def __init__(self, c, name, kind, q, tiles_, where, **more):
        self.c, self.kind, self.q, self.tiles, self.more = c, kind, q, tiles_, more
        self.branches = 2 if kind == "sparse" else 1
        self.units = [(h, b, i) for h in range(2) for b in range(self.branches) for i in range(NT)]
        self.U = len(self.units)
        a = where
        self.scores_sb = [c.arena(f"{name}_sc{k}", a[0] + 2 * k, [P, S]) for k in range(self.RING)]
        self.probs_sb = [c.arena(f"{name}_pr{k}", a[1] + 2 * k, [P, S]) for k in range(self.PROBS)]
        self.pt_sb = [c.arena(f"{name}_pt{k}", kib, [P, S]) for k, kib in enumerate(a[2])]
        self.qs = c.up
        self.ks = c.pre[:, 0, :]
        if kind == "sparse":
            self.q_high = c.place("staged_high", [P, 2, S], FR, offset=c.up_at)
            self.q_low = c.place("staged_low", [P, 2, S], FR, offset=c.square_at)
        self.bias = c.pre
        names = ("at_staged", "at_scores", "at_scored", "at_probs", "at_turned", "at_copied", "at_out", "at_added",
                 "at_coef", "at_fox")
        (self.staged, self.scores, self.scored, self.probs, self.turned, self.copied, self.out, self.added,
         self.coef, self.foxed) = [c.flag(n) for n in names]
        n = tiles_ * self.U
        self.b0 = {s: s.reserve(n) for s in (self.scores, self.scored, self.probs, self.turned, self.copied,
                                             self.out, self.added)}
        self.per_stage = 6 if kind == "sparse" else 3
        self.first_stage = 3 if kind == "sparse" else 2
        self.staged0 = self.staged.reserve(self.per_stage * tiles_)
        self.coef0 = self.coef.reserve(2 * n if kind == "sparse" else n)
        self.fox0 = self.foxed.reserve(n) if kind == "fox" else 0

    def v(self, signal, it, u):
        return self.b0[signal] + u + 1 + self.U * it

    def turns(self, eng, body):
        steps, per = range(self.U), self.tiles // 2 if self.kind == "sparse" else self.tiles
        for g in range(self.tiles // per):
            body(g * per, (g, max(g - 1, 0)), steps, g == 0)
            with eng.Fori(g * per + 1, (g + 1) * per) as it:
                body(it, (g, g), steps, False)
        body(self.tiles - 1, (g, g), range(self.U, self.U + self.LAG + 3), False)

    def small(self, k, u):
        return self.c.small[:, 16 * k + u % self.U:16 * k + u % self.U + 1]

    def tensor(self, pe):
        c, U, ring = self.c, self.U, self.RING
        sparse = self.kind == "sparse"
        self.more["wait_tensor"](pe)

        def body(it, groups, steps, first):
            for s in steps:
                u = s - self.LAG
                if u < U and (u >= 0 or not first):
                    i = self.units[u % U][2]
                    bank = self.TURN_BANKS[u % 2]
                    pe.wait_ge(self.probs.sem, self.v(self.probs, it, u))
                    if u >= 2 or not first:
                        pe.wait_ge(self.copied.sem, self.v(self.copied, it, u - 2))
                    for t in range(i + 1):
                        mm = pe.transpose(c.psum[:, bank, t * P:(t + 1) * P],
                                          self.probs_sb[u % self.PROBS][:, t * P:(t + 1) * P], c.sq["ident"][:])
                    mm.then_inc(self.turned.sem, 1)
                u = s - self.LAG - 2
                if u < U and (u >= 0 or not first):
                    h, b, i = self.units[u % U]
                    pair = it * P - (P if u < 0 else 0)
                    pe.wait_ge(self.copied.sem, self.v(self.copied, it, u))
                    if u >= 2 or not first:
                        pe.wait_ge(self.added.sem, self.v(self.added, it, u - 2))
                    for t in range(i + 1):
                        vals = self.more["values"][:, b, t, :] if sparse else \
                            self.more["values"][:, t, bass.ds(pair, P)]
                        mm = pe.matmul(c.psum[:, 1 + u % 2, 0:P], self.pt_sb[u % 4][:, t * P:(t + 1) * P], vals,
                                       start=(t == 0), stop=(t == i))
                    mm.then_inc(self.out.sem, 1)
                if s < U:
                    h, b, i = self.units[s]
                    if s == 0 or s == U // 2:
                        pe.wait_ge(self.staged.sem, self.staged0 + (self.first_stage if s == 0 else self.per_stage) + self.per_stage * it)
                    if s >= ring or not first:
                        pe.wait_ge(self.scored.sem, self.v(self.scored, it, s - ring))
                    width = (i + 1) * P
                    bank = self.SCORE_BANKS[s % ring]
                    out, t = c.psum[:, bank, 0:width], slice(i * P, (i + 1) * P)
                    if sparse:
                        keys = self.more["keys"][h][:, 2 * b + groups[0], 0:width]
                        pe.matmul(out, self.q_high[:, h, t], keys, start=True, stop=False)
                        mm = pe.matmul(out, self.q_low[:, h, t], keys, start=False, stop=True)
                    else:
                        pe.matmul(out, self.qs[:, h, t], self.ks[:, 0:width], start=True, stop=False)
                        mm = pe.matmul(c.psum[:, bank, i * P:width], c.sq["ident"][:], self.more["mask"][:],
                                       start=False, stop=True)
                    mm.then_inc(self.scores.sem, 1)
        self.turns(pe, body)

    def stage(self, act, it, first, h):
        c, U = self.c, self.U
        if self.kind == "sparse":
            if not first:
                act.wait_ge(self.scored.sem, self.v(self.scored, it, (h + 1) * U // 2 - 1 - U))
            act.activation(self.bias[:, h, :], self.more["distance"][:], ACT.Copy,
                           scale=c.col("slopes", 2 * it + h)).then_inc(self.staged.sem, 1)
        elif h == 0:
            if not first:
                act.wait_ge(self.scores.sem, self.v(self.scores, it, -1))
            act.activation(self.ks.rearrange("p (a n) -> p a n", a=1), self.more["keys"][:, bass.ds(it, 1), :],
                           ACT.Copy).then_inc(self.staged.sem, 1)
        if self.kind == "sparse":
            act.activation(self.q_high[:, h:h + 1, :], self.more["twice"][h][:, bass.ds(it, 1), :].bitcast(F32),
                           ACT.Copy).then_inc(self.staged.sem, 1)
            act.activation(self.q_low[:, h:h + 1, :], self.q[:, bass.ds(it, 1), :], ACT.Copy,
                           scale=c.col("halves", h)).then_inc(self.staged.sem, 1)
        else:
            act.activation(self.qs[:, h:h + 1, :], self.q[:, bass.ds(it, 1), :], ACT.Copy,
                           scale=c.col("halves", h)).then_inc(self.staged.sem, 1)

    def scalar(self, act):
        c, U, ring = self.c, self.U, self.RING
        self.more["wait_scalar"](act)
        act.preload_act_table(ACT.Exp)

        def body(it, groups, steps, first):
            for s in steps:
                u = s - self.LAG
                if u < U and (u >= 0 or not first):
                    width = (self.units[u % U][2] + 1) * P
                    act.wait_ge(self.turned.sem, self.v(self.turned, it, u))
                    if u >= 4 or not first:
                        act.wait_ge(self.out.sem, self.v(self.out, it, u - 4))
                    act.activation(self.pt_sb[u % 4][:, 0:width], c.psum[:, self.TURN_BANKS[u % 2], 0:width],
                                   ACT.Copy).then_inc(self.copied.sem, 1)
                if s == 0:
                    self.stage(act, it, first, 0)
                if s == self.U // 2 - 2:
                    self.stage(act, it, first, 1)
                if s < U:
                    width = (self.units[s][2] + 1) * P
                    act.wait_ge(self.scored.sem, self.v(self.scored, it, s))
                    if s >= self.PROBS or not first:
                        act.wait_ge(self.turned.sem, self.v(self.turned, it, s - self.PROBS))
                    act.activation(self.probs_sb[s % self.PROBS][:, 0:width], self.scores_sb[s % ring][:, 0:width],
                                   ACT.Exp, bias=self.small(0, s), scale=-1.0, accum_out=self.small(1, s)).then_inc(
                        self.probs.sem, 1)
        self.turns(act, body)

    def vector(self, dve):
        c, U, ring = self.c, self.U, self.RING
        self.more["wait_vector"](dve)

        def body(it, groups, steps, first):
            for s in steps:
                u = s - self.LAG - 3
                if u < U and (u >= 0 or not first):
                    self.add(dve, it, u, groups[u < 0])
                u = s - self.LAG - 2
                inside = u < U and (u >= 0 or not first)
                if inside:
                    if s >= U:
                        dve.wait_ge(self.probs.sem, self.v(self.probs, it, u))
                    dve.reciprocal(self.small(2, u), self.small(1, u)).then_inc(self.coef.sem, 1)
                if s < U:
                    self.score(dve, it, s, first)
                if inside and self.kind == "sparse":
                    self.gate(dve, it, u)
        self.turns(dve, body)

    def score(self, dve, it, s, first):
        c, U, ring = self.c, self.U, self.RING
        h, b, i = self.units[s]
        width = (i + 1) * P
        if s == 0:
            dve.wait_ge(self.staged.sem, self.staged0 + 2 + self.per_stage * it)
        if s == U // 2 and self.kind == "sparse":
            dve.wait_ge(self.staged.sem, self.staged0 + 4 + self.per_stage * it)
        dve.wait_ge(self.scores.sem, self.v(self.scores, it, s))
        if s >= ring or not first:
            dve.wait_ge(self.probs.sem, self.v(self.probs, it, s - ring))
        scores, out = c.psum[:, self.SCORE_BANKS[s % ring], 0:width], self.scores_sb[s % ring][:, 0:width]
        if self.kind == "sparse":
            dve.tensor_copy(self.small(4, s), c.eps[:])
            dve.tensor_tensor_reduce(out, scores, self.bias[:, h, S - width:S], -1.0, BIG, ALU.add,
                                     ALU.min, self.small(0, s)).then_inc(self.scored.sem, 1)
        else:
            at = it * 2 + h
            dve.scalar_tensor_tensor(out.rearrange("p (a n) -> p a n", a=1),
                                     self.more["sums"][:, bass.ds(at, 1), 0:width],
                                     self.more["own_sum"][:, i, bass.ds(at, 1)],
                                     scores.rearrange("p (a n) -> p a n", a=1),
                                     ALU.subtract, ALU.subtract).then_inc(self.foxed.sem, 1)
            dve.wait_ge(self.foxed.sem, self.fox0 + s + 1 + self.U * it)
            dve.tensor_reduce(self.small(0, s), out, AXX, ALU.min).then_inc(self.scored.sem, 1)

    def gate(self, dve, it, u):
        h, b, i = self.units[u % self.U]
        at = it * 2 + ((b + 1) * HEADS + h - (2 if u < 0 else 0))
        dve.wait_ge(self.coef.sem, self.coef0 + 2 * u + 1 + 2 * self.U * it)
        dve.tensor_tensor(self.small(3, u), self.small(2, u), self.more["gates"][:, i, bass.ds(at, 1)],
                          ALU.mult).then_inc(self.coef.sem, 1)

    def add(self, dve, it, u, g):
        c, U = self.c, self.U
        h, b, i = self.units[u % U]
        half = g if self.kind == "sparse" else h
        acc = c.psum[:, 1 + u % 2, half * HALF:(half + 1) * HALF]
        o = self.more["out"][:, i, bass.ds(it * P + (h * HALF - (P if u < 0 else 0)), HALF)]
        dve.wait_ge(self.out.sem, self.v(self.out, it, u))
        if self.kind == "sparse":
            dve.wait_ge(self.coef.sem, self.coef0 + 2 * u + 2 + 2 * U * it)
            dve.scalar_tensor_tensor(o, acc, self.small(3, u), o, ALU.mult, ALU.add).then_inc(self.added.sem, 1)
        else:
            dve.wait_ge(self.coef.sem, self.coef0 + u + 1 + U * it)
            dve.tensor_scalar(o, acc, self.small(2, u), None, ALU.mult).then_inc(self.added.sem, 1)


class Loads(Stage):

    def __init__(self, c, items, wait, signal):
        self.c, self.items, self.held_until = c, items, wait
        self.done = c.flag(signal)
        self.d0 = self.done.total
        self.done.reserve(16 * len(items))

    def value(self):
        return self.d0 + 16 * len(self.items)

    def gpsimd(self, pool):
        self.held_until(pool)
        for dst, src in self.items:
            pool.dma_start(dst, src).then_inc(self.done.sem, 16)


class GateNorm(Stage):

    def __init__(self, c, loads, v, v_stage, gain):
        self.c, self.loads, self.v, self.vs, self.gain = c, loads, v, v_stage, gain
        names = ("sg_square", "sg_summed", "sg_root", "sg_ready")
        self.squared, self.summed, self.root, self.normed = [c.flag(n) for n in names]
        self.ms = c.small[:, 0:16]
        self.chain = c.flag("vector_chain")

    def scalar(self, act):
        c = self.c
        for i in range(NT):
            act.wait_ge(self.vs.acted.sem, self.vs.acted0 + i + 1)
            after(act, self.summed, i - 1)
            act.activation(c.pre[:, i % 2, :], self.v[:, i, :], ACT.Square).then_inc(self.squared.sem, 1)
        act.wait_ge(self.summed.sem, NT)
        act.activation(self.ms, self.ms, ACT.Sqrt, bias=c.eps[:], scale=1.0 / P).then_inc(self.root.sem, 1)

    def vector(self, dve):
        c = self.c
        ch = Chain(dve, self.chain)
        for i in range(NT):
            dve.wait_ge(self.squared.sem, i + 1)
            dve.tensor_reduce(self.ms[:, 4 * i:4 * i + 4], c.pre[:, i % 2, :].rearrange("p (g n) -> p g n", g=4), AXX,
                              ALU.add).then_inc(self.summed.sem, 1)
        dve.wait_ge(self.root.sem, 1)
        ch.link(dve.reciprocal(self.ms, self.ms))
        dve.wait_ge(self.loads.done.sem, self.loads.value())
        for i in range(NT):
            for g in range(4):
                v = self.v[:, i, g * P:(g + 1) * P]
                dve.scalar_tensor_tensor(v, v, self.ms[:, 4 * i + g:4 * i + g + 1], self.gain[:, g * P:(g + 1) * P],
                                         ALU.mult, ALU.mult).then_inc(self.normed.sem, 1)


class SpatialGate(Stage):

    def __init__(self, c, loads, u, v, u_stage, gate_norm, w, bias, parts):
        self.c, self.loads, self.u, self.v, self.us, self.normed = c, loads, u, v, u_stage, gate_norm.normed
        self.w, self.bias, self.parts = w, bias, parts
        names = ("sg_masked", "sg_mixed", "sg_made", "sg_high", "sg_split")
        self.masked, self.mixed, self.made, self.high, self.ready = [c.flag(n) for n in names]
        self.chain = c.flag("vector_chain")

    def gpsimd(self, pool):
        pool.wait_ge(self.us.norm.stat.sem, self.us.norm.stat0 + 1)
        pool.wait_ge(self.loads.done.sem, self.loads.value())
        pool.memset(self.w[64:128, :, 0:64], 0.0).then_inc(self.masked.sem, 1)

    def scalar(self, act):
        c = self.c
        for g in range(4):
            act.wait_ge(self.made.sem, g + 1)
            act.activation(self.parts[0][:, g, :], c.up[:, g % 2, :], ACT.Copy).then_inc(self.high.sem, 1)

    def vector(self, dve):
        c = self.c
        ch = Chain(dve, self.chain)
        dve.wait_ge(self.us.acted.sem, self.us.acted0 + 4)
        for g in range(5):
            if g < 4:
                dve.wait_ge(self.mixed.sem, g + 1)
                t = c.pre[:, g % 2, :]
                ch.link(dve.tensor_tensor(t.rearrange("p (i n) -> p i n", i=NT),
                                          c.psum[:, 6 + g % 2, :].rearrange("p (i n) -> p i n", i=NT),
                                          self.bias[:, g:g + 1, :].to_broadcast([P, NT, P]), ALU.add))
                dve.tensor_tensor(c.up[:, g % 2, :], t, self.u[:, g, :], ALU.mult).then_inc(self.made.sem, 1)
            if g >= 1:
                dve.wait_ge(self.high.sem, g)
                dve.tensor_tensor(self.parts[1][:, g - 1, :], c.up[:, (g - 1) % 2, :],
                                  self.parts[0][:, g - 1, :].bitcast(F32), ALU.subtract).then_inc(self.ready.sem, 1)

    def tensor(self, pe):
        c = self.c
        pe.wait_ge(self.masked.sem, 1)
        pe.wait_ge(self.normed.sem, 16)
        for g in range(4):
            after(pe, self.made, g - 1)
            for i in range(NT):
                mm = pe.matmul(c.psum[:, 6 + g % 2, i * P:(i + 1) * P], self.v[:, i, g * P:(g + 1) * P],
                               self.w[:, g, :], start=True, stop=True, skip_group_check=True)
            mm.then_inc(self.mixed.sem, 1)


class LogForget(Stage):

    def __init__(self, c, loads, bf, tri, sums, free):
        self.c, self.loads, self.bf, self.tri, self.sums, self.free = c, loads, bf, tri, sums, free
        self.panel0, self.product0 = c.take_panels(1), c.take_products(1)
        c.take_products(3)
        self.own = c.place("own_sums", [P, NT, FOX])
        self.gq = c.place("fox_gain", [P, 1])
        self.z = [c.small[:, 64 + 32 * k:96 + 32 * k] for k in range(4)]
        self.turned = c.flag("lf_turned")
        names = ("lf_z", "lf_abs", "lf_exp", "lf_ln", "lf_done", "lf_sum", "lf_kept")
        (self.zed, self.absed, self.exped, self.lned, self.lf, self.summed, self.kept) = [c.flag(n) for n in names]
        self.chain = c.flag("vector_chain")

    def sync(self, sp):
        self.c.load_panel(sp, self.panel0, None, self.panel0, self.c.dram["e_w_f"], KD * FOX)

    def tensor(self, pe):
        c = self.c
        slot, n = self.panel0 % SLOTS, self.panel0
        pe.wait_ge(c.weights_split.sem, n + 1)
        after(pe, c.banks_freed, self.product0 - (RING_BANKS - 1))
        for k in range(KD):
            w = slice(k * FOX, (k + 1) * FOX)
            mm = three(c.nc, c.psum[0:FOX, self.product0 % RING_BANKS, :], c.wh[:, slot, w], c.wl[:, slot, w],
                       c.xh[:, k, :], c.xl[:, k, :], k == 0, k == KD - 1)
        mm.then_inc(c.panels_used.sem, 1)
        pe.wait_ge(c.banks_freed.sem, self.product0 + 1)
        for i in range(NT):
            mm = pe.transpose(c.psum[:, 5, i * FOX:(i + 1) * FOX], c.up[0:FOX, 0, i * P:(i + 1) * P],
                              c.sq["ident"][0:FOX, 0:FOX])
        mm.then_inc(self.turned.sem, 1)

    def scalar(self, act):
        c = self.c
        c.ahead(c.split_high, act, self.panel0, 0, 0, 1)
        act.wait_ge(self.zed.sem, NT)
        act.activation(self.z[1], self.z[0], ACT.Abs).then_inc(self.absed.sem, 1)
        act.wait_ge(self.absed.sem, 1)
        act.activation(self.z[1], self.z[1], ACT.Exp, scale=-1.0).then_inc(self.exped.sem, 1)
        act.wait_ge(self.exped.sem, 1)
        act.activation(self.z[1], self.z[1], ACT.Ln, bias=c.sq["ones"][:, 0:1]).then_inc(self.lned.sem, 1)

    def vector(self, dve):
        c = self.c
        ch = Chain(dve, self.chain)
        bank = self.product0 % RING_BANKS
        c.ahead(c.split_low, dve, self.panel0, 0, 0, 1)
        dve.wait_ge(self.loads.done.sem, self.loads.value())
        dve.wait_ge(c.panels_used.sem, self.panel0 + 1)
        dve.tensor_copy(c.up[0:FOX, 0, :], c.psum[0:FOX, bank, :]).then_inc(c.banks_freed.sem, 1)
        dve.wait_ge(self.turned.sem, 1)
        for i in range(NT):
            t = slice(i * FOX, (i + 1) * FOX)
            dve.scalar_tensor_tensor(self.z[0][:, t], c.psum[:, 5, t], c.rstd_tok[:, i:i + 1], self.bf[:],
                                     ALU.mult, ALU.add).then_inc(self.zed.sem, 1)
        dve.wait_ge(self.zed.sem, NT)
        dve.wait_ge(c.banks_freed.sem, self.product0 + 1)
        dve.sem_inc(c.banks_freed.sem, 3)
        ch.link(dve.tensor_scalar(self.gq[:], c.col("e_gq"), 1.0 / 8, None, ALU.mult))
        ch.link(dve.tensor_scalar(self.z[2], self.z[0], 0.0, None, ALU.min))
        dve.wait_ge(self.lned.sem, 1)
        dve.tensor_tensor(self.z[3], self.z[2], self.z[1], ALU.subtract).then_inc(self.lf.sem, 1)


class ForgetSums(Stage):

    def __init__(self, c, lf):
        self.c, self.lf = c, lf

    def tensor(self, pe):
        c, s = self.c, self.lf
        lf, tri = s.z[3].rearrange("p (i h) -> p i h", i=NT), s.tri
        pe.wait_ge(s.lf.sem, 1)
        for i in range(NT):
            for j in range(i + 1):
                mm = pe.matmul(c.psum[:, 6, i * FOX:(i + 1) * FOX], tri[:, 0:P] if j == i else tri[:, P:2 * P],
                               lf[:, j, :], start=(j == 0), stop=(j == i), skip_group_check=True)
        mm.then_inc(s.summed.sem, 1)
        pe.wait_ge(s.kept.sem, 1)
        for h in range(FOX):
            after(pe, s.kept, h if h >= 2 else 0)
            for i in range(NT):
                mm = pe.matmul(c.psum[:, 4 + h % 2, i * P:(i + 1) * P], s.own[:, i, h:h + 1].to_broadcast([P, P]),
                               c.sq["ident"][:], start=True, stop=True, skip_group_check=True)
            mm.then_inc(s.summed.sem, 1)

    def scalar(self, act):
        c, s = self.c, self.lf
        act.wait_ge(s.summed.sem, 1)
        act.activation(s.own[:], c.psum[:, 6, 0:NT * FOX].rearrange("p (i h) -> p i h", i=NT), ACT.Copy).then_inc(
            s.kept.sem, 1)
        s.free(act)
        for h in range(FOX):
            act.wait_ge(s.summed.sem, h + 2)
            act.activation(s.sums[:, h, :], c.psum[:, 4 + h % 2, :], ACT.Copy).then_inc(s.kept.sem, 1)


class PoolMeans(Stage):
    W = 16

    def __init__(self, c, loads, zc, project, inv, pads):
        self.c, self.loads, self.zc, self.project, self.inv, self.pads = c, loads, zc, project, inv, pads
        self.t = [c.arena(f"pool_t{k}", 74 + 2.5 * k, [P, self.W + S]) for k in range(2)]
        self.pooled = c.flag("pooled")
        self.chain = c.flag("vector_chain")

    def gpsimd(self, pool):
        pool.memset(self.t[0][:, 0:self.W], 0.0).then_inc(self.pads.sem, 1)
        pool.memset(self.t[1][:, 0:self.W], 0.0).then_inc(self.pads.sem, 1)

    def vector(self, dve):
        c, W = self.c, self.W
        ch = Chain(dve, self.chain)
        dve.wait_ge(self.pads.sem, 3)
        dve.wait_ge(self.loads.done.sem, self.loads.value())
        dve.wait_ge(c.banks_freed.sem, self.project.product0 + 4)
        for g, w in enumerate(POOLS):
            src, k = self.zc[:, g, :], 0
            for level in range(g + 1):
                dst = self.t[k]
                shift = 1 << level
                ch.link(dve.tensor_tensor(dst[:, W:], src[:, W:], src[:, W - shift:W + S - shift], ALU.add))
                src, k = dst, 1 - k
            mean = self.t[k]
            ch.link(dve.tensor_scalar(mean[:, W:], src[:, W:], 1.0 / w, None, ALU.mult))
            ch.link(dve.tensor_tensor(mean[:, W:2 * W], src[:, W:2 * W], self.inv[:, g, :], ALU.mult))
            dve.tensor_tensor(self.zc[:, g, W:], mean[:, W:], self.zc[:, g, W:], ALU.subtract).then_inc(
                self.pooled.sem, 1)
            dve.wait_ge(self.pooled.sem, g + 1)


class ShortTaps(Stage):

    def __init__(self, c, hgg, project, pads):
        self.c, self.hgg, self.project, self.pads = c, hgg, project, pads
        self.xg = c.arena("pool_xg", 65, [P, 4, 2 + S])
        self.chain = c.flag("vector_chain")

    def gpsimd(self, pool):
        pool.memset(self.xg[:, :, 0:2], 0.0).then_inc(self.pads.sem, 1)

    def vector(self, dve):
        c = self.c
        ch = Chain(dve, self.chain)
        dve.wait_ge(self.pads.sem, 4)
        dve.wait_ge(c.banks_freed.sem, self.project.product0 + 4)
        for t in range(4):
            hd, gc = self.hgg[:, t, :], self.hgg[:, 8 + t, :]
            x = self.xg[:, t, :]
            ch.link(dve.tensor_tensor(x[:, 2:], gc, hd, ALU.mult))
            ch.link(dve.tensor_scalar(hd, x[:, 0:S], c.col("conv_w", t), None, ALU.mult))
            ch.link(dve.scalar_tensor_tensor(hd, x[:, 1:1 + S], c.col("conv_w", 4 + t), hd, ALU.mult, ALU.add))
            ch.link(dve.scalar_tensor_tensor(hd, x[:, 2:2 + S], c.col("conv_w", 8 + t), hd, ALU.mult, ALU.add))


class OddParts(Stage):

    def __init__(self, c, loads, means, hgg, gate, parts, wpool):
        self.c, self.loads, self.means, self.hgg, self.gate = c, loads, means, hgg, gate
        self.parts, self.wpool = parts, wpool
        self.ready, self.high = c.flag("pc_ready"), c.flag("pc_high")
        self.ready0 = 0
        self.mapped, self.made = c.flag("pool_mapped"), c.flag("pc_made")

    def vector(self, dve):
        c = self.c
        dve.wait_ge(c.banks_freed.sem, self.gate.product0 + 4)
        for t in range(4):
            gb = self.hgg[:, 4 + t, :]
            dve.tensor_tensor(gb, self.hgg[:, t, :], gb, ALU.mult).then_inc(self.made.sem, 1)
        dve.wait_ge(self.made.sem, 4)
        for g in range(4):
            dve.wait_ge(self.high.sem, g + 1)
            dve.scalar_tensor_tensor(self.parts[1][:, g, :], c.psum[:, 6 + g % 2, :], c.col("s_pool", g),
                                     self.parts[0][:, g, :].bitcast(F32), ALU.mult, ALU.subtract).then_inc(
                self.ready.sem, 1)
        for t in range(4):
            dve.wait_ge(self.high.sem, 4 + t + 1)
            dve.tensor_tensor(self.parts[1][:, 4 + t, :], self.hgg[:, 4 + t, :],
                              self.parts[0][:, 4 + t, :].bitcast(F32), ALU.subtract).then_inc(self.ready.sem, 1)

    def scalar(self, act):
        c = self.c
        for g in range(4):
            act.wait_ge(self.mapped.sem, g + 1)
            act.activation(self.parts[0][:, g, :], c.psum[:, 6 + g % 2, :], ACT.Copy, scale=c.col("s_pool", g)
                           ).then_inc(self.high.sem, 1)
        for t in range(4):
            act.wait_ge(self.made.sem, t + 1)
            act.activation(self.parts[0][:, 4 + t, :], self.hgg[:, 4 + t, :], ACT.Copy).then_inc(self.high.sem, 1)

    def tensor(self, pe):
        c = self.c
        pe.wait_ge(self.loads.done.sem, self.loads.value())
        for g in range(4):
            pe.wait_ge(self.means.pooled.sem, g + 1)
            after(pe, self.ready, g - 1)
            pe.matmul(c.psum[:, 6 + g % 2, :], self.wpool[:, g, :], self.means.zc[:, g, PoolMeans.W:], start=True,
                      stop=True).then_inc(self.mapped.sem, 1)


class MemoryLoad(Stage):

    def __init__(self, mem):
        self.mem = mem

    def gpsimd(self, pool):
        self.mem.load(pool)


class Memory(Stage):

    def __init__(self, c, layer, wait, mixer):
        self.c, self.layer, self.held_until, self.mixer = c, layer, wait, mixer
        n = f"mem{layer}_"
        self.m = c.arena(n + "x", 64, [P, KD, MEM])
        self.parts = (c.arena(n + "high", 72, [P, KD, MEM], FR), c.arena(n + "low", 80, [P, KD, MEM], FR))
        self.sq = c.arena(n + "sq", 60, [P, 2, MEM])
        self.sum = c.arena(n + "sum", 62, [P, MEM])
        self.rs = c.arena(n + "rs", 63, [P, MEM])
        names = ("mem_in", "mem_squared", "mem_summed", "mem_stat", "mem_root", "mem_normed", "mem_high", "mem_ready")
        (self.loaded, self.squared, self.summed, self.stat, self.root, self.normed, self.high,
         self.ready) = [c.flag(x) for x in names]
        self.s = [s.reserve(k) for s, k in ((self.loaded, 16), (self.squared, KD), (self.summed, KD + 1),
                                            (self.stat, 1), (self.root, 1), (self.normed, KD + 1), (self.high, KD),
                                            (self.ready, KD))]
        self.ready0 = self.s[7]

    def load(self, pool):
        self.held_until(pool)
        pool.dma_start(self.m[:], self.c.dram["memT"]).then_inc(self.loaded.sem, 16)
        pool.memset(self.sum[:], 0.0).then_inc(self.summed.sem, 1)
        pool.wait_ge(self.loaded.sem, self.s[0] + 16)
        for k in range(KD):
            pool.tensor_tensor(self.sq[:, k % 2, :], self.m[:, k, :], self.m[:, k, :], ALU.mult).then_inc(
                self.squared.sem, 1)
            pool.wait_ge(self.squared.sem, self.s[1] + k + 1)
            pool.wait_ge(self.summed.sem, self.s[2] + k + 1)
            pool.tensor_tensor(self.sum[:], self.sum[:], self.sq[:, k % 2, :], ALU.add).then_inc(self.summed.sem, 1)

    def tensor(self, pe):
        c = self.c
        pe.wait_ge(self.summed.sem, self.s[2] + KD + 1)
        pe.wait_ge(self.mixer.ready.sem, self.mixer.ready0 + KD)
        pe.matmul(c.psum[:, 6, 0:MEM], c.sq["mean"][:], self.sum[:], start=True, stop=True).then_inc(self.stat.sem, 1)

    def scalar(self, act):
        c = self.c
        act.wait_ge(self.stat.sem, self.s[3] + 1)
        act.activation(self.rs[:], c.psum[:, 6, 0:MEM], ACT.Sqrt, bias=c.eps[:]).then_inc(self.root.sem, 1)
        for k in range(KD):
            act.wait_ge(self.normed.sem, self.s[5] + k + 2)
            act.activation(self.parts[0][:, k, :], self.m[:, k, :], ACT.Copy).then_inc(self.high.sem, 1)

    def vector(self, dve):
        c = self.c
        dve.wait_ge(self.root.sem, self.s[4] + 1)
        dve.reciprocal(self.rs[:], self.rs[:]).then_inc(self.normed.sem, 1)
        dve.wait_ge(self.normed.sem, self.s[5] + 1)
        for k in range(KD):
            dve.scalar_tensor_tensor(self.m[:, k, :], self.m[:, k, :], c.col("g_mem", 8 * self.layer + k), self.rs[:],
                                     ALU.mult, ALU.mult).then_inc(self.normed.sem, 1)
        for k in range(KD):
            dve.wait_ge(self.high.sem, self.s[6] + k + 1)
            dve.tensor_tensor(self.parts[1][:, k, :], self.m[:, k, :], self.parts[0][:, k, :].bitcast(F32),
                              ALU.subtract).then_inc(self.ready.sem, 1)


class MemoryKeys(Stage):

    def __init__(self, c, weights, mem, dest):
        self.c, self.weights, self.mem, self.dest = c, weights, mem, dest
        self.panel0, self.product0 = c.take_panels(4), c.take_products(4)

    def sync(self, sp):
        c = self.c
        for j in range(4):
            n = self.panel0 + j
            c.load_panel(sp, n, None, n, c.dram[self.weights][j], PANEL)

    def tensor(self, pe):
        c = self.c
        ah, al = self.mem.parts
        for j in range(4):
            n, t = self.panel0 + j, self.product0 + j
            after(pe, c.banks_freed, t - (RING_BANKS - 1))
            pe.wait_ge(c.weights_split.sem, n + 1)
            for k in range(KD):
                pe.wait_ge(self.mem.ready.sem, self.mem.ready0 + k + 1)
                w = slice(k * P, (k + 1) * P)
                mm = three(c.nc, c.psum[:, t % RING_BANKS, 0:MEM], c.wh[:, n % SLOTS, w], c.wl[:, n % SLOTS, w],
                           ah[:, k, :], al[:, k, :], k == 0, k == KD - 1)
            mm.then_inc(c.panels_used.sem, 1)

    def scalar(self, act):
        for j in range(4):
            self.c.ahead(self.c.split_high, act, self.panel0, j, 0, 4)

    def vector(self, dve):
        c = self.c
        for j in range(4):
            dve.wait_ge(c.panels_used.sem, self.panel0 + j + 1)
            dve.tensor_copy(self.dest[:, j, :], c.psum[:, (self.product0 + j) % RING_BANKS, 0:MEM]).then_inc(
                c.banks_freed.sem, 1)
            c.ahead(c.split_low, dve, self.panel0, j, 0, 4)


class MemoryAttention(Stage):
    SCALE = 1.0 / float(np.sqrt(P))

    def __init__(self, c, layer, q, keys, values, parts, wait):
        self.c, self.q, self.keys, self.values, self.parts, self.held_until = c, q, keys, values, parts, wait
        n = f"xa{layer}_"
        self.probs = [c.arena(n + f"p{k}", 56 + k, [P, MEM]) for k in range(3)]
        self.pt = [c.arena(n + f"pt{k}", 24 + 4 * k, [P, 2, S]) for k in range(2)]
        names = ("xm_scores", "xm_max", "xm_exp", "xm_sum", "xm_probs", "xm_turned", "xm_copied", "xm_out",
                 "xm_high", "xm_ready")
        (self.scores, self.maxed, self.exped, self.summed, self.probd, self.turned, self.copied, self.out,
         self.high, self.ready) = [c.flag(x) for x in names]
        u = 4 * NT
        self.b = [s.reserve(k) for s, k in ((self.scores, u), (self.maxed, 2 * u), (self.exped, u), (self.summed, u),
                                            (self.probd, u), (self.turned, u), (self.copied, u), (self.out, 4),
                                            (self.high, 4), (self.ready, 4))]
        self.ready0 = self.b[9]

    def tensor(self, pe):
        c, U = self.c, 4 * NT
        self.held_until(pe)
        for s in range(U + 3):
            if s < U:
                h, i = divmod(s, NT)
                if s >= 2:
                    pe.wait_ge(self.exped.sem, self.b[2] + s - 1)
                pe.matmul(c.psum[:, 4 + s % 2, 0:MEM], self.q[:, h, i * P:(i + 1) * P], self.keys[:, h, :],
                          start=True, stop=True).then_inc(self.scores.sem, 1)
            u = s - 2
            if 0 <= u < U:
                pe.wait_ge(self.probd.sem, self.b[4] + u + 1)
                if u >= 2:
                    pe.wait_ge(self.copied.sem, self.b[6] + u - 1)
                for a in range(2):
                    mm = pe.transpose(c.psum[:, (7, 0)[u % 2], a * P:(a + 1) * P],
                                      self.probs[u % 3][:, a * P:(a + 1) * P], c.sq["ident"][:])
                mm.then_inc(self.turned.sem, 1)
            u = s - 3
            if u >= 0 and u % NT == NT - 1:
                h = u // NT
                pe.wait_ge(self.copied.sem, self.b[6] + u + 1)
                if h >= 2:
                    pe.wait_ge(self.ready.sem, self.b[9] + h - 1)
                for a in range(2):
                    mm = pe.matmul(c.psum[:, 1 + h % 2, :], self.values[:, a, h * P:(h + 1) * P],
                                   self.pt[h % 2][:, a, :], start=(a == 0), stop=(a == 1))
                mm.then_inc(self.out.sem, 1)

    def scalar(self, act):
        c, U = self.c, 4 * NT
        self.held_until(act)
        for s in range(U + 4):
            if s < U:
                act.wait_ge(self.maxed.sem, self.b[1] + 2 * s + 2)
                if s >= 3:
                    act.wait_ge(self.turned.sem, self.b[5] + s - 2)
                act.activation(self.probs[s % 3][:], c.psum[:, 4 + s % 2, 0:MEM], ACT.Exp,
                               bias=c.small[:, 16 + s:17 + s], scale=self.SCALE,
                               accum_out=c.small[:, 32 + s:33 + s]).then_inc(self.exped.sem, 1)
            u = s - 2
            if 0 <= u < U:
                h, i = divmod(u, NT)
                act.wait_ge(self.turned.sem, self.b[5] + u + 1)
                if h >= 2 and i == 0:
                    act.wait_ge(self.out.sem, self.b[7] + h - 1)
                act.activation(self.pt[h % 2][:, :, i * P:(i + 1) * P],
                               c.psum[:, (7, 0)[u % 2], 0:MEM].rearrange("p (a n) -> p a n", a=2),
                               ACT.Copy).then_inc(self.copied.sem, 1)
            u = s - 4
            if u >= 0 and u % NT == NT - 1:
                h = u // NT
                act.wait_ge(self.out.sem, self.b[7] + h + 1)
                act.activation(self.parts[0][:, h, :], c.psum[:, 1 + h % 2, :], ACT.Copy).then_inc(self.high.sem, 1)

    def vector(self, dve):
        c, U = self.c, 4 * NT
        self.held_until(dve)
        for s in range(U + 5):
            if s < U:
                dve.wait_ge(self.scores.sem, self.b[0] + s + 1)
                dve.tensor_reduce(c.small[:, s:s + 1], c.psum[:, 4 + s % 2, 0:MEM], AXX, ALU.max).then_inc(
                    self.maxed.sem, 1)
                dve.wait_ge(self.maxed.sem, self.b[1] + 2 * s + 1)
                dve.tensor_scalar(c.small[:, 16 + s:17 + s], c.small[:, s:s + 1], -self.SCALE, None,
                                  ALU.mult).then_inc(self.maxed.sem, 1)
            u = s - 1
            if 0 <= u < U:
                dve.wait_ge(self.exped.sem, self.b[2] + u + 1)
                dve.reciprocal(c.small[:, 48 + u:49 + u], c.small[:, 32 + u:33 + u]).then_inc(self.summed.sem, 1)
                dve.wait_ge(self.summed.sem, self.b[3] + u + 1)
                dve.tensor_scalar(self.probs[u % 3][:], self.probs[u % 3][:], c.small[:, 48 + u:49 + u], None,
                                  ALU.mult).then_inc(self.probd.sem, 1)
            u = s - 5
            if u >= 0 and u % NT == NT - 1:
                self.low(dve, u // NT)

    def low(self, dve, h):
        c = self.c
        dve.wait_ge(self.high.sem, self.b[8] + h + 1)
        dve.tensor_tensor(self.parts[1][:, h, :], c.psum[:, 1 + h % 2, :], self.parts[0][:, h, :].bitcast(F32),
                          ALU.subtract).then_inc(self.ready.sem, 1)


class From:

    def __init__(self, ready, ready0):
        self.ready, self.ready0 = ready, ready0


def plan(c):
    stages = []

    def add(stage):
        stages.append(stage)
        return stage

    def feed_forward(w_in, w_out, source, norm, gain, last=False):
        gated = add(Gated(c, w_in, KF, source, norm, hidden=hidden))
        return add(Residual(c, w_out, hidden, From(gated.ready, gated.ready0), [7, 7, 8], 1, gain, last=last))

    def memory_attention(layer, free, w_out, mixer_parts, source):
        mem = Memory(c, layer, free, source)
        add(MemoryLoad(mem))
        res = add(Residual(c, w_out, mixer_parts, source, [KD], 1, ("g_xa", KD * layer)))
        norm = add(Norm(c, res))
        add(mem)
        mk = c.arena(f"mk{layer}", 48, [P, XAH, MEM])
        mv = c.arena(f"mv{layer}", 52, [P, 2, 512])
        q = c.arena(f"xq{layer}", 16, [P, XAH, S])
        qs = add(Project(c, f"xa_wq{layer}", XAH, (c.xh, c.xl), res, norm, q))
        keys = add(MemoryKeys(c, f"xa_wk{layer}", mem, mk))

        def queries(eng):
            eng.wait_ge(c.banks_freed.sem, qs.product0 + XAH)

        def both(eng):
            eng.wait_ge(c.banks_freed.sem, keys.product0 + XAH)
        rows = [c.pre[:, 0, :], c.pre[:, 1, :], c.up[:, 0, :], c.up[:, 1, :]]
        qsum = HeadSums(c, f"xq_rms{layer}", [q[:, h, :] for h in range(XAH)], 1, S, queries, rows)
        rows = [c.square[:, k // 2, k % 2 * MEM:(k % 2 + 1) * MEM] for k in range(XAH)]
        ksum = HeadSums(c, f"xk_rms{layer}", [mk[:, h, :] for h in range(XAH)], 1, MEM, both, rows)
        add(HeadSquares(qsum))
        add(HeadSquares(ksum))
        add(ProjectTokens(c, f"xa_wv{layer}", mem.parts, mem, mv, tiles_=2))
        add(qsum)
        add(ksum)
        add(HeadScale(c, ksum, [c.col("xa_gk", layer)] * XAH))
        hn = add(HeadScale(c, qsum, [c.col("xa_gq", layer)] * XAH))
        parts = (c.arena(f"xo_high{layer}", 0, [P, XAH, S], FR), c.arena(f"xo_low{layer}", 8, [P, XAH, S], FR))

        def normed(eng):
            eng.wait_ge(hn.done.sem, hn.d0 + XAH)
            eng.wait_ge(c.banks_freed.sem, keys.product0 + XAH + RING_BANKS)
        att = add(MemoryAttention(c, layer, q, mk, mv, parts, normed))
        res = add(Residual(c, f"xa_wo{layer}", parts, att, [XAH], 2, ("g_ffn", KD * layer)))
        return res, add(Norm(c, res))

    add(Load(c))
    hidden = (c.arena("hidden_high", 0, [P, KF, S], FR), c.arena("hidden_low", 44, [P, KF, S], FR))

    start = add(Prepare(c, ("a_norm", 0)))
    add(FirstPanels(c))
    norm = add(Norm(c, start))
    conv_at = len(stages)
    pw1 = add(Gated(c, "pw1", KD, start, norm, conv=True))
    conv = add(Convolution(c, pw1))
    pw1.conv, pw1.taps = conv.padded, conv
    stages.insert(conv_at, PadZeros(c, conv.padded, PAD, "pads"))
    res = add(Residual(c, "pw2", conv.parts, conv, [KD], 1, ("ffn_norm", 0), bias="pw2_b"))
    norm = add(Norm(c, res))
    res = feed_forward("ffn_in0", "ffn_out0", res, norm, ("kv_norm", 0))
    norm = add(Norm(c, res))

    kv = add(KeysValues(c, res, norm))
    comp = Compress(c, kv)
    add(CompressBlocks(comp))
    q = c.arena("queries", 72, [P, KD, S])
    qp = add(Project(c, "w_q", KD, kv.parts, kv, norm, q, scale=0.125))
    gates = add(Gates(c, kv, norm))
    stacked = add(StackQueries(c, q, qp))
    comp.gates = gates
    add(comp)
    cmp_att = add(CompressedAttention(c, q, kv, comp, gates, qp))
    distance = c.arena("distance", 28, [P, S])

    def gates_done(pool):
        pool.wait_ge(gates.turned.sem, 1)
    dist = add(Loads(c, [(distance[:], c.dram["distance"])], gates_done, "distance_in"))

    def wait_tensor(pe):
        pe.wait_ge(cmp_att.kept.sem, 8)
        pe.wait_ge(keys.high.sem, 8)
        pe.wait_ge(keys.done.sem, 8)
        pe.wait_ge(kv.copied.sem, 2)

    def wait_scalar(act):
        act.wait_ge(dist.done.sem, dist.value())
        act.wait_ge(stacked.copied.sem, 32)
        act.wait_ge(stacked.low_done.sem, 2)
        act.wait_ge(cmp_att.kept.sem, 8)
    keys = add(StackKeys(c, kv, cmp_att))
    att = add(CausalAttention(c, "sparse", "sparse", stacked.low, KD, (0, 72, (8, 10, 30, 56)), keys=(keys.even, keys.odd),
                              twice=stacked.twice, values=kv.values,
                              distance=distance, gates=gates.gates, out=cmp_att.o, wait_tensor=wait_tensor,
                              wait_scalar=wait_scalar, wait_vector=lambda dve: None))
    done = att.v(att.added, KD - 1, att.U - 1)
    parts = (c.arena("o_high", 0, [P, KD, S], FR), c.arena("o_low", 16, [P, KD, S], FR))
    split = add(Split(c, cmp_att.o, KD, parts, 0, lambda pe: pe.wait_ge(att.added.sem, done)))
    res = add(Residual(c, "w_o", parts, From(split.ready, split.r0), [KD], 1, ("ffn_norm", KD)))
    norm = add(Norm(c, res))
    res = feed_forward("ffn_in1", "ffn_out1", res, norm, None)
    norm = add(Norm(c, res, now=True))

    start = add(Prepare(c, ("g_mix", 0), norm=norm))
    norm = add(Norm(c, start))
    parts = (c.arena("ey_high", 0, [P, KD, S], FR), c.arena("ey_low", 16, [P, KD, S], FR))
    u, v = c.arena("u", 32, [P, 4, S]), c.arena("v", 40, [P, NT, 512])
    ws, gv, bs = c.arena("w_s", 48, [P, 4, P]), c.arena("g_v", 50, [P, 512]), c.arena("b_s", 52, [P, 4, P])
    qk, vv = c.arena("fox_qk", 54, [P, 8, S]), c.arena("fox_v", 70, [P, NT, 512])
    tri = c.arena("tri", 84, [P, S])
    bf, mask = c.place("b_f", [P, FOX]), c.place("mask", [P, P])
    hidden_read = res.product0 + KD

    def arena_free(pool):
        pool.wait_ge(c.banks_freed.sem, hidden_read)
    loads = add(Loads(c, [(ws[:], c.dram["e_w_s"]), (gv[:], c.dram["e_g_v"].to_broadcast([P, 512])),
                          (bs[:], c.dram["e_b_s"].to_broadcast([P, 4, P])), (tri[:], c.dram["tri"]),
                          (bf[:], c.dram["e_b_f"].to_broadcast([P, FOX])), (mask[:], c.dram["mask"])],
                      arena_free, "even_in"))
    up = add(Project(c, "e_w_u", 4, (c.xh, c.xl), start, norm, u, func=ACT.Gelu_apprx_tanh))
    vp = add(ProjectTokens(c, "e_w_v", (c.xh, c.xl), start, v, norm=norm, func=ACT.Gelu_apprx_tanh))
    gate_norm = GateNorm(c, loads, v, vp, gv)
    spatial = SpatialGate(c, loads, u, v, up, gate_norm, ws, bs, parts)
    sums = c.arena("sums", 32, [P, FOX, S])

    def sums_free(act):
        act.wait_ge(spatial.ready.sem, 4)
    lf = add(LogForget(c, loads, bf, tri, sums, sums_free))
    add(gate_norm)
    qkp = add(Project(c, "e_w_qk", 8, (c.xh, c.xl), start, norm, qk))
    add(spatial)
    def qk_done(eng):
        eng.wait_ge(c.banks_freed.sem, qkp.product0 + 8)
        eng.wait_ge(spatial.ready.sem, 4)
    rows = [c.pre[:, 0, :], c.pre[:, 1, :], c.up[:, 0, :], c.up[:, 1, :], c.square[:, 0, :], c.square[:, 1, :],
            c.ssq[:], c.rstd[:]]
    qk_sums = HeadSums(c, "fox_rms", [qk[:, t, :] for t in range(8)], 2, S, qk_done, rows)
    add(HeadSquares(qk_sums))
    vvp = add(ProjectTokens(c, "e_w_vv", (c.xh, c.xl), start, vv, norm=norm))
    add(qk_sums)
    add(ForgetSums(c, lf))
    hn = add(HeadScale(c, qk_sums, [lf.gq[:] if t < 4 else c.col("e_gk") for t in range(8)]))
    o = c.place("fox_o", [P, NT, 512], offset=c.xh_at)

    borrowed = (c.xh_at - c.arena0) / 1024

    def fox_tensor(pe):
        pe.wait_ge(hn.done.sem, hn.d0 + 8)
        pe.wait_ge(lf.kept.sem, FOX + 1)
        pe.wait_ge(c.banks_freed.sem, vvp.product0 + 4)

    def fox_other(eng):
        eng.wait_ge(hn.done.sem, hn.d0 + 8)
        eng.wait_ge(lf.kept.sem, FOX + 1)
    att = add(CausalAttention(c, "fox", "fox", qk[:, 0:4, :], 4, (borrowed + 8, borrowed + 16, (78, 80, 82, 84)), keys=qk[:, 4:8, :], values=vv,
                              sums=sums, own_sum=lf.own, mask=mask, out=o, wait_tensor=fox_tensor,
                              wait_scalar=fox_other, wait_vector=fox_other))
    fox_done = att.v(att.added, 3, att.U - 1)
    split = add(Split(c, o, 4, parts, 4, lambda pe: pe.wait_ge(att.added.sem, fox_done)))
    res, norm = memory_attention(0, lambda pool: pool.wait_ge(att.added.sem, fox_done), "e_w_out", parts,
                                 From(split.ready, split.r0 - 4))
    res = feed_forward("ffn2_in0", "ffn2_out0", res, norm, ("g_mix", KD))
    norm = add(Norm(c, res))

    parts = (c.arena("oy_high", 0, [P, KD, S], FR), c.arena("oy_low", 16, [P, KD, S], FR))
    hgg = c.arena("hgg", 32, [P, 12, S])
    zc = c.arena("zc", 56, [P, 4, PoolMeans.W + S])
    wpool, inv = c.arena("w_pool", 80, [P, 4, P]), c.arena("inverse_counts", 82, [P, 4, PoolMeans.W])
    free1 = res.product0 + KD

    def arena_free1(pool):
        pool.wait_ge(c.banks_freed.sem, free1)
    loads = add(Loads(c, [(wpool[:], c.dram["o_w_pool"]), (inv[:], c.dram["inverse_counts"])], arena_free1,
                      "odd_in"))
    pads = add(PadZeros(c, zc, PoolMeans.W, "odd_pads"))
    zs = add(Project(c, "o_w_c", 4, (c.xh, c.xl), res, norm, zc, pad=PoolMeans.W))
    means = add(PoolMeans(c, loads, zc, zs, inv, pads.done))
    add(Project(c, "o_w_hgg", 4, (c.xh, c.xl), res, norm, hgg[:, 8:12, :], first=8))
    hs = add(Project(c, "o_w_hgg", 4, (c.xh, c.xl), res, norm, hgg[:, 0:4, :]))
    add(ShortTaps(c, hgg, hs, pads.done))
    gate = add(Project(c, "o_w_hgg", 4, (c.xh, c.xl), res, norm, hgg[:, 4:8, :], first=4))
    pc = add(OddParts(c, loads, means, hgg, gate, parts, wpool))
    res, norm = memory_attention(1, lambda pool: pool.wait_ge(pc.ready.sem, 8), "o_w_out", parts, pc)
    res = feed_forward("ffn2_in1", "ffn2_out1", res, norm, None, last=True)
    add(Store(c, res))
    c.last_panel = c.panels
    return stages


def program(nc, dram):
    with ExitStack() as ctx:
        stages = plan(Core(nc, ctx, dram))
        block = ctx.enter_context(nc.Block())

        @block.sync
        def _(sp):
            for stage in stages:
                stage.sync(sp)

        @block.gpsimd
        def _(pool):
            for stage in stages:
                stage.gpsimd(pool)

        @block.scalar
        def _(act):
            for stage in stages:
                stage.scalar(act)

        @block.vector
        def _(dve):
            for stage in stages:
                stage.vector(dve)

        @block.tensor
        def _(pe):
            for stage in stages:
                stage.tensor(pe)


def blocks(w, m=P):
    k, n = w.shape
    return w.reshape(k // P, P, n // m, m).transpose(2, 1, 0, 3).reshape(n // m, P, k // P * m)


def rows(w, per=2):
    k, n = w.shape
    return w.reshape(k // P // per, per, P, n).transpose(0, 2, 1, 3).reshape(k // P // per, P, per * n)


def tiles(v):
    return v.reshape(-1, P).T


def narrow(w):
    k, n = w.shape
    return w.reshape(k // P, P, n).transpose(1, 0, 2).reshape(P, k // P * n)


def twice(a):
    return np.concatenate([a, a], axis=0)


def pairs(a, b):
    return np.stack([blocks(a), blocks(b)], axis=1).reshape(-1, P, PANEL)


def constants():
    p = np.arange(P)[:, None]
    ident = np.eye(P)
    ones = np.ones((P, P))
    squares = np.stack([ident, ones, ones / D, np.kron(np.eye(2), np.ones((HALF, HALF))) / HALF, ones / P])
    slopes = 2.0 ** (-8.0 * (np.arange(HEADS) + 1) / HEADS)
    away = np.arange(S)[None, :] - (S - P) - p
    distance = np.where(away <= 0, away, NEG)
    t = (np.arange(NT)[None, :] * P + p)[:, :, None, None]
    n = np.arange(32)[None, None, None, :]
    dist = t - (n * STRIDE + LCMP - 1)
    cmp_bias = np.where((dist >= 0) & (n < NCMP), -slopes.astype(np.float32)[None, None, :, None] * dist, NEG)
    tri = np.concatenate([(p <= np.arange(P)[None, :]).astype(float)] + [ones] * (NT - 1), axis=1)
    mask = np.where(np.arange(P)[None, :] > p, NEG, 0.0)
    counts = np.stack([1.0 / np.minimum(np.arange(PoolMeans.W) + 1, w) for w in POOLS])
    inverse = np.broadcast_to(counts[None], (P, len(POOLS), PoolMeans.W))
    f = {"squares": squares, "distance": distance, "cmp_bias": cmp_bias, "tri": tri, "mask": mask,
         "inverse_counts": inverse}
    f = {k: np.ascontiguousarray(v.astype(np.float32)) for k, v in f.items()}
    return f, np.broadcast_to(slopes.astype(np.float32)[None, :], (P, HEADS)), (p >= LCMP - 1).astype(np.float32)


def lay_out(inputs):
    i = {k: np.asarray(v) for k, v in inputs.items()}
    arrays, slopes, seen = constants()
    dw = i["a_dw_w"][0].reshape(TAPS, KD, P).transpose(2, 1, 0).reshape(P, KD * TAPS)
    table = {
        "a_norm": tiles(i["a_norm"][0]), "pw1_b": tiles(i["a_pw1_b"][0]), "dw_w": dw, "dw_b": tiles(i["a_dw_b"][0]),
        "ln_g": tiles(i["a_ln_g"][0]), "ln_b": tiles(i["a_ln_b"][0]), "pw2_b": tiles(i["a_pw2_b"][0]),
        "kv_norm": tiles(i["kv_norm"]), "b_norm": tiles(i["b_norm"][0]), "ffn_norm": tiles(i["ffn_norm"]),
        "final_norm": tiles(i["final_norm"]), "g_mix": tiles(i["g_mix_2"]), "g_xa": tiles(i["g_xa_2"]),
        "g_mem": tiles(i["g_mem_2"]), "xa_gq": tiles(i["xa_gq_2"]), "xa_gk": tiles(i["xa_gk_2"]),
        "g_ffn": tiles(i["g_ffn_2"]), "e_gq": twice(i["e_g_qn_2"][0][:, None]), "e_gk": twice(i["e_g_kn_2"][0][:, None]),
        "s_pool": tiles(i["o_s_pool_2"][0]), "conv_w": tiles(i["o_conv_w_2"][0]), "slopes": slopes, "seen": seen,
        "halves": (np.arange(P)[:, None] // HALF == np.arange(2)[None, :]).astype(np.float32),
    }
    arrays["cols"] = np.concatenate([table[n] for n, _ in COLUMNS], axis=1)
    arrays["xT"] = i["x"][0].T.reshape(KD, P, S).transpose(1, 0, 2)
    arrays["memT"] = i["mem_2"][0].T.reshape(KD, P, MEM).transpose(1, 0, 2)
    pw1 = i["a_pw1_w"][0]
    arrays["pw1"] = pairs(pw1[:, D:], pw1[:, :D])
    arrays["pw2"] = blocks(i["a_pw2_w"][0])
    for l in range(2):
        w = i["ffn_w_in"][l]
        arrays[f"ffn_in{l}"] = pairs(w[:, :F], w[:, F:])
        arrays[f"ffn_out{l}"] = blocks(i["ffn_w_out"][l])
        arrays[f"ffn2_in{l}"] = pairs(i["w_gate_2"][l], i["w_up_2"][l])
        arrays[f"ffn2_out{l}"] = blocks(i["w_down_2"][l])
        arrays[f"xa_wq{l}"] = blocks(i["xa_wq_2"][l])
        arrays[f"xa_wk{l}"] = blocks(i["xa_wkv_2"][l][:, :512])
        arrays[f"xa_wv{l}"] = rows(i["xa_wkv_2"][l][:, 512:])
        arrays[f"xa_wo{l}"] = blocks(i["xa_wo_2"][l]).reshape(4, 2, P, 512).transpose(0, 2, 1, 3).reshape(4, P, PANEL)
    arrays["w_kv"] = blocks(i["w_kv"])
    arrays["w_q"] = blocks(i["b_w_in"][0][:, :D])
    arrays["w_gates"] = narrow(i["b_w_in"][0][:, D:])
    arrays["w_o"] = blocks(i["b_w_out"][0])
    w1 = [i[n].reshape(LCMP, HALF, HALF).transpose(1, 0, 2).reshape(HALF, LCMP * HALF) for n in ("phi_k_w1", "phi_v_w1")]
    arrays["phi_w1"] = twice(np.stack(w1, axis=1))
    arrays["phi_w2"] = twice(np.stack([i["phi_k_w2"], i["phi_v_w2"]], axis=1))
    arrays["cmp_pos"] = twice(np.stack([i["cmp_pos_k"].T, i["cmp_pos_v"].T], axis=1))
    e = i["e_w_in_2"][0]
    arrays["e_w_u"], arrays["e_w_v"] = blocks(e[:, :512]), rows(e[:, 512:1024])
    arrays["e_w_qk"], arrays["e_w_vv"] = blocks(e[:, 1024:2048]), rows(e[:, 2048:2560])
    arrays["e_w_f"] = narrow(e[:, 2560:])
    arrays["e_b_f"] = i["e_b_f_2"]
    arrays["e_g_v"] = i["e_g_v_2"]
    arrays["e_w_s"] = i["e_w_s_2"][0].transpose(2, 0, 1)
    arrays["e_b_s"] = i["e_b_s_2"]
    arrays["e_w_out"] = blocks(i["e_w_out_2"][0])
    o = i["o_w_in_2"][0]
    arrays["o_w_c"], arrays["o_w_hgg"] = blocks(o[:, :512]), blocks(o[:, 512:])
    arrays["o_w_pool"] = i["o_w_pool_2"][0].transpose(1, 0, 2)
    arrays["o_w_out"] = blocks(i["o_w_out_2"][0])
    return {k: np.ascontiguousarray(v) for k, v in arrays.items()}


def kernel(**inputs):
    import concourse.bacc as bacc
    from concourse.bass_utils import run_bass_kernel_spmd

    arrays = lay_out(inputs)
    nc = bacc.Bacc("TRN2", target_bir_lowering=False, num_devices=1)
    dram = {n: nc.dram_tensor(n, a.shape, mybir.dt.from_np(a.dtype), kind="ExternalInput").ap()
            for n, a in arrays.items()}
    dram["out"] = nc.dram_tensor("out", [KD, P, S], F32, kind="ExternalOutput").ap()
    program(nc, dram)
    result = run_bass_kernel_spmd(nc, [arrays], core_ids=[0]).results[0]["out"]
    return np.ascontiguousarray(result.reshape(D, S).T)[None]
```
